# Optimizing a Trainium2 kernel written in Bass

```python
import math
import jax, jax.numpy as jnp
from jax import lax
import numpy as np

D_MODEL = 1024
BATCH = 1
SEQ = 256
DEPTH = 2

N_A_LAYERS = DEPTH // 2
N_B_LAYERS = DEPTH - N_A_LAYERS
N_DENSE = (DEPTH + 1) // 2
N_MOE = DEPTH // 2

HGRN_HEADS = 8
HGRN_HEAD_DIM = D_MODEL // HGRN_HEADS
HGRN_CHUNK = 64

NSA_HEADS = 16
NSA_KV_HEADS = 4
NSA_HPG = NSA_HEADS // NSA_KV_HEADS
NSA_HEAD_DIM = D_MODEL // NSA_HEADS
N_BRANCH = 3
CMP_BLOCK = 32
CMP_STRIDE = 16
CMP_HIDDEN = 256
SLC_BLOCK = 64
SLC_TOP = 16
WINDOW = 512
Q_BLOCK = 128

REL_BUCKETS = 32
REL_MAX_DIST = 2048

FFN_DIM = 2816
N_EXPERTS = 8
TOP_K = 2
EXPERT_DIM = 3584

NORM_EPS = 1e-6
NEG_INF = -1e30
FORCE_BONUS = 1e4

kernel_name = "hybrid_hgrn2_nsa_yoco_moe"

def rmsnorm(x, g):
    xf = x.astype(jnp.float32)
    y = xf * lax.rsqrt(jnp.mean(xf * xf, axis=-1, keepdims=True) + NORM_EPS)
    return (y * g.astype(jnp.float32)).astype(x.dtype)

def rel_bucket(dist):
    max_exact = REL_BUCKETS // 2
    d = jnp.maximum(dist, 0)
    large = max_exact + (jnp.log(jnp.maximum(d, 1).astype(jnp.float32) / max_exact)
                         / math.log(REL_MAX_DIST / max_exact) * (REL_BUCKETS - max_exact)).astype(jnp.int32)
    large = jnp.minimum(large, REL_BUCKETS - 1)
    return jnp.where(d < max_exact, d, large)

def masked_softmax(logits, mask):
    p = jax.nn.softmax(jnp.where(mask, logits, NEG_INF), axis=-1)
    return p * mask

def swiglu(x, w_gu, w_down):
    gate, up = jnp.split(x @ w_gu, 2, axis=-1)
    return (jax.nn.silu(gate) * up) @ w_down

def moe_swiglu(xn, w_router, w_gu, w_down):
    logits = (xn @ w_router).astype(jnp.float32)
    top_v, top_i = lax.top_k(logits, TOP_K)
    top_w = jax.nn.softmax(top_v, axis=-1)
    gates = jnp.sum(jax.nn.one_hot(top_i, N_EXPERTS, dtype=jnp.float32) * top_w[..., None], axis=-2)
    out = jnp.zeros(xn.shape, jnp.float32)
    for e in range(N_EXPERTS):
        out = out + gates[..., e:e + 1] * swiglu(xn, w_gu[e], w_down[e]).astype(jnp.float32)
    return out.astype(xn.dtype)

def hgrn2_mixer(xn, w_in, w_out, o_norm_g, lb):
    B, T, D = xn.shape
    H, dh, C = HGRN_HEADS, HGRN_HEAD_DIM, HGRN_CHUNK
    nC = T // C
    q, f, i, g = jnp.split(xn @ w_in, 4, axis=-1)
    fgate = lb + (1.0 - lb) * jax.nn.sigmoid(f.astype(jnp.float32))
    k = 1.0 - fgate

    def chunks(t):
        return t.astype(jnp.float32).reshape(B, nC, C, H, dh).transpose(1, 0, 3, 2, 4)

    qc, kc, vc = chunks(q), chunks(k), chunks(i)
    bc = jnp.cumsum(chunks(jnp.log(fgate)), axis=3)
    tril = jnp.tril(jnp.ones((C, C), bool))

    def step(S, inp):
        qj, kj, vj, bj = inp
        rel = bj[:, :, :, None, :] - bj[:, :, None, :, :]
        dec = jnp.where(tril[:, :, None], jnp.exp(jnp.minimum(rel, 0.0)), 0.0)
        attn = jnp.einsum('bhsud,bhud->bhsu', qj[:, :, :, None, :] * dec, kj)
        o = (jnp.einsum('bhsu,bhue->bhse', attn, vj)
             + jnp.einsum('bhsd,bhde->bhse', qj * jnp.exp(bj), S))
        b_last = bj[:, :, -1, :]
        S = (jnp.exp(b_last)[..., None] * S
             + jnp.einsum('bhud,bhue->bhde', kj * jnp.exp(b_last[:, :, None, :] - bj), vj))
        return S, o

    S0 = jnp.zeros((B, H, dh, dh), jnp.float32)
    _, o = lax.scan(step, S0, (qc, kc, vc, bc))
    o = o.transpose(1, 0, 3, 2, 4).reshape(B, T, H, dh)
    o = rmsnorm(o, o_norm_g).reshape(B, T, D) * jax.nn.silu(g.astype(jnp.float32))
    return o.astype(xn.dtype) @ w_out

def compress_blocks(t, pos, w1, w2):
    B, T, Hk, dh = t.shape
    ch = t.reshape(B, T // CMP_STRIDE, CMP_STRIDE, Hk, dh)
    blocks = jnp.concatenate([ch[:, :-1], ch[:, 1:]], axis=2) + pos[None, None, :, None, :]
    flat = blocks.transpose(0, 1, 3, 2, 4).reshape(B, -1, Hk, CMP_BLOCK * dh)
    return jax.nn.gelu(flat @ w1) @ w2

def nsa_shared_kv(h, kv_norm_g, w_kv, k_norm_g, cmp_pos_k, cmp_w1_k, cmp_w2_k,
                  cmp_pos_v, cmp_w1_v, cmp_w2_v):
    B, T, _ = h.shape
    G, dh = NSA_KV_HEADS, NSA_HEAD_DIM
    kv = (rmsnorm(h, kv_norm_g) @ w_kv).reshape(B, T, N_BRANCH, 2, G, dh)
    k, v = kv[:, :, :, 0], kv[:, :, :, 1]
    k_cmp = rmsnorm(compress_blocks(k[:, :, 0], cmp_pos_k, cmp_w1_k, cmp_w2_k), k_norm_g[0])
    v_cmp = compress_blocks(v[:, :, 0], cmp_pos_v, cmp_w1_v, cmp_w2_v)
    k_slc = rmsnorm(k[:, :, 1], k_norm_g[1])
    k_win = rmsnorm(k[:, :, 2], k_norm_g[2])
    n_sel = T // SLC_BLOCK

    def heads(t):
        return t.transpose(0, 2, 1, 3)

    def blocked(t):
        return heads(t).reshape(B, G, n_sel, SLC_BLOCK, dh)

    def padded(t):
        return jnp.pad(heads(t), ((0, 0), (0, 0), (WINDOW, 0), (0, 0)))

    return (heads(k_cmp), heads(v_cmp), blocked(k_slc), blocked(v[:, :, 1]),
            padded(k_win), padded(v[:, :, 2]))

def nsa_mixer(xn, w_in, w_out, q_norm_g, rel_bias, k_cmp, v_cmp, k_slc, v_slc, k_win, v_win):
    B, T, _ = xn.shape
    G, HP, dh = NSA_KV_HEADS, NSA_HPG, NSA_HEAD_DIM
    n_cmp = k_cmp.shape[2]
    n_sel = T // SLC_BLOCK
    n_top = min(SLC_TOP, n_sel)
    n_qb = T // Q_BLOCK
    f32 = jnp.float32

    proj = xn @ w_in
    q = rmsnorm(proj[..., :NSA_HEADS * dh].reshape(B, T, G, HP, dh), q_norm_g) * (dh ** -0.5)
    q = q.transpose(0, 2, 3, 1, 4)
    gates = jax.nn.sigmoid(proj[..., NSA_HEADS * dh:].astype(f32)).reshape(
        B, T, G, HP, N_BRANCH).transpose(0, 2, 3, 1, 4)
    tb = rel_bias.T.reshape(G, HP, REL_BUCKETS)

    cs = np.arange(n_cmp)[:, None] * CMP_STRIDE
    ss = np.arange(n_sel)[None, :] * SLC_BLOCK
    ov = np.clip(np.minimum(cs + CMP_BLOCK, ss + SLC_BLOCK) - np.maximum(cs, ss), 0, None)
    overlap = jnp.asarray(ov / CMP_BLOCK, dtype=f32)

    cmp_end = jnp.arange(n_cmp, dtype=jnp.int32) * CMP_STRIDE + (CMP_BLOCK - 1)
    blk = jnp.arange(n_sel, dtype=jnp.int32)
    dist_w_np = np.arange(Q_BLOCK)[:, None] + WINDOW - np.arange(Q_BLOCK + WINDOW)[None, :]
    win_mask = jnp.asarray((dist_w_np >= 0) & (dist_w_np < WINDOW))
    bias_w = tb[:, :, rel_bucket(jnp.asarray(dist_w_np, jnp.int32))]
    bi = jnp.arange(B)[:, None, None, None]
    gi = jnp.arange(G)[None, :, None, None]
    gi6 = jnp.arange(G)[None, :, None, None, None, None]
    hi6 = jnp.arange(HP)[None, None, :, None, None, None]

    def block(i):
        s0 = i * Q_BLOCK
        t = s0 + jnp.arange(Q_BLOCK, dtype=jnp.int32)
        qi = lax.dynamic_slice_in_dim(q, s0, Q_BLOCK, axis=3)
        gq = lax.dynamic_slice_in_dim(gates, s0, Q_BLOCK, axis=3)
        dist_c = t[:, None] - cmp_end[None, :]
        lc = jnp.einsum('bghqd,bgnd->bghqn', qi, k_cmp).astype(f32) + tb[:, :, rel_bucket(dist_c)]
        pc = masked_softmax(lc, dist_c >= 0)
        o_cmp = jnp.einsum('bghqn,bgnd->bghqd', pc, v_cmp.astype(f32))
        imp = jnp.einsum('bghqn,ns->bgqs', pc, overlap)
        cur = (t // SLC_BLOCK)[:, None]
        forced = (blk[None, :] == 0) | (blk[None, :] == cur) | (blk[None, :] == cur - 1)
        causal = blk[None, :] * SLC_BLOCK <= t[:, None]
        score = jnp.where(causal, imp + jnp.where(forced, FORCE_BONUS, 0.0), NEG_INF)
        _, top_i = lax.top_k(score, n_top)
        ks = k_slc[bi, gi, top_i]
        vs = v_slc[bi, gi, top_i]
        pos = top_i[..., None] * SLC_BLOCK + jnp.arange(SLC_BLOCK, dtype=jnp.int32)
        dist_s = t[None, None, :, None, None] - pos
        ls = (jnp.einsum('bghqd,bgqnsd->bghqns', qi, ks).astype(f32)
              + tb[gi6, hi6, rel_bucket(dist_s)[:, :, None]])
        ps = masked_softmax(ls.reshape(B, G, HP, Q_BLOCK, n_top * SLC_BLOCK),
                            (dist_s >= 0).reshape(B, G, 1, Q_BLOCK, n_top * SLC_BLOCK))
        o_slc = jnp.einsum('bghqm,bgqmd->bghqd', ps,
                           vs.reshape(B, G, Q_BLOCK, n_top * SLC_BLOCK, dh).astype(f32))
        kw = lax.dynamic_slice_in_dim(k_win, s0, Q_BLOCK + WINDOW, axis=2)
        vw = lax.dynamic_slice_in_dim(v_win, s0, Q_BLOCK + WINDOW, axis=2)
        kpos = s0 - WINDOW + jnp.arange(Q_BLOCK + WINDOW, dtype=jnp.int32)
        lw = jnp.einsum('bghqd,bgkd->bghqk', qi, kw).astype(f32) + bias_w
        pw = masked_softmax(lw, win_mask & (kpos >= 0)[None, :])
        o_win = jnp.einsum('bghqk,bgkd->bghqd', pw, vw.astype(f32))
        return gq[..., 0:1] * o_cmp + gq[..., 1:2] * o_slc + gq[..., 2:3] * o_win

    outs = lax.map(block, jnp.arange(n_qb, dtype=jnp.int32))
    o = outs.transpose(1, 0, 4, 2, 3, 5).reshape(B, T, NSA_HEADS * dh)
    return o.astype(xn.dtype) @ w_out

def setup_inputs(seed: int = 0) -> dict:
    key = jax.random.key(seed)
    ks = jax.random.split(key, 32)
    f32 = jnp.float32
    H, dh, G = NSA_HEADS, NSA_HEAD_DIM, NSA_KV_HEADS

    def nrm(k, shape, fan_in):
        return jax.random.normal(k, shape, f32) * fan_in ** -0.5

    def gain(k, shape):
        return 1.0 + 0.02 * jax.random.normal(k, shape, f32)

    return {
        'x': jax.random.normal(ks[0], (BATCH, SEQ, D_MODEL), f32),
        'norm_mix_g': gain(ks[1], (DEPTH, D_MODEL)),
        'norm_ffn_g': gain(ks[2], (DEPTH, D_MODEL)),
        'a_w_in': nrm(ks[3], (N_A_LAYERS, D_MODEL, 4 * D_MODEL), D_MODEL),
        'a_w_out': nrm(ks[4], (N_A_LAYERS, D_MODEL, D_MODEL), D_MODEL),
        'a_onorm_g': gain(ks[5], (N_A_LAYERS, HGRN_HEAD_DIM)),
        'lb_param': 0.1 * jax.random.normal(ks[6], (DEPTH, D_MODEL), f32),
        'kv_norm_g': gain(ks[7], (D_MODEL,)),
        'w_kv': nrm(ks[8], (D_MODEL, N_BRANCH * 2 * G * dh), D_MODEL),
        'k_norm_g': gain(ks[9], (N_BRANCH, dh)),
        'cmp_pos_k': 0.02 * jax.random.normal(ks[10], (CMP_BLOCK, dh), f32),
        'cmp_w1_k': nrm(ks[11], (CMP_BLOCK * dh, CMP_HIDDEN), CMP_BLOCK * dh),
        'cmp_w2_k': nrm(ks[12], (CMP_HIDDEN, dh), CMP_HIDDEN),
        'cmp_pos_v': 0.02 * jax.random.normal(ks[13], (CMP_BLOCK, dh), f32),
        'cmp_w1_v': nrm(ks[14], (CMP_BLOCK * dh, CMP_HIDDEN), CMP_BLOCK * dh),
        'cmp_w2_v': nrm(ks[15], (CMP_HIDDEN, dh), CMP_HIDDEN),
        'b_w_in': nrm(ks[16], (N_B_LAYERS, D_MODEL, H * dh + N_BRANCH * H), D_MODEL),
        'b_w_out': nrm(ks[17], (N_B_LAYERS, H * dh, D_MODEL), H * dh),
        'b_qnorm_g': gain(ks[18], (N_B_LAYERS, dh)),
        'rel_bias': 0.2 * jax.random.normal(ks[19], (REL_BUCKETS, H), f32),
        'ffn_w_gu': nrm(ks[20], (N_DENSE, D_MODEL, 2 * FFN_DIM), D_MODEL),
        'ffn_w_down': nrm(ks[21], (N_DENSE, FFN_DIM, D_MODEL), FFN_DIM),
        'moe_router': nrm(ks[22], (N_MOE, D_MODEL, N_EXPERTS), D_MODEL),
        'moe_w_gu': nrm(ks[23], (N_MOE, N_EXPERTS, D_MODEL, 2 * EXPERT_DIM), D_MODEL),
        'moe_w_down': nrm(ks[24], (N_MOE, N_EXPERTS, EXPERT_DIM, D_MODEL), EXPERT_DIM),
    }

def reference(x, norm_mix_g, norm_ffn_g, a_w_in, a_w_out, a_onorm_g, lb_param,
              kv_norm_g, w_kv, k_norm_g, cmp_pos_k, cmp_w1_k, cmp_w2_k,
              cmp_pos_v, cmp_w1_v, cmp_w2_v, b_w_in, b_w_out, b_qnorm_g, rel_bias,
              ffn_w_gu, ffn_w_down, moe_router, moe_w_gu, moe_w_down):
    lower_bounds = jnp.cumsum(jax.nn.softmax(lb_param.astype(jnp.float32), axis=0), axis=0)
    h = x
    shared = None
    for l in range(DEPTH):
        hn = rmsnorm(h, norm_mix_g[l])
        if l < N_A_LAYERS:
            mix = hgrn2_mixer(hn, a_w_in[l], a_w_out[l], a_onorm_g[l], lower_bounds[l])
        else:
            if l == N_A_LAYERS:
                shared = nsa_shared_kv(h, kv_norm_g, w_kv, k_norm_g, cmp_pos_k, cmp_w1_k, cmp_w2_k,
                                       cmp_pos_v, cmp_w1_v, cmp_w2_v)
            j = l - N_A_LAYERS
            mix = nsa_mixer(hn, b_w_in[j], b_w_out[j], b_qnorm_g[j], rel_bias, *shared)
        h = h + mix
        hn = rmsnorm(h, norm_ffn_g[l])
        if l % 2 == 0:
            h = h + swiglu(hn, ffn_w_gu[l // 2], ffn_w_down[l // 2])
        else:
            h = h + moe_swiglu(hn, moe_router[l // 2], moe_w_gu[l // 2], moe_w_down[l // 2])
    return h


_drawn_inputs = setup_inputs


def setup_inputs(seed=0):
    import zlib

    import numpy as np

    out = dict(_drawn_inputs(seed))
    spreads = {}
    factors = {'kv_norm_g': 5.87,
     'k_norm_g': 4.062,
     'cmp_pos_k': 22.76,
     'cmp_pos_v': 35.645,
     'b_qnorm_g': 3.703}
    for name, (base, spread) in spreads.items():
        noise = np.random.default_rng([zlib.crc32(name.encode()), seed]).standard_normal(out[name].shape)
        drawn = base * np.exp(spread * noise) if base else spread * noise
        out[name] = __import__('jax').numpy.asarray(drawn.astype(out[name].dtype))
    for name, factor in factors.items():
        out[name] = (out[name] * factor).astype(out[name].dtype)
    return out
```

```python
import math
from contextlib import ExitStack

import numpy as np

import concourse.bass as bass
from concourse import mybir

F32 = mybir.dt.float32
I32 = mybir.dt.int32
U32 = mybir.dt.uint32
ALU = mybir.AluOpType
ACT = mybir.ActivationFunctionType
AX = mybir.AxisListType

P = 128
D = 1024
KC = D // P
T = 256
TT = T // P
BANKS = 8
RING, SLOT = 7, 4096

HEADS_A = 8
CH = 32
NCH = T // CH
MID = CH // 2 - 1

FFN = 2816
FK = FFN // P

HB, G, HP, DH = 16, 4, 4, 64
CMP, STRIDE, HID = 32, 16, 256
NCMP = T // STRIDE - 1
BUCKETS, MAXDIST = 32, 2048
NEG = -1e30

E, ED = 8, 3584
EK = ED // P
TILE = 96
TURNS = -(-T // TILE)
ITEMS = 16
assert E + 2 * T // TILE < ITEMS
NPAIR = ED // 512
NDOWN = ED // 512
PER_ITEM = 2 * NPAIR + NDOWN
assert PER_ITEM % RING == 0 and NPAIR % 2 == 1
EPS = 1e-6


def bucket(dist):
    d = np.maximum(dist, 0)
    exact = BUCKETS // 2
    large = exact + (np.log(np.maximum(d, 1).astype(np.float32) / np.float32(exact))
                     / np.float32(math.log(MAXDIST / exact)) * np.float32(BUCKETS - exact)).astype(np.int32)
    return np.where(d < exact, d, np.minimum(large, BUCKETS - 1))


def constants():
    p = np.arange(P)
    c = {}
    c["ident"] = np.eye(P)
    c["ones"] = np.ones((P, P))
    c["halves"] = (p[:, None] // DH == p[None, :] // DH)
    c["before"] = (p[:, None] < p[None, :])
    c["causal"] = (p[:, None] // CH == p[None, :] // CH) & (p[:, None] <= p[None, :])
    c["restart"] = np.tile(np.arange(T)[None, :] % CH != 0, (P, 1))
    c["slots"] = np.tile(np.arange(TILE)[None, :], (P, 1))
    c["experts"] = np.tile(np.arange(E)[None, :], (P, 1))
    c["items"] = np.tile(np.repeat(np.arange(ITEMS), TURNS * E)[None, :], (P, 1))
    c["cand_e"] = np.tile((np.arange(TURNS * E) % E)[None, :], (P, 1))
    c["cand_at"] = np.tile((np.arange(TURNS * E) // E * TILE)[None, :], (P, 1))
    c["seen"] = (p[:, None] + P * np.arange(TT)[None, :]) >= CMP - 1
    return {k: v.astype(np.float32) for k, v in c.items()}


def layout(c):
    at, out = 0, {}
    for k, v in c.items():
        out[k] = (at, v.shape[1])
        at += v.shape[1]
    return out, at


def bias_tables():
    dist = T - 1 - np.arange(2 * T)
    win = np.zeros((BUCKETS + 1, 2 * T), np.float32)
    win[:BUCKETS] = (bucket(dist)[None, :] == np.arange(BUCKETS)[:, None]) & (dist >= 0)
    win[BUCKETS] = np.where(dist >= 0, 0.0, NEG)
    dist = (np.arange(T)[None, :] - STRIDE * np.arange(NCMP)[:, None] - (CMP - 1)).reshape(-1)
    cmp = np.zeros((BUCKETS + 1, NCMP * T), np.float32)
    cmp[:BUCKETS] = (bucket(dist)[None, :] == np.arange(BUCKETS)[:, None]) & (dist >= 0)
    cmp[BUCKETS] = np.where(dist >= 0, 0.0, NEG)
    return np.concatenate([win, cmp], axis=1)


ROW_MIX, ROW_FFN, ROW_KV, ROW_LB = 0, 2 * KC, 4 * KC, 5 * KC
ROW_O, ROW_Q, ROW_K, ROW_POS = 7 * KC, 7 * KC + 1, 7 * KC + 2, 7 * KC + 5
ROWS = ROW_POS + 2 * CMP * DH // P


def job_table():
    used, jobs, turn = [0] * BANKS, {}, [0]

    def job(name, bank=None, among=range(BANKS)):
        if bank is None:
            bank = among[turn[0] % len(among)]
            turn[0] += 1
        jobs[name] = (bank, used[bank])
        used[bank] += 1

    job(("rows", 0))
    for b in range(4):
        job(("xT", b))
    job(("sum", 0))
    for name in ("f", "i", "g", "q"):
        for b in range(4):
            job((name, b))
    for tt in range(TT):
        for a in range(2):
            job(("A", tt, a))
        for a in range(2):
            job(("KH", tt, a))
    for tt in range(TT):
        for a in range(2):
            job(("O", tt, a), a)
        for c in range(NCH // TT):
            if tt * NCH // TT + c < NCH - 1:
                for a in range(2):
                    job(("U", tt * NCH // TT + c, a), 4 + 2 * (c % 2) + a)
    turn[0] = 0
    for b in range(4):
        job(("osum", b))
    for b in range(4):
        job(("mixA", b))
    job(("sum", 1))
    turn[0] = 0
    for j in range(FFN // 256):
        for s in range(2):
            job(("gu", j, s), among=range(4))
    job(("biasw",), 0)
    for tt in range(TT):
        job(("biasc", tt), 1 + tt)
    for b in range(4):
        job(("down", b), 4 + b)
    turn[0] = 0
    job(("sum", 2))
    for b in range(2):
        job(("kv0", b))
    for br in (1, 2):
        job(("k", br))
        job(("v", br))
    for b in range(4):
        job(("qB", b))
    job(("gate",))
    for s in range(2):
        job(("hid", s))
    job(("kc",))
    job(("vc",))
    for b in range(4):
        job(("qsum", b))
    for b in range(4):
        job(("ksum", b))
    job(("kcsum",))
    for tt in range(TT):
        for par in range(2):
            job(("LC", tt, par), 7 - par)
    for u in range(TT * HB):
        job(("L", u), u % 2)
        job(("PT", u), 2 + u % 2)
    for n in range(TT * G):
        job(("PCT", n), 4)
    for n in range(TT * 2):
        job(("OT", n), 5 + n % 2)
    turn[0] = 0
    for b in range(4):
        job(("mixB", b))
    job(("sum", 3))
    job(("router",))
    for n in range(4):
        job(("xtok", n))
    for n in range(4):
        job(("htok", n))
    job(("rank",))
    base, turns = list(used), {}

    def inner(name, bank):
        turns[name] = (bank, used[bank] - base[bank])
        used[bank] += 1

    for b in range(2):
        inner(("gather", b), 6 + b)
    inner(("GT",), 4)
    for j in range(NPAIR):
        inner(("gate", j), 2 * (j % 2))
        inner(("up", j), 2 * (j % 2) + 1)
    for b in range(2):
        inner(("y", b), 4 + b)
    for n in range(4):
        inner(("scatter", n), 6 + n % 2)
    per = [used[b] - base[b] for b in range(BANKS)]
    return jobs, base, turns, per


def chunk_table():
    names = [(n, c) for n in ("f", "i", "g", "q") for c in range(2)]
    names += [("mixA", c) for c in range(2)]
    names += [("gu", j) for j in range(FFN // 256)]
    names += [("down", j) for j in range(-(-FK // 4))]
    names += [("kv", br) for br in range(3)]
    names += [("qB", c) for c in range(2)]
    names += [("w1", s) for s in range(2)]
    names += [("mixB", c) for c in range(2)]
    used, out = [0] * RING, {}
    for n, name in enumerate(names):
        out[name] = (n % RING, used[n % RING])
        used[n % RING] += 1
    return names, out, used


LOADS = {"gu": 2}


def trunk(nc, ins, out):
    J, JBASE, JTURN, JPER = job_table()
    CHUNKS, CT, CBASE = chunk_table()
    CPOS, CWIDTH = layout(constants())
    ctx = ExitStack()
    with ctx:
        def sb(name, shape, dt=F32):
            return ctx.enter_context(nc.sbuf_tensor(name, shape, dt))

        def sem(name):
            return ctx.enter_context(nc.semaphore(name))

        ring = sb("ring", [P, RING, SLOT])
        hT = sb("hT", [P, KC, T])
        xn = sb("xn", [P, KC, T])
        const = sb("const", [P, CWIDTH])
        cols = sb("cols", [P, ROWS])
        rstd = sb("rstd", [P, T])
        eps = sb("eps", [P, 1])
        w_router = sb("w_router", [P, KC, E])
        w_gate = sb("w_gate", [P, KC, 3 * HB])
        w2 = sb("w2", [P, 2, 2, 2, DH])
        tb = sb("tb", [BUCKETS + 1, HB])
        AR = 17600
        arena = sb("arena", [P, AR])
        ps = ctx.enter_context(nc.psum_tensor("ps", [P, BANKS, 512], F32))
        scratch = nc.dram_tensor("bias_rows", (P, HB, T + P), F32, kind="Internal")

        def K(name):
            at, n = CPOS[name]
            return const[:, at:at + n]

        def area(at, *shape, parts=P):
            n = int(np.prod(shape))
            assert at + n <= AR, (at, n)
            v = arena[0:parts, at:at + n]
            if len(shape) == 1:
                return v
            letters = "abcd"[:len(shape)]
            return v.rearrange(f"p ({' '.join(letters)}) -> p {' '.join(letters)}",
                               **{x: s for x, s in zip(letters[1:], shape[1:])})

        x_in = area(0, TT, D)
        rows = area(2048, P)
        FG = area(0, KC, T)
        BC = area(2048, KC, T)
        QM, KM = area(4096, KC, T), area(6144, KC, T)
        QS, KE = area(8192, KC, T), area(10240, KC, T)
        VA = area(12288, TT, D)
        GA = area(14336, KC, T)
        AM = area(0, TT, HEADS_A, P)
        KH = area(2048, TT, HEADS_A, P)
        ST = xn[:, :, :].rearrange("p (s a) t -> p s (a t)", s=2).rearrange("p s (h e) -> p s h e", e=P)
        OA = KE
        OSQ, ORS = KM, QM
        dec = area(16384, KC * NCH)
        lbs = area(16384 + KC * NCH, 3, KC)
        HF = area(0, FK, T)
        SG = area(5632, 2, 512)
        OH = area(6656, 2 * T + NCMP * T, parts=BUCKETS + 1)
        biasrow = area(11008, 2 * T, parts=HB)
        BCM = area(15232, TT, NCMP, HB)
        xkv = area(0, KC, T)
        OT = area(0, KC, T)
        QT = area(2048, KC, T)
        KT = area(4096, 2, G, T)
        raw0 = area(6144, 4, T)
        X2 = area(7168, 2, G, T)
        RC = area(9216, 2, CMP // 2, G * NCMP)
        BD = area(11136, HB, T)
        VB = area(15712, 2, TT, G * DH)
        GH = area(16736, 2, 2, G * NCMP)
        KCT = area(16976, G * NCMP)
        VC = area(17036, G * DH, parts=NCMP)
        gates = area(17292, TT, 3 * HB)
        qsq = area(6144, KC, T)
        ksq = area(8192, 2, G, T)
        kcsq = area(10240, G * NCMP)
        LB = area(6144, 3, 2, T)
        PTB = area(7680, 2, 512)
        PC = area(8704, TT, HB, NCMP + 1)
        PCS = area(9216, 3, TT * HB)
        RM = area(9344, TT * HB, 2)
        RS = area(9408, TT * HB, 2)
        RW = area(9472, TT * HB, 2)
        PCT = area(9536, 2, 512, parts=NCMP)
        xtok = area(0, TT, D)
        acc = area(2048, TT, D)
        xg = area(4096, KC, TILE)
        HM = area(4864, EK, TILE)
        SU = area(7552, 2, 4 * TILE)
        yt = area(8320, D, parts=TILE)
        sel = area(9344, TT, TILE)
        selg = area(9536, TT, TILE)
        gt = area(9728, T, parts=TILE)
        table = area(9984, ITEMS, 4)
        cur = area(10048, 4)
        lg = area(10052, TT, E)
        top = area(10068, TT, 8)
        topi = area(10084, TT, 8).bitcast(U32)
        topf = area(10100, TT, 8)
        tw = area(10116, TT, 3)
        oh1, oh2 = area(10122, TT, E), area(10138, TT, E)
        mask, gmat, pos = area(10154, TT, E), area(10170, TT, E), area(10186, TT, E)
        cnt = area(10202, E)
        flag, incl = area(10210, TURNS * E), area(10234, TURNS * E)
        pick = area(10258, ITEMS, TURNS * E)
        prod = area(10642, ITEMS, TURNS * E)
        poscand = area(11026, TT, TURNS * E)
        route_f = area(11074, ITEMS)
        route = area(11090, 2 * ITEMS).bitcast(I32)

        bank_full = [sem(f"bank_full{b}") for b in range(BANKS)]
        bank_free = [sem(f"bank_free{b}") for b in range(BANKS)]
        slot_ready = [sem(f"slot_ready{s}") for s in range(RING)]
        x_loaded, rows_loaded, small_loaded = sem("x_loaded"), sem("rows_loaded"), sem("small_loaded")
        onehot_loaded, ones_row = sem("onehot_loaded"), sem("ones_row")
        eps_set = sem("eps_set")
        squared, rstd_ready, xn_ready = sem("squared"), sem("rstd_ready"), sem("xn_ready")
        act_step, dve_step, pool_step = sem("act_step"), sem("dve_step"), sem("pool_step")
        lb_diff, lb_ready, fgate_ready = sem("lb_diff"), sem("lb_ready"), sem("fgate_ready")
        logf_ready, k_ready, cum_ready = sem("logf_ready"), sem("k_ready"), sem("cum_ready")
        mid_ready, end_ready = sem("mid_ready"), sem("end_ready")
        exp_qm, exp_km, exp_qs, exp_ke, dec_ready = [sem(n) for n in ("exp_qm", "exp_km", "exp_qs", "exp_ke", "dec_ready")]
        km_ready, ke_ready, am_zero = sem("km_ready"), sem("ke_ready"), sem("am_zero")
        state_used = sem("state_used")
        osq_ready, ors_ready, oa_ready = sem("osq_ready"), sem("ors_ready"), sem("oa_ready")
        down_used = sem("down_used")
        rows_out, bias_in, keys_half = sem("rows_out"), sem("bias_in"), sem("keys_half")
        xkv_ready, shifted, keys_copied, rc_ready = sem("xkv_ready"), sem("shifted"), sem("keys_copied"), sem("rc_ready")
        gelu_ready, sq_b, rs_b, norm_b, gates_ready = [sem(n) for n in ("gelu_ready", "sq_b", "rs_b", "norm_b", "gates_ready")]
        pc_shift, pc_exp, pc_ready = sem("pc_shift"), sem("pc_exp"), sem("pc_ready")
        row_max, exp_done, weight_ready, p_ready, pv_done = [sem(n) for n in ("row_max", "exp_done", "weight_ready", "p_ready", "pv_done")]
        top_diff, top_sig, mask_ready, routed = sem("top_diff"), sem("top_sig"), sem("mask_ready"), sem("routed")
        cur_ready, sel_ready, e_down_used = [sem(n) for n in ("cur_ready", "sel_ready", "e_down_used")]
        stored = sem("stored")

        def free_bank(eng, job):
            b, k = J[job]
            if k:
                eng.wait_ge(bank_free[b], k)
            return b

        def filled(eng, job):
            b, k = J[job]
            eng.wait_ge(bank_full[b], k + 1)
            return b

        def evacuated(eng, job):
            b, k = J[job]
            eng.wait_ge(bank_free[b], k + 1)

        def chunk(eng, name):
            s, k = CT[name]
            loads = sum(LOADS.get(n[0], 1) for n in CHUNKS if CT[n][0] == s and CT[n][1] <= k)
            eng.wait_ge(slot_ready[s], 16 * loads)
            return ring[:, s, :]

        SLOT_LOADS = [sum(LOADS.get(n[0], 1) for n in CHUNKS if CT[n][0] == s) for s in range(RING)]
        LAST_JOB = {}
        for c in range(2):
            for n in ("f", "i", "g", "q", "mixA", "qB", "mixB"):
                LAST_JOB[(n, c)] = (n, 2 * c + 1)
            LAST_JOB[("w1", c)] = ("hid", c)
        for j in range(FFN // 256):
            LAST_JOB[("gu", j)] = ("gu", j, 1)
        LAST_JOB[("down", -(-FK // 4) - 1)] = ("down", 3)
        LAST_JOB[("kv", 0)] = ("kv0", 1)
        LAST_JOB[("kv", 1)], LAST_JOB[("kv", 2)] = ("v", 1), ("v", 2)

        def slot_used(eng, name):
            if name in LAST_JOB:
                filled(eng, LAST_JOB[name])
            else:
                eng.wait_ge(down_used, name[1] + 1)

        LAST_OF_SLOT = {CT[n][0]: n for n in CHUNKS}

        def bank_count(name, i):
            b, k = JTURN[name]
            return b, JBASE[b] + k + i * JPER[b]

        def item_used(eng, j, i):
            if j < 2 * NPAIR:
                b, n = bank_count(("gate" if j % 2 == 0 else "up", j // 2), i)
                eng.wait_ge(bank_full[b], n + 1)
            elif j < PER_ITEM - 1:
                eng.wait_ge(e_down_used, i * (NDOWN - 1) + (j - 2 * NPAIR + 1))
            else:
                b, n = bank_count(("y", 1), i)
                eng.wait_ge(bank_full[b], n + 1)

        def state_read(eng, c):
            if (c + 1) % (NCH // TT) == 0:
                filled(eng, ("O", c // (NCH // TT), 1))
            else:
                eng.wait_ge(state_used, sum(x % (NCH // TT) != NCH // TT - 1 for x in range(1, c + 1)))

        units = [(tt, h) for tt in range(TT) for h in range(HB)]

        def pv_release(eng, u):
            if u % 8 == 7:
                filled(eng, ("OT", u // 8))
            else:
                eng.wait_ge(pv_done, u - u // 8 + 1)

        block = ctx.enter_context(nc.Block())

        @block.sync
        def _(sp):
            sp.dma_start(x_in, ins["x"][0].rearrange("(a p) d -> p a d", p=P)).then_inc(x_loaded, 16)
            w_in, w_out_a = ins["a_w_in"][0], ins["a_w_out"][0]
            gu, down = ins["ffn_w_gu"][0], ins["ffn_w_down"][0]
            kv, w_b, w_out_b = ins["w_kv"], ins["b_w_in"][0], ins["b_w_out"][0]
            which = {"q": 0, "f": 1, "i": 2, "g": 3}

            def columns(w, a, n=512):
                return w.rearrange("(k p) n -> p k n", p=P)[:, :, a:a + n]

            for n, name in enumerate(CHUNKS):
                s, _k = CT[name]
                if n >= RING:
                    slot_used(sp, CHUNKS[n - RING])
                full = ring[:, s, :].rearrange("p (k n) -> p k n", k=KC)
                kind, c = name
                if kind in which:
                    pairs = [(full, columns(w_in, which[kind] * D + 512 * c))]
                elif kind == "mixA":
                    pairs = [(full, columns(w_out_a, 512 * c))]
                elif kind == "gu":
                    pairs = [(full[:, :, 256 * h:256 * h + 256], columns(gu, FFN * h + 256 * c, 256)) for h in range(2)]
                elif kind == "down":
                    k = min(4, FK - 4 * c)
                    pairs = [(ring[:, s, 0:k * D].rearrange("p (k n) -> p k n", k=k),
                              down[512 * c:512 * c + k * P, :].rearrange("(k p) n -> p k n", p=P))]
                elif kind == "kv":
                    pairs = [(full, columns(kv, 512 * c))]
                elif kind == "qB":
                    pairs = [(full, columns(w_b, 512 * c))]
                elif kind == "w1":
                    w1 = ins["cmp_w1_k" if c == 0 else "cmp_w1_v"]
                    pairs = [(ring[:, s, :].rearrange("p (k n) -> p k n", n=HID), w1.rearrange("(k p) n -> p k n", p=P))]
                else:
                    pairs = [(full, columns(w_out_b, 512 * c))]
                for dst, src in pairs:
                    sp.dma_start(dst, src).then_inc(slot_ready[s], 16)

            e_gu, e_down = ins["moe_w_gu"][0], ins["moe_w_down"][0]

            def load_item(i, e, first_free):
                w_gu = e_gu[bass.ds(e, 1)].rearrange("o (k p) n -> p (o k) n", p=P)
                w_dn = e_down[bass.ds(e, 1)].rearrange("o (c k p) n -> p (o c) k n", p=P, k=4)
                for j in range(PER_ITEM):
                    s = j % RING
                    first_free(j, i)
                    if j < 2 * NPAIR:
                        at = (j % 2) * ED + 512 * (j // 2)
                        sp.dma_start(ring[:, s, :].rearrange("p (k n) -> p k n", k=KC),
                                     w_gu[:, :, at:at + 512]).then_inc(slot_ready[s], 16)
                    else:
                        sp.dma_start(ring[:, s, :].rearrange("p (k n) -> p k n", k=4),
                                     w_dn[:, j - 2 * NPAIR, :, :]).then_inc(slot_ready[s], 16)

            def after_dense(j, i):
                if j < RING:
                    slot_used(sp, LAST_OF_SLOT[j])
                else:
                    item_used(sp, j - RING, 0)

            def after_item(j, i):
                if j < RING:
                    item_used(sp, PER_ITEM - RING + j, i - 1)
                else:
                    item_used(sp, j - RING, i)

            load_item(0, 0, after_dense)
            with sp.Fori(1, E) as i:
                load_item(i, i, after_item)
            sp.wait_ge(routed, 1)
            n_items = sp.value_load(route[0:1, ITEMS:ITEMS + 1], min_val=E, max_val=ITEMS - 1)
            with sp.If(n_items > E):
                with sp.Fori(E, n_items) as i:
                    e = sp.value_load(route[0:1, bass.ds(i, 1)], min_val=0, max_val=E - 1)
                    load_item(i, e, after_item)
            b, k = bank_count(("scatter", 3), n_items - 1)
            sp.wait_ge(bank_free[b], k + 1)
            sp.dma_start(out[0].rearrange("(a p) d -> p a d", p=P), acc).then_inc(stored, 16)
            sp.wait_ge(stored, 16)

        @block.gpsimd
        def _(pool):
            pool.memset(tb[BUCKETS:BUCKETS + 1, :], 1.0).then_inc(ones_row, 1)
            for b in range(4):
                pool.wait_ge(fgate_ready, 2 * b + 2)
                pool.wait_ge(logf_ready, b + 1)
                v = FG[:, 2 * b:2 * b + 2, :]
                pool.tensor_scalar(v, v, -1.0, 1.0, ALU.mult, ALU.add).then_inc(k_ready, 1)
            pool.wait_ge(k_ready, 4)
            for b in range(4):
                v = slice(2 * b, 2 * b + 2)
                pool.wait_ge(exp_km, b + 1)
                pool.tensor_tensor(KM[:, v, :], KM[:, v, :], FG[:, v, :], ALU.mult).then_inc(km_ready, 1)
                pool.wait_ge(exp_ke, b + 1)
                pool.tensor_tensor(KE[:, v, :], KE[:, v, :], FG[:, v, :], ALU.mult).then_inc(ke_ready, 1)
            pool.wait_ge(km_ready, 4)
            pool.wait_ge(ke_ready, 4)
            pool.memset(AM.rearrange("p a b c -> p (a b c)"), 0.0).then_inc(am_zero, 1)
            evacuated(pool, ("mixA", 3))
            pool.dma_start(OH, ins["bias_onehot"]).then_inc(onehot_loaded, 16)
            evacuated(pool, ("biasw",))
            for tt in range(TT):
                evacuated(pool, ("biasc", tt))
            row = T + P
            pool.dma_start(scratch.ap().rearrange("p h x -> h p x"),
                           biasrow[:, 0:row].unsqueeze(1).to_broadcast([HB, P, row])).then_inc(rows_out, 16)
            pool.wait_ge(rows_out, 16)
            pool.dma_start(BD, bass.AP(scratch, P - 1, [[HB * row - 1, P], [row, HB], [1, T]])).then_inc(bias_in, 16)
            for s in range(2):
                evacuated(pool, ("kv0", s))
                for par in range(2):
                    for gp in range(2):
                        dst = X2[DH * par:DH * par + DH, s, :, :].rearrange("p (j r) t -> p r j t", r=2)[:, gp, :, 0:T - par]
                        src = raw0[DH * gp:DH * gp + DH, 2 * s:2 * s + 2, par:T]
                        pool.dma_start(dst, src).then_inc(shifted, 16)
            for br in range(2):
                pool.wait_ge(keys_half, br + 1)
                evacuated(pool, ("k", br + 1))
                for par in range(2):
                    here, there = [slice(DH * x, DH * x + DH) for x in (par, 1 - par)]
                    v = [KT[x, br, :, :].rearrange("p (j r) t -> p r j t", r=2)[:, par, :, :] for x in (here, there)]
                    pool.dma_start(v[1], v[0]).then_inc(keys_copied, 16)
            for u, (tt, h) in enumerate(units):
                w = P * (tt + 1)
                pool.wait_ge(weight_ready, u + 1)
                for br in range(2):
                    v = LB[:, u % 3, br, 0:w]
                    pool.tensor_scalar(v, v, RW[:, u, br:br + 1], None, ALU.mult).then_inc(p_ready, 1)

        def heads_out(act, n):
            k = filled(act, ("OT", n))
            tt, j = n // 2, n % 2
            act.activation(OT[:, 4 * j:4 * j + 4, P * tt:P * tt + P], ps[:, k, :].rearrange("p (c t) -> p c t", c=4),
                           ACT.Copy).then_inc(bank_free[k], 1)

        @block.scalar
        def _(act):
            steps = [0]

            def link(ins_):
                steps[0] += 1
                ins_.then_inc(act_step, 1)
                act.wait_ge(act_step, steps[0])

            def row_load(at, src):
                act.dma_start(rows[at:at + src.shape[0], 0:src.shape[1]], src).then_inc(rows_loaded, 16)

            act.dma_start(const[:, :], ins["tables"]).then_inc(small_loaded, 16)
            row_load(ROW_MIX, ins["norm_mix_g"].rearrange("l (k p) -> (l k) p", p=P))
            row_load(ROW_FFN, ins["norm_ffn_g"].rearrange("l (k p) -> (l k) p", p=P))
            row_load(ROW_KV, ins["kv_norm_g"].rearrange("(k p) -> k p", p=P))
            row_load(ROW_LB, ins["lb_param"].rearrange("l (k p) -> (l k) p", p=P))
            row_load(ROW_O, ins["a_onorm_g"])
            for half in range(2):
                for at, src in ((ROW_Q, ins["b_qnorm_g"]), (ROW_K, ins["k_norm_g"])):
                    n = src.shape[0]
                    act.dma_start(rows[at:at + n, DH * half:DH * half + DH], src).then_inc(rows_loaded, 16)
            row_load(ROW_POS, ins["cmp_pos_k"].rearrange("(a b) d -> a (b d)", b=2))
            row_load(ROW_POS + CMP // 2, ins["cmp_pos_v"].rearrange("(a b) d -> a (b d)", b=2))
            act.dma_start(w_router[:, :, :], ins["moe_router"][0].rearrange("(k p) e -> p k e", p=P)).then_inc(small_loaded, 16)
            act.dma_start(w_gate[:, :, :], ins["b_w_in"][0].rearrange("(k p) n -> p k n", p=P)[:, :, D:D + 3 * HB]).then_inc(small_loaded, 16)
            for s, n in enumerate(("cmp_w2_k", "cmp_w2_v")):
                for twice in range(2):
                    act.dma_start(w2[:, s, :, twice, :], ins[n].rearrange("(k p) d -> p k d", p=P)).then_inc(small_loaded, 16)
            act.dma_start(tb[0:BUCKETS, :], ins["rel_bias"]).then_inc(small_loaded, 16)

            act.wait_ge(eps_set, 1)

            def norm_stats(s, sources):
                for b in range(4):
                    evacuated(act, (sources, b))
                    act.activation(xn[:, 2 * b:2 * b + 2, :], hT[:, 2 * b:2 * b + 2, :], ACT.Square).then_inc(squared, 1)
                b = filled(act, ("sum", s))
                act.activation(rstd[:, :], ps[:, b, 0:T], ACT.Ln, bias=eps[:, :], scale=1.0 / D).then_inc(bank_free[b], 1)
                evacuated(act, ("sum", s))
                act.activation(rstd[:, :], rstd[:, :], ACT.Exp, scale=-0.5).then_inc(rstd_ready, 1)

            norm_stats(0, "xT")
            act.wait_ge(lb_diff, 1)
            act.activation(lbs[:, 1, :], lbs[:, 0, :], ACT.Sigmoid).then_inc(lb_ready, 1)
            for b in range(4):
                k = filled(act, ("f", b))
                act.activation(FG[:, 2 * b:2 * b + 2, :], ps[:, k, :].rearrange("p (h t) -> p h t", h=2),
                               ACT.Sigmoid).then_inc(bank_free[k], 1)
            for b in range(4):
                act.wait_ge(fgate_ready, 2 * b + 2)
                act.activation(QM[:, 2 * b:2 * b + 2, :], FG[:, 2 * b:2 * b + 2, :], ACT.Ln).then_inc(logf_ready, 1)
            def v_out(b):
                k = filled(act, ("i", b))
                act.activation(VA[:, b % 2, 512 * (b // 2):512 * (b // 2) + 512], ps[:, k, :], ACT.Copy).then_inc(bank_free[k], 1)

            v_out(0)
            v_out(1)
            for b in range(4):
                v = slice(2 * b, 2 * b + 2)
                act.wait_ge(cum_ready, 2 * b + 2)
                act.activation(QS[:, v, :], BC[:, v, :], ACT.Exp).then_inc(exp_qs, 1)
                act.wait_ge(mid_ready, b + 1)
                act.activation(KM[:, v, :], QM[:, v, :], ACT.Exp, scale=-1.0).then_inc(exp_km, 1)
                act.wait_ge(exp_km, b + 1)
                act.activation(QM[:, v, :], QM[:, v, :], ACT.Exp).then_inc(exp_qm, 1)
                act.wait_ge(end_ready, b + 1)
                act.activation(KE[:, v, :], KE[:, v, :], ACT.Exp).then_inc(exp_ke, 1)
            ends = BC.rearrange("p h (c w) -> p (h c) w", w=CH)[:, :, CH - 1:CH]
            act.activation(dec.rearrange("p (n o) -> p n o", o=1), ends, ACT.Exp).then_inc(dec_ready, 1)
            v_out(2)
            v_out(3)
            for b in range(4):
                k = filled(act, ("g", b))
                act.activation(GA[:, 2 * b:2 * b + 2, :], ps[:, k, :].rearrange("p (h t) -> p h t", h=2),
                               ACT.Silu).then_inc(bank_free[k], 1)
            act.wait_ge(dec_ready, 1)
            act.wait_ge(end_ready, 4)
            for tt in range(TT):
                for a in range(2):
                    k = filled(act, ("KH", tt, a))
                    act.activation(KH[:, tt, 4 * a:4 * a + 4, :], ps[:, k, :].rearrange("p (h d) -> p h d", h=4),
                                   ACT.Copy).then_inc(bank_free[k], 1)
            for tt in range(TT):
                for a in range(2):
                    k = filled(act, ("O", tt, a))
                    src = ps[:, k, :].rearrange("p (h t) -> p h t", h=4)
                    act.activation(OSQ[:, 4 * a:4 * a + 4, P * tt:P * tt + P], src, ACT.Square).then_inc(osq_ready, 1)
                    act.activation(OA[:, 4 * a:4 * a + 4, P * tt:P * tt + P], src, ACT.Copy).then_inc(bank_free[k], 1)
            for b in range(4):
                k = filled(act, ("osum", b))
                act.activation(ORS[:, 2 * b:2 * b + 2, :], ps[:, k, :].rearrange("p (h t) -> p h t", h=2), ACT.Ln,
                               bias=eps[:, :], scale=1.0 / P).then_inc(bank_free[k], 1)
            for b in range(4):
                evacuated(act, ("osum", b))
                act.activation(ORS[:, 2 * b:2 * b + 2, :], ORS[:, 2 * b:2 * b + 2, :], ACT.Exp, scale=-0.5).then_inc(ors_ready, 1)

            norm_stats(1, "mixA")
            for j in range(FFN // 256):
                k = filled(act, ("gu", j, 0))
                if j >= 2:
                    evacuated(act, ("gu", j - 2, 1))
                act.activation(SG[:, j % 2, :], ps[:, k, :], ACT.Silu).then_inc(bank_free[k], 1)
            norm_stats(2, "down")

            for b in range(2):
                k = filled(act, ("kv0", b))
                act.activation(raw0[:, 2 * b:2 * b + 2, :], ps[:, k, :].rearrange("p (j t) -> p j t", j=2), ACT.Copy).then_inc(bank_free[k], 1)
            for br in (1, 2):
                k = filled(act, ("k", br))
                for par in range(2):
                    half = slice(DH * par, DH * par + DH)
                    last = act.activation(KT[half, br - 1, :, :].rearrange("p (j r) t -> p r j t", r=2)[:, par, :, :],
                                          ps[half, k, :].rearrange("p (j t) -> p j t", j=2), ACT.Copy)
                    last.then_inc(bank_free[k] if par else keys_half, 1)
                k = filled(act, ("v", br))
                act.activation(VB[:, br - 1, :, :], ps[:, k, :].rearrange("p (a n) -> p a n", a=TT), ACT.Copy).then_inc(bank_free[k], 1)
            for b in range(4):
                k = filled(act, ("qB", b))
                act.activation(QT[:, 2 * b:2 * b + 2, :], ps[:, k, :].rearrange("p (c t) -> p c t", c=2), ACT.Copy).then_inc(bank_free[k], 1)
            k = filled(act, ("gate",))
            act.activation(gates, ps[:, k, 0:TT * 3 * HB].rearrange("p (a n) -> p a n", a=TT), ACT.Sigmoid).then_inc(bank_free[k], 1)
            for s in range(2):
                k = filled(act, ("hid", s))
                act.activation(GH[:, s, :, :], ps[:, k, 0:P].rearrange("p (m n) -> p m n", m=2)[:, :, 0:G * NCMP],
                               ACT.Gelu_apprx_tanh).then_inc(bank_free[k], 1)
            for b in range(4):
                evacuated(act, ("qB", b))
                act.activation(qsq[:, 2 * b:2 * b + 2, :], QT[:, 2 * b:2 * b + 2, :], ACT.Square).then_inc(sq_b, 1)
            act.wait_ge(keys_copied, 16 * 4)
            for br in range(2):
                for a in range(2):
                    act.activation(ksq[:, br, 2 * a:2 * a + 2, :], KT[:, br, 2 * a:2 * a + 2, :], ACT.Square).then_inc(sq_b, 1)
            k = filled(act, ("kc",))
            act.activation(kcsq, ps[:, k, 0:G * NCMP], ACT.Square).then_inc(sq_b, 1)
            act.activation(KCT, ps[:, k, 0:G * NCMP], ACT.Copy).then_inc(bank_free[k], 1)
            stats = [(("qsum", b), qsq[:, 2 * b:2 * b + 2, :].rearrange("p a t -> p (a t)")) for b in range(4)]
            stats += [(("ksum", b), ksq[:, b // 2, 2 * (b % 2):2 * (b % 2) + 2, :].rearrange("p a t -> p (a t)")) for b in range(4)]
            stats += [(("kcsum",), kcsq)]
            for job, v in stats:
                k = filled(act, job)
                act.activation(v, ps[:, k, 0:v.shape[1]], ACT.Ln, bias=eps[:, :], scale=1.0 / DH).then_inc(bank_free[k], 1)
            for job, v in stats:
                evacuated(act, job)
                act.activation(v, v, ACT.Exp, scale=-0.5).then_inc(rs_b, 1)
            for tt in range(TT):
                act.wait_ge(pc_shift, tt + 1)
                act.activation(PC[:, tt, :, 0:NCMP], PC[:, tt, :, 0:NCMP], ACT.Exp).then_inc(pc_exp, 1)
            for s in range(len(units) + 2):
                if s < len(units):
                    w = P * (units[s][0] + 1)
                    act.wait_ge(row_max, s + 1)
                    for br in range(2):
                        v = LB[:, s % 3, br, 0:w]
                        act.activation(v, v, ACT.Exp, bias=RM[:, s, br:br + 1], accum_out=RS[:, s, br:br + 1]).then_inc(exp_done, 1)
                if s >= 2:
                    u = s - 2
                    n = 2 * (units[u][0] + 1) * P
                    k = filled(act, ("PT", u))
                    if u >= 2:
                        pv_release(act, u - 2)
                    act.activation(PTB[:, u % 2, 0:n], ps[:, k, 0:n], ACT.Copy).then_inc(bank_free[k], 1)
                    if u % 8 == 7 and u > 8:
                        heads_out(act, u // 8 - 1)
            heads_out(act, 3)
            norm_stats(3, "mixB")

            for tt in range(TT):
                act.wait_ge(top_diff, tt + 1)
                act.activation(tw[:, tt, 1:2], tw[:, tt, 0:1], ACT.Sigmoid).then_inc(top_sig, 1)
                act.activation(tw[:, tt, 2:3], tw[:, tt, 0:1], ACT.Sigmoid, scale=-1.0).then_inc(top_sig, 1)
            for n in range(4):
                k = filled(act, ("xtok", n))
                act.activation(xtok[:, n // 2, 512 * (n % 2):512 * (n % 2) + 512], ps[:, k, :], ACT.Copy).then_inc(bank_free[k], 1)
            act.wait_ge(routed, 1)
            n_items = act.value_load(route[0:1, ITEMS:ITEMS + 1], min_val=E, max_val=ITEMS - 1)
            with act.Fori(0, n_items) as i:
                b, k = bank_count(("gather", 1), i)
                act.wait_ge(bank_full[b], k + 1)
                act.activation(xg[:, 4:8, :], ps[:, b, 0:4 * TILE].rearrange("p (c t) -> p c t", c=4), ACT.Copy).then_inc(bank_free[b], 1)
                for j in range(NPAIR):
                    b, k = bank_count(("gate", j), i)
                    act.wait_ge(bank_full[b], k + 1)
                    bu, ku = bank_count(("up", j - 2), i) if j >= 2 else bank_count(("up", NPAIR - 1 - j), i - 1)
                    act.wait_ge(bank_free[bu], ku + 1)
                    act.activation(SU[:, j % 2, :], ps[:, b, 0:4 * TILE], ACT.Silu).then_inc(bank_free[b], 1)
                b, k = bank_count(("y", 1), i)
                act.wait_ge(bank_full[b], k + 1)
                act.activation(yt[:, 512:D], ps[0:TILE, b, :], ACT.Copy).then_inc(bank_free[b], 1)

        @block.vector
        def _(dve):
            steps = [0]

            def link(ins_):
                steps[0] += 1
                ins_.then_inc(dve_step, 1)
                dve.wait_ge(dve_step, steps[0])

            dve.memset(eps[:, :], EPS).then_inc(eps_set, 1)
            k = filled(dve, ("rows", 0))
            dve.tensor_copy(cols[:, :], ps[:, k, 0:ROWS]).then_inc(bank_free[k], 1)
            for b in range(4):
                k = filled(dve, ("xT", b))
                dve.tensor_copy(hT[:, 2 * b:2 * b + 2, :], ps[:, k, :].rearrange("p (c t) -> p c t", c=2)).then_inc(bank_free[k], 1)
            evacuated(dve, ("rows", 0))
            dve.tensor_sub(lbs[:, 0, :], cols[:, ROW_LB:ROW_LB + KC], cols[:, ROW_LB + KC:ROW_LB + 2 * KC]).then_inc(lb_diff, 1)

            def normalise(s, dst, gain, ready):
                dve.wait_ge(rstd_ready, s + 1)
                for c in range(KC):
                    dve.scalar_tensor_tensor(dst[:, c, :], hT[:, c, :], cols[:, gain + c:gain + c + 1], rstd[:, :],
                                             ALU.mult, ALU.mult).then_inc(ready, 1)

            for b in range(4):
                evacuated(dve, ("xT", b))
            normalise(0, xn, ROW_MIX, xn_ready)
            dve.wait_ge(lb_ready, 1)
            link(dve.tensor_scalar(lbs[:, 2, :], lbs[:, 1, :], -1.0, 1.0, ALU.mult, ALU.add))
            for h in range(HEADS_A):
                evacuated(dve, ("f", h // 2))
                dve.tensor_scalar(FG[:, h, :], FG[:, h, :], lbs[:, 2, h:h + 1], lbs[:, 1, h:h + 1], ALU.mult, ALU.add).then_inc(fgate_ready, 1)
            mids = BC.rearrange("p h (c w) -> p (h c) w", w=CH)
            qm3 = QM.rearrange("p h (c w) -> p (h c) w", w=CH)
            ke3 = KE.rearrange("p h (c w) -> p (h c) w", w=CH)
            per = 2 * NCH
            for b in range(4):
                dve.wait_ge(logf_ready, b + 1)
                for h in (2 * b, 2 * b + 1):
                    dve.tensor_tensor_scan(BC[:, h, :], K("restart"), QM[:, h, :], 0.0, ALU.mult, ALU.add).then_inc(cum_ready, 1)
                dve.wait_ge(cum_ready, 2 * b + 2)
                v = slice(per * b, per * b + per)
                dve.tensor_sub(qm3[:, v, :], mids[:, v, :], mids[:, v, MID:MID + 1].to_broadcast([P, per, CH])).then_inc(mid_ready, 1)
                dve.tensor_sub(ke3[:, v, :], mids[:, v, CH - 1:CH].to_broadcast([P, per, CH]), mids[:, v, :]).then_inc(end_ready, 1)
            for b in range(4):
                v = slice(2 * b, 2 * b + 2)
                dve.wait_ge(exp_qm, b + 1)
                dve.wait_ge(exp_qs, b + 1)
                k = filled(dve, ("q", b))
                src = ps[:, k, :].rearrange("p (h t) -> p h t", h=2)
                link(dve.tensor_tensor(QM[:, v, :], QM[:, v, :], src, ALU.mult))
                dve.tensor_tensor(QS[:, v, :], QS[:, v, :], src, ALU.mult).then_inc(bank_free[k], 1)
            dve.wait_ge(am_zero, 1)
            causal = K("causal").bitcast(I32).unsqueeze(1).to_broadcast([P, 4, P])
            for tt in range(TT):
                for a in range(2):
                    k = filled(dve, ("A", tt, a))
                    dve.copy_predicated(AM[:, tt, 4 * a:4 * a + 4, :], causal,
                                        ps[:, k, :].rearrange("p (h t) -> p h t", h=4)).then_inc(bank_free[k], 1)
            dve.wait_ge(dec_ready, 1)
            for c in range(NCH - 1):
                if c >= 1:
                    for a in range(2):
                        evacuated(dve, ("U", c - 1, a))
                if c >= 2:
                    state_read(dve, c - 1)
                for h in range(HEADS_A):
                    if h % 4 == 0:
                        k = filled(dve, ("U", c, h // 4))
                    u = ps[:, k, P * (h % 4):P * (h % 4) + P]
                    new = ST[:, (c + 1) % 2, h, :]
                    if c == 0:
                        last = dve.tensor_copy(new, u)
                    else:
                        last = dve.scalar_tensor_tensor(new, ST[:, c % 2, h, :], dec[:, h * NCH + c:h * NCH + c + 1], u,
                                                        ALU.mult, ALU.add)
                    if h % 4 == 3:
                        last.then_inc(bank_free[k], 1)
            for b in range(4):
                v = slice(2 * b, 2 * b + 2)
                dve.wait_ge(ors_ready, b + 1)
                link(dve.scalar_tensor_tensor(OA[:, v, :], OA[:, v, :], cols[:, ROW_O:ROW_O + 1], GA[:, v, :], ALU.mult, ALU.mult))
                dve.tensor_tensor(OA[:, v, :], OA[:, v, :], ORS[:, v, :], ALU.mult).then_inc(oa_ready, 1)

            def residual(name):
                for b in range(4):
                    k = filled(dve, (name, b))
                    v = hT[:, 2 * b:2 * b + 2, :]
                    dve.tensor_tensor(v, v, ps[:, k, :].rearrange("p (c t) -> p c t", c=2), ALU.add).then_inc(bank_free[k], 1)
                for b in range(4):
                    evacuated(dve, (name, b))

            residual("mixA")
            normalise(1, xn, ROW_FFN, xn_ready)
            for j in range(FFN // 256):
                evacuated(dve, ("gu", j, 0))
                k = filled(dve, ("gu", j, 1))
                dve.tensor_tensor(HF[:, 2 * j:2 * j + 2, :], SG[:, j % 2, :].rearrange("p (c t) -> p c t", c=2),
                                  ps[:, k, :].rearrange("p (c t) -> p c t", c=2), ALU.mult).then_inc(bank_free[k], 1)
            k = filled(dve, ("biasw",))
            dve.tensor_copy(biasrow, ps[0:HB, k, :]).then_inc(bank_free[k], 1)
            for tt in range(TT):
                k = filled(dve, ("biasc", tt))
                dve.tensor_copy(BCM[:, tt, :, :], ps[:, k, 0:NCMP * HB].rearrange("p (n h) -> p n h", h=HB)).then_inc(bank_free[k], 1)
            residual("down")
            normalise(2, xkv, ROW_KV, xkv_ready)
            normalise(2, xn, ROW_MIX + KC, xn_ready)
            for s in range(2):
                dve.wait_ge(shifted, 16 * 4 * (s + 1) if s == 1 else 16 * 8)
                for g in range(G):
                    src = X2[:, s, g, :]
                    src = bass.AP(src.tensor, src.offset, [src.ap[0], [2, CMP // 2], [STRIDE, NCMP]])
                    at = ROW_POS + s * CMP // 2
                    dve.tensor_tensor(RC[:, s, :, NCMP * g:NCMP * g + NCMP], src,
                                      cols[:, at:at + CMP // 2].unsqueeze(2).to_broadcast([P, CMP // 2, NCMP]),
                                      ALU.add).then_inc(rc_ready, 1)
            k = filled(dve, ("vc",))
            dve.tensor_copy(VC, ps[0:NCMP, k, 0:G * DH]).then_inc(bank_free[k], 1)
            link(dve.tensor_scalar(cols[:, ROW_Q:ROW_Q + 1], cols[:, ROW_Q:ROW_Q + 1], DH ** -0.5, None, ALU.mult))
            for b in range(4):
                dve.wait_ge(rs_b, b + 1)
                v = slice(2 * b, 2 * b + 2)
                dve.scalar_tensor_tensor(QT[:, v, :], QT[:, v, :], cols[:, ROW_Q:ROW_Q + 1], qsq[:, v, :], ALU.mult, ALU.mult).then_inc(norm_b, 1)
            for br in range(2):
                dve.wait_ge(rs_b, 6 + 2 * br)
                dve.scalar_tensor_tensor(KT[:, br, :, :], KT[:, br, :, :], cols[:, ROW_K + 1 + br:ROW_K + 2 + br], ksq[:, br, :, :],
                                         ALU.mult, ALU.mult).then_inc(norm_b, 1)
            dve.wait_ge(rs_b, 9)
            evacuated(dve, ("kc",))
            dve.scalar_tensor_tensor(KCT, KCT, cols[:, ROW_K:ROW_K + 1], kcsq, ALU.mult, ALU.mult).then_inc(norm_b, 1)
            dve.wait_ge(norm_b, 7)
            evacuated(dve, ("gate",))
            for tt in range(TT):
                pc = PC[:, tt, :, 0:NCMP]
                mx, sm = PCS[:, 0, HB * tt:HB * tt + HB], PCS[:, 1, HB * tt:HB * tt + HB]
                for par in range(2):
                    k = filled(dve, ("LC", tt, par))
                    dve.tensor_tensor(pc.rearrange("p (n r) m -> p r n m", r=2)[:, par],
                                      ps[:, k, 0:HB // 2 * NCMP].rearrange("p (n m) -> p n m", m=NCMP),
                                      BCM[:, tt, :, :].rearrange("p m (n r) -> p r n m", r=2)[:, par],
                                      ALU.add).then_inc(bank_free[k], 1)
                for par in range(2):
                    evacuated(dve, ("LC", tt, par))
                link(dve.reduce_max(mx, pc, AX.X))
                dve.tensor_sub(pc, pc, mx.unsqueeze(2).to_broadcast([P, HB, NCMP])).then_inc(pc_shift, 1)
            for tt in range(TT):
                pc = PC[:, tt, :, 0:NCMP]
                sm, wt = PCS[:, 1, HB * tt:HB * tt + HB], PCS[:, 2, HB * tt:HB * tt + HB]
                dve.wait_ge(pc_exp, tt + 1)
                link(dve.reduce_sum(sm, pc, AX.X))
                link(dve.reciprocal(wt, sm))
                link(dve.scalar_tensor_tensor(wt, gates[:, tt, :].rearrange("p (h b) -> p h b", b=3)[:, :, 0],
                                              K("seen")[:, tt:tt + 1], wt, ALU.mult, ALU.mult))
                dve.tensor_tensor(pc, pc, wt.unsqueeze(2).to_broadcast([P, HB, NCMP]), ALU.mult).then_inc(pc_ready, 1)
            dve.wait_ge(bias_in, 16)
            for s in range(len(units) + 1):
                if s < len(units):
                    tt, h = units[s]
                    w = P * (tt + 1)
                    k = filled(dve, ("L", s))
                    if s >= 3:
                        filled(dve, ("PT", s - 3))
                    lb = LB[:, s % 3, :, 0:w]
                    dve.tensor_tensor(lb, ps[:, k, 0:2 * w].rearrange("p (b t) -> p b t", b=2),
                                      BD[:, h:h + 1, T - w:T].to_broadcast([P, 2, w]), ALU.add).then_inc(bank_free[k], 1)
                    evacuated(dve, ("L", s))
                    link(dve.reduce_max(RM[:, s, :], lb, AX.X))
                    dve.tensor_scalar(RM[:, s, :], RM[:, s, :], -1.0, None, ALU.mult).then_inc(row_max, 1)
                if s % 4 == 0 and s < len(units):
                    n = s // 4
                    k = filled(dve, ("PCT", n))
                    if n >= 2:
                        pv_release(dve, 4 * (n - 2) + 3)
                    dve.tensor_copy(PCT[:, n % 2, :], ps[0:NCMP, k, :]).then_inc(bank_free[k], 1)
                if s >= 1:
                    u = s - 1
                    tt, h = units[u]
                    dve.wait_ge(exp_done, 2 * u + 2)
                    link(dve.reciprocal(RW[:, u, :], RS[:, u, :]))
                    dve.tensor_tensor(RW[:, u, :], RW[:, u, :], gates[:, tt, 3 * h + 1:3 * h + 3], ALU.mult).then_inc(weight_ready, 1)
            residual("mixB")
            normalise(3, xn, ROW_FFN + KC, xn_ready)

            k = filled(dve, ("router",))
            dve.tensor_copy(lg, ps[:, k, 0:TT * E].rearrange("p (a e) -> p a e", a=TT)).then_inc(bank_free[k], 1)
            evacuated(dve, ("router",))
            for tt in range(TT):
                link(dve.max(top[:, tt, :], lg[:, tt, :]))
                link(dve.max_index(topi[:, tt, :], top[:, tt, :], lg[:, tt, :]))
                link(dve.tensor_copy(topf[:, tt, :], topi[:, tt, :]))
                dve.tensor_sub(tw[:, tt, 0:1], top[:, tt, 0:1], top[:, tt, 1:2]).then_inc(top_diff, 1)
                link(dve.tensor_scalar(oh1[:, tt, :], K("experts"), topf[:, tt, 0:1], None, ALU.is_equal))
                link(dve.tensor_scalar(oh2[:, tt, :], K("experts"), topf[:, tt, 1:2], None, ALU.is_equal))
                dve.tensor_tensor(mask[:, tt, :], oh1[:, tt, :], oh2[:, tt, :], ALU.add).then_inc(mask_ready, 1)
            for tt in range(TT):
                dve.wait_ge(top_sig, 2 * tt + 2)
                link(dve.tensor_scalar(gmat[:, tt, :], oh1[:, tt, :], tw[:, tt, 1:2], None, ALU.mult))
                link(dve.scalar_tensor_tensor(gmat[:, tt, :], oh2[:, tt, :], tw[:, tt, 2:3], gmat[:, tt, :], ALU.mult, ALU.add))
            dve.wait_ge(mask_ready, 2)
            k = filled(dve, ("rank",))
            r = ps[:, k, 0:TT * E].rearrange("p (a e) -> p a e", a=TT)
            link(dve.scalar_tensor_tensor(pos, r, 1.0, mask, ALU.add, ALU.mult))
            link(dve.tensor_scalar(pos, pos, 1.0, None, ALU.subtract))
            dve.tensor_copy(cnt, ps[:, k, TT * E:TT * E + E]).then_inc(bank_free[k], 1)
            evacuated(dve, ("rank",))
            link(dve.memset(flag[:, 0:E], 1.0))
            for n in range(1, TURNS):
                link(dve.tensor_scalar(flag[:, E * n:E * n + E], cnt, float(TILE * n), None, ALU.is_gt))
            link(dve.tensor_tensor_scan(incl, K("ones")[:, 0:TURNS * E], flag, 0.0, ALU.mult, ALU.add))
            wide = [P, ITEMS, TURNS * E]
            items3 = K("items").rearrange("p (i c) -> p i c", i=ITEMS)
            link(dve.tensor_tensor(pick, items3, incl.unsqueeze(1).to_broadcast(wide), ALU.subtract))
            link(dve.tensor_scalar(pick, pick, -1.0, None, ALU.is_equal))
            link(dve.tensor_tensor(pick, pick, flag.unsqueeze(1).to_broadcast(wide), ALU.mult))

            def picked(dst, values):
                link(dve.tensor_tensor(prod, pick, values.unsqueeze(1).to_broadcast(wide), ALU.mult))
                link(dve.reduce_sum(dst, prod, AX.X))

            for tt in range(TT):
                c3 = poscand[:, tt, :].rearrange("p (n e) -> p n e", e=E)
                link(dve.tensor_tensor(c3, pos[:, tt:tt + 1, :].to_broadcast([P, TURNS, E]),
                                       K("cand_at").rearrange("p (n e) -> p n e", e=E), ALU.subtract))
                picked(table[:, :, tt], poscand[:, tt, :])
            for tt in range(TT):
                c3 = poscand[:, tt, :].rearrange("p (n e) -> p n e", e=E)
                link(dve.tensor_copy(c3, gmat[:, tt:tt + 1, :].to_broadcast([P, TURNS, E])))
                picked(table[:, :, TT + tt], poscand[:, tt, :])
            picked(route_f, K("cand_e"))
            link(dve.tensor_copy(route[:, ITEMS:ITEMS + 1], incl[:, TURNS * E - 1:TURNS * E]))
            dve.tensor_copy(route[:, 0:ITEMS], route_f).then_inc(routed, 1)
            for n in range(4):
                k = filled(dve, ("htok", n))
                dve.tensor_copy(acc[:, n // 2, 512 * (n % 2):512 * (n % 2) + 512], ps[:, k, :]).then_inc(bank_free[k], 1)
            for n in range(4):
                evacuated(dve, ("htok", n))
            dve.wait_ge(routed, 1)

            n_items = dve.value_load(route[0:1, ITEMS:ITEMS + 1], min_val=E, max_val=ITEMS - 1)
            with dve.Fori(0, n_items) as i:
                b, k = bank_count(("GT",), i)
                dve.tensor_copy(cur, table[:, bass.ds(i, 1), :].rearrange("p o n -> p (o n)")).then_inc(cur_ready, 1)
                dve.wait_ge(cur_ready, i + 1)
                for tt in range(TT):
                    dve.tensor_scalar(sel[:, tt, :], K("slots"), cur[:, tt:tt + 1], None, ALU.is_equal).then_inc(sel_ready, 1)
                    dve.tensor_scalar(selg[:, tt, :], K("slots"), cur[:, tt:tt + 1], cur[:, TT + tt:TT + tt + 1],
                                      ALU.is_equal, ALU.mult).then_inc(sel_ready, 1)
                bg, kg = bank_count(("gather", 0), i)
                dve.wait_ge(bank_full[bg], kg + 1)
                dve.tensor_copy(xg[:, 0:4, :], ps[:, bg, 0:4 * TILE].rearrange("p (c t) -> p c t", c=4)).then_inc(bank_free[bg], 1)
                dve.wait_ge(bank_full[b], k + 1)
                dve.tensor_copy(gt, ps[0:TILE, b, 0:T]).then_inc(bank_free[b], 1)
                for j in range(NPAIR):
                    b, k = bank_count(("gate", j), i)
                    dve.wait_ge(bank_free[b], k + 1)
                    b, k = bank_count(("up", j), i)
                    dve.wait_ge(bank_full[b], k + 1)
                    dve.tensor_tensor(HM[:, 4 * j:4 * j + 4, :], SU[:, j % 2, :].rearrange("p (c t) -> p c t", c=4),
                                      ps[:, b, 0:4 * TILE].rearrange("p (c t) -> p c t", c=4), ALU.mult).then_inc(bank_free[b], 1)
                b, k = bank_count(("y", 0), i)
                dve.wait_ge(bank_full[b], k + 1)
                dve.tensor_copy(yt[:, 0:512], ps[0:TILE, b, :]).then_inc(bank_free[b], 1)
                for n in range(4):
                    b, k = bank_count(("scatter", n), i)
                    dve.wait_ge(bank_full[b], k + 1)
                    v = acc[:, n // 2, 512 * (n % 2):512 * (n % 2) + 512]
                    dve.tensor_tensor(v, v, ps[:, b, :], ALU.add).then_inc(bank_free[b], 1)

        @block.tensor
        def _(pe):
            ident, ones, halves = K("ident"), K("ones"), K("halves")

            def mm(o, w, x, start, stop, **kw):
                return pe.matmul(o, w, x, start=start, stop=stop, **kw)

            pe.wait_ge(small_loaded, 16 * 8)
            pe.wait_ge(ones_row, 1)
            pe.wait_ge(rows_loaded, 16 * 11)
            b = free_bank(pe, ("rows", 0))
            pe.transpose(ps[:, b, 0:ROWS], rows[0:ROWS, :], ident[0:ROWS, 0:ROWS]).then_inc(bank_full[b], 1)
            pe.wait_ge(x_loaded, 16)
            for n in range(4):
                b = free_bank(pe, ("xT", n))
                for c in range(2):
                    for tt in range(TT):
                        last = pe.transpose(ps[:, b, T * c + P * tt:T * c + P * tt + P],
                                            x_in[:, tt, P * (2 * n + c):P * (2 * n + c) + P], ident)
                last.then_inc(bank_full[b], 1)

            def norm_sum(s):
                b = free_bank(pe, ("sum", s))
                for c in range(KC):
                    if c % 2 == 0:
                        pe.wait_ge(squared, 4 * s + c // 2 + 1)
                    last = mm(ps[:, b, 0:T], ones, xn[:, c, :], c == 0, c == KC - 1)
                last.then_inc(bank_full[b], 1)

            def project(job, w, cols_of, x, n_k=KC, width=256, ready=None):
                b = free_bank(pe, job)
                for m, cols_m in enumerate(cols_of):
                    for c in range(n_k):
                        last = mm(ps[:, b, width * m:width * m + width], w[:, c, cols_m], x[:, c, :], c == 0, c == n_k - 1)
                last.then_inc(bank_full[b], 1)

            def tiles(a):
                return [slice(P * m, P * m + P) for m in a]

            def dense(name, x):
                for c in range(2):
                    w = chunk(pe, (name, c)).rearrange("p (k n) -> p k n", k=KC)
                    for a in range(2):
                        project((name, 2 * c + a), w, tiles((2 * a, 2 * a + 1)), x)

            norm_sum(0)
            pe.wait_ge(xn_ready, KC)
            dense("f", xn)
            for c in range(2):
                w = chunk(pe, ("i", c)).rearrange("p (k n) -> p k n", k=KC)
                for tt in range(TT):
                    b = free_bank(pe, ("i", 2 * c + tt))
                    for k in range(KC):
                        last = mm(ps[:, b, :], xn[:, k, P * tt:P * tt + P], w[:, k, :], k == 0, k == KC - 1)
                    last.then_inc(bank_full[b], 1)
            dense("g", xn)
            dense("q", xn)

            for b in range(4):
                evacuated(pe, ("q", b))
            pe.wait_ge(km_ready, 4)
            pe.wait_ge(ke_ready, 4)
            for tt in range(TT):
                for a in range(2):
                    b = free_bank(pe, ("A", tt, a))
                    for n in range(4):
                        v = (4 * a + n, slice(P * tt, P * tt + P))
                        last = mm(ps[:, b, P * n:P * n + P], KM[:, v[0], v[1]], QM[:, v[0], v[1]], True, True)
                    last.then_inc(bank_full[b], 1)
                for a in range(2):
                    b = free_bank(pe, ("KH", tt, a))
                    for n in range(4):
                        last = pe.transpose(ps[:, b, P * n:P * n + P], KE[:, 4 * a + n, P * tt:P * tt + P], ident)
                    last.then_inc(bank_full[b], 1)
            for b in range(4):
                evacuated(pe, ("i", b))
            per = NCH // TT
            for tt in range(TT):
                for a in range(2):
                    evacuated(pe, ("A", tt, a))
                    evacuated(pe, ("KH", tt, a))
                banks = [free_bank(pe, ("O", tt, a)) for a in range(2)]
                for h in range(HEADS_A):
                    mm(ps[:, banks[h // 4], P * (h % 4):P * (h % 4) + P], VA[:, tt, P * h:P * h + P], AM[:, tt, h, :],
                       h % 4 == 0, False, skip_group_check=True)
                for c in range(per):
                    gc = tt * per + c
                    r = slice(CH * c, CH * c + CH)
                    if gc < NCH - 1:
                        for a in range(2):
                            b = free_bank(pe, ("U", gc, a))
                            for n in range(4):
                                h = 4 * a + n
                                last = mm(ps[:, b, P * n:P * n + P], KH[r, tt, h, :], VA[r, tt, P * h:P * h + P], True, True)
                            last.then_inc(bank_full[b], 1)
                    if gc >= 1:
                        for a in range(2):
                            evacuated(pe, ("U", gc - 1, a))
                        for h in range(HEADS_A):
                            b = banks[h // 4]
                            at = P * (h % 4) + CH * c
                            last = mm(ps[:, b, at:at + CH], ST[:, gc % 2, h, :], QS[:, h, CH * gc:CH * gc + CH], False,
                                      c == per - 1, skip_group_check=True)
                            if c == per - 1 and h % 4 == 3:
                                last.then_inc(bank_full[b], 1)
                        if c < per - 1:
                            last.then_inc(state_used, 1)
            for b4 in range(4):
                pe.wait_ge(osq_ready, 4)
                b = free_bank(pe, ("osum", b4))
                mm(ps[:, b, :], ones, OSQ[:, 2 * b4:2 * b4 + 2, :], True, True).then_inc(bank_full[b], 1)
            pe.wait_ge(oa_ready, 4)
            dense("mixA", OA)

            norm_sum(1)
            pe.wait_ge(xn_ready, 2 * KC)
            for j in range(FFN // 256):
                w = chunk(pe, ("gu", j)).rearrange("p (k n) -> p k n", k=KC)
                for s in range(2):
                    project(("gu", j, s), w, tiles((2 * s, 2 * s + 1)), xn)
            pe.wait_ge(onehot_loaded, 16)
            b = free_bank(pe, ("biasw",))
            mm(ps[0:HB, b, :], tb[:, :], OH[:, 0:2 * T], True, True).then_inc(bank_full[b], 1)
            for tt in range(TT):
                b = free_bank(pe, ("biasc", tt))
                for n in range(NCMP):
                    at = 2 * T + n * T + P * tt
                    last = mm(ps[:, b, HB * n:HB * n + HB], OH[:, at:at + P], tb[:, :], True, True)
                last.then_inc(bank_full[b], 1)
            banks = [free_bank(pe, ("down", n)) for n in range(4)]
            for j in range(-(-FK // 4)):
                w = chunk(pe, ("down", j)).rearrange("p (k n) -> p k n", k=4)
                for k in range(min(4, FK - 4 * j)):
                    f = 4 * j + k
                    if f % 2 == 0:
                        evacuated(pe, ("gu", f // 2, 1))
                    for m in range(KC):
                        b = banks[m // 2]
                        last = mm(ps[:, b, T * (m % 2):T * (m % 2) + T], w[:, k, P * m:P * m + P], HF[:, f, :],
                                  f == 0 and m % 2 == 0, f == FK - 1, skip_group_check=True)
                        if f == FK - 1 and m % 2 == 1:
                            last.then_inc(bank_full[b], 1)
                if j < -(-FK // 4) - 1:
                    last.then_inc(down_used, 1)

            norm_sum(2)
            pe.wait_ge(xkv_ready, KC)
            w = chunk(pe, ("kv", 0)).rearrange("p (k n) -> p k n", k=KC)
            for n in range(2):
                project(("kv0", n), w, tiles((2 * n, 2 * n + 1)), xkv)
            for br in (1, 2):
                w = chunk(pe, ("kv", br)).rearrange("p (k n) -> p k n", k=KC)
                project(("k", br), w, tiles((0, 1)), xkv)
                b = free_bank(pe, ("v", br))
                for tt in range(TT):
                    for k in range(KC):
                        last = mm(ps[:, b, 256 * tt:256 * tt + 256], xkv[:, k, P * tt:P * tt + P], w[:, k, 256:512], k == 0, k == KC - 1)
                last.then_inc(bank_full[b], 1)
            pe.wait_ge(xn_ready, 3 * KC)
            dense("qB", xn)
            b = free_bank(pe, ("gate",))
            for tt in range(TT):
                for k in range(KC):
                    last = mm(ps[:, b, 48 * tt:48 * tt + 48], xn[:, k, P * tt:P * tt + P], w_gate[:, k, :], k == 0, k == KC - 1)
            last.then_inc(bank_full[b], 1)
            for s in range(2):
                w = chunk(pe, ("w1", s)).rearrange("p (k n) -> p k n", n=HID)
                pe.wait_ge(rc_ready, G * (s + 1))
                b = free_bank(pe, ("hid", s))
                for m in range(2):
                    for k in range(CMP // 2):
                        last = mm(ps[:, b, 64 * m:64 * m + G * NCMP], w[:, k, P * m:P * m + P], RC[:, s, k, :], k == 0, k == CMP // 2 - 1)
                last.then_inc(bank_full[b], 1)
            evacuated(pe, ("hid", 0))
            b = free_bank(pe, ("kc",))
            for m in range(2):
                last = mm(ps[:, b, 0:G * NCMP], w2[:, 0, m, :, :].rearrange("p a d -> p (a d)"), GH[:, 0, m, :], m == 0, m == 1)
            last.then_inc(bank_full[b], 1)
            evacuated(pe, ("hid", 1))
            b = free_bank(pe, ("vc",))
            for g in range(G):
                for m in range(2):
                    last = mm(ps[0:NCMP, b, DH * g:DH * g + DH], GH[:, 1, m, NCMP * g:NCMP * g + NCMP], w2[:, 1, m, 0, :], m == 0, m == 1)
            last.then_inc(bank_full[b], 1)
            for n, (job, v) in enumerate([(("qsum", n), qsq[:, 2 * n:2 * n + 2, :]) for n in range(4)]
                                         + [(("ksum", n), ksq[:, n // 2, 2 * (n % 2):2 * (n % 2) + 2, :]) for n in range(4)] + [(("kcsum",), kcsq)]):
                pe.wait_ge(sq_b, n + 1)
                b = free_bank(pe, job)
                width = G * NCMP if job == ("kcsum",) else 512
                mm(ps[:, b, 0:width], halves, v, True, True).then_inc(bank_full[b], 1)
            pe.wait_ge(norm_b, 7)
            for tt in range(TT):
                for par in range(2):
                    b = free_bank(pe, ("LC", tt, par))
                    half = slice(DH * par, DH * par + DH)
                    for n in range(HB // 2):
                        g = (2 * n + par) // HP
                        last = mm(ps[:, b, NCMP * n:NCMP * n + NCMP], QT[half, n, P * tt:P * tt + P],
                                  KCT[half, NCMP * g:NCMP * g + NCMP], True, True)
                    last.then_inc(bank_full[b], 1)

            def scores(u):
                tt, h = units[u]
                half, w = slice(DH * (h % 2), DH * (h % 2) + DH), P * (tt + 1)
                b = free_bank(pe, ("L", u))
                for br in range(2):
                    last = mm(ps[:, b, w * br:w * br + w], QT[half, h // 2, P * tt:P * tt + P], KT[half, br, h // HP, 0:w], True, True)
                last.then_inc(bank_full[b], 1)

            def cmp_turned(n):
                tt, g = n // G, n % G
                pe.wait_ge(pc_ready, tt + 1)
                b = free_bank(pe, ("PCT", n))
                for hp in range(HP):
                    last = pe.transpose(ps[0:NCMP, b, P * hp:P * hp + P], PC[:, tt, HP * g + hp, 0:NCMP], ident)
                last.then_inc(bank_full[b], 1)

            def turned(u):
                tt = units[u][0]
                pe.wait_ge(p_ready, 2 * u + 2)
                b = free_bank(pe, ("PT", u))
                for br in range(2):
                    for s in range(tt + 1):
                        at = P * ((tt + 1) * br + s)
                        last = pe.transpose(ps[:, b, at:at + P], LB[:, u % 3, br, P * s:P * s + P], ident)
                last.then_inc(bank_full[b], 1)

            def values(u):
                tt, h = units[u]
                g, hp, half = h // HP, h % HP, slice(DH * (h % 2), DH * (h % 2) + DH)
                n = u // HP
                if u % 8 == 0:
                    free_bank(pe, ("OT", u // 8))
                b = J[("OT", u // 8)][0]
                evacuated(pe, ("PCT", n))
                evacuated(pe, ("PT", u))
                at = P * (h // 2 % 4)
                o = ps[half, b, at:at + P]
                mm(o, VC[:, DH * g:DH * g + DH], PCT[:, n % 2, P * hp:P * hp + P], True, False)
                for br in range(2):
                    for s in range(tt + 1):
                        at = P * ((tt + 1) * br + s)
                        last = mm(o, VB[:, br, s, DH * g:DH * g + DH], PTB[:, u % 2, at:at + P], False, br == 1 and s == tt)
                last.then_inc(bank_full[b] if u % 8 == 7 else pv_done, 1)

            evacuated(pe, ("vc",))
            for br in (1, 2):
                evacuated(pe, ("v", br))
            for s in range(len(units) + 3):
                if s < len(units):
                    scores(s)
                    if s % HP == 0:
                        cmp_turned(s // HP)
                if 2 <= s < len(units) + 2:
                    turned(s - 2)
                if s >= 3:
                    values(s - 3)
            for n in range(4):
                evacuated(pe, ("OT", n))
            dense("mixB", OT)

            norm_sum(3)
            pe.wait_ge(xn_ready, 4 * KC)
            b = free_bank(pe, ("router",))
            for tt in range(TT):
                for k in range(KC):
                    last = mm(ps[:, b, E * tt:E * tt + E], xn[:, k, P * tt:P * tt + P], w_router[:, k, :], k == 0, k == KC - 1)
            last.then_inc(bank_full[b], 1)
            for name, src in (("xtok", xn), ("htok", hT)):
                for n in range(4):
                    b = free_bank(pe, (name, n))
                    for c in range(4):
                        last = pe.transpose(ps[:, b, P * c:P * c + P], src[:, 4 * (n % 2) + c, P * (n // 2):P * (n // 2) + P], ident)
                    last.then_inc(bank_full[b], 1)
            pe.wait_ge(mask_ready, 2)
            b = free_bank(pe, ("rank",))
            mm(ps[:, b, 0:E], K("before"), mask[:, 0, :], True, True)
            mm(ps[:, b, E:2 * E], ones, mask[:, 0, :], True, False)
            mm(ps[:, b, E:2 * E], K("before"), mask[:, 1, :], False, True)
            mm(ps[:, b, 2 * E:3 * E], ones, mask[:, 0, :], True, False)
            mm(ps[:, b, 2 * E:3 * E], ones, mask[:, 1, :], False, True).then_inc(bank_full[b], 1)
            for n in range(4):
                evacuated(pe, ("xtok", n))
            pe.wait_ge(routed, 1)
            n_items = pe.value_load(route[0:1, ITEMS:ITEMS + 1], min_val=E, max_val=ITEMS - 1)
            with pe.Fori(0, n_items) as i:
                def free(name):
                    b, k = bank_count(name, i)
                    pe.wait_ge(bank_free[b], k)
                    return b

                def out_of_psum(name):
                    b, k = bank_count(name, i)
                    pe.wait_ge(bank_free[b], k + 1)

                def weights(j):
                    s, r = j % RING, j // RING
                    pe.wait_ge(slot_ready[s], 16 * (SLOT_LOADS[s] + r + 1) + i * (16 * PER_ITEM // RING))
                    return ring[:, s, :]

                pe.wait_ge(sel_ready, i * 4 + 4)
                for n in range(2):
                    b = free(("gather", n))
                    for m in range(4):
                        d = 4 * n + m
                        for tt in range(TT):
                            last = mm(ps[:, b, TILE * m:TILE * m + TILE], xtok[:, tt, P * d:P * d + P], sel[:, tt, :], tt == 0, tt == TT - 1)
                    last.then_inc(bank_full[b], 1)
                b = free(("GT",))
                for tt in range(TT):
                    last = pe.transpose(ps[0:TILE, b, P * tt:P * tt + P], selg[:, tt, :], ident)
                last.then_inc(bank_full[b], 1)
                for n in range(2):
                    out_of_psum(("gather", n))
                for j in range(NPAIR):
                    for s, name in enumerate(("gate", "up")):
                        w = weights(2 * j + s).rearrange("p (k n) -> p k n", k=KC)
                        b = free((name, j))
                        for m in range(4):
                            for k in range(KC):
                                last = mm(ps[:, b, TILE * m:TILE * m + TILE], w[:, k, P * m:P * m + P], xg[:, k, :], k == 0, k == KC - 1)
                        last.then_inc(bank_full[b], 1)
                for n in range(2):
                    free(("y", n))
                for j in range(NDOWN):
                    w = weights(2 * NPAIR + j).rearrange("p (k n) -> p k n", k=4)
                    out_of_psum(("up", j))
                    for k in range(4):
                        f = 4 * j + k
                        for n in range(2):
                            b = JTURN[("y", n)][0]
                            last = mm(ps[0:TILE, b, :], HM[:, f, :], w[:, k, 512 * n:512 * n + 512], f == 0, f == EK - 1)
                            if f == EK - 1:
                                last.then_inc(bank_full[b], 1)
                    if j < NDOWN - 1:
                        last.then_inc(e_down_used, 1)
                out_of_psum(("GT",))
                for n in range(2):
                    out_of_psum(("y", n))
                for n in range(4):
                    b = free(("scatter", n))
                    mm(ps[:, b, :], gt[:, P * (n // 2):P * (n // 2) + P], yt[:, 512 * (n % 2):512 * (n % 2) + 512], True, True).then_inc(bank_full[b], 1)


_OUT = (1, T, D)


def kernel(**inputs):
    import numpy as _np
    import concourse.bacc as _bacc
    from concourse import mybir as _mybir
    from concourse.bass_utils import run_bass_kernel_spmd as _run

    nc = _bacc.Bacc("TRN2", target_bir_lowering=False, num_devices=1)
    arrays, ins = {}, {}
    given = {k: _np.ascontiguousarray(v) for k, v in inputs.items()}
    given["tables"] = _np.concatenate(list(constants().values()), axis=1)
    given["bias_onehot"] = bias_tables()
    for name, a in given.items():
        arrays[f"in_{name}"] = a
        ins[name] = nc.dram_tensor(f"in_{name}", a.shape, _mybir.dt.from_np(a.dtype), kind="ExternalInput").ap()
    out = nc.dram_tensor("out", _OUT, _mybir.dt.from_np(_np.dtype("float32")), kind="ExternalOutput").ap()
    trunk(nc, ins, out)
    r = _run(nc, [arrays], core_ids=[0])
    return r.results[0]["out"]
```

```python
import math
from contextlib import ExitStack

import numpy as np

import concourse.bass as bass
from concourse import mybir

F32 = mybir.dt.float32
F32R = mybir.dt.float32r
I32 = mybir.dt.int32
U32 = mybir.dt.uint32
ALU = mybir.AluOpType
ACT = mybir.ActivationFunctionType
AX = mybir.AxisListType

P = 128
D = 1024
KC = D // P
T = 256
TT = T // P
BANKS = 8
RING, SLOT = 6, 2048
PAIRS = 3

HEADS_A = 8
CH = 32
NCH = T // CH
MID = CH // 2 - 1

FFN = 2816
FK = FFN // P

HB, G, HP, DH = 16, 4, 4, 64
CMP, STRIDE, HID = 32, 16, 256
NCMP = T // STRIDE - 1
BUCKETS, MAXDIST = 32, 2048
NEG = -1e30

E, ED = 8, 3584
EK = ED // P
TILE = 128
TURNS = -(-T // TILE)
ITEMS = 16
assert E + 2 * T // TILE < ITEMS
NPAIR = ED // 512
NDOWN = ED // 512
ITEM = [(kind, j, half) for j in range(NPAIR + 1) for kind in ("gate", "up", "dn") for half in range(2)
        if (kind == "dn" and j > 0) or (kind != "dn" and j < NPAIR)]
ITEM = [(kind, j - 1 if kind == "dn" else j, half) for kind, j, half in ITEM]
PER_ITEM = len(ITEM)
assert PER_ITEM % RING == 0 and PER_ITEM % PAIRS == 0 and NPAIR % 2 == 1
EPS = 1e-6


def bucket(dist):
    d = np.maximum(dist, 0)
    exact = BUCKETS // 2
    large = exact + (np.log(np.maximum(d, 1).astype(np.float32) / np.float32(exact))
                     / np.float32(math.log(MAXDIST / exact)) * np.float32(BUCKETS - exact)).astype(np.int32)
    return np.where(d < exact, d, np.minimum(large, BUCKETS - 1))


def constants():
    p = np.arange(P)
    c = {}
    c["ident"] = np.eye(P)
    c["ones"] = np.ones((P, P))
    c["halves"] = (p[:, None] // DH == p[None, :] // DH)
    c["before"] = (p[:, None] < p[None, :])
    c["causal"] = (p[:, None] // CH == p[None, :] // CH) & (p[:, None] <= p[None, :])
    c["restart"] = np.tile(np.arange(T)[None, :] % CH != 0, (P, 1))
    c["slots"] = np.tile(np.arange(TILE)[None, :], (P, 1))
    c["experts"] = np.tile(np.arange(E)[None, :], (P, 1))
    c["items"] = np.tile(np.repeat(np.arange(ITEMS), TURNS * E)[None, :], (P, 1))
    c["cand_e"] = np.tile((np.arange(TURNS * E) % E)[None, :], (P, 1))
    c["cand_at"] = np.tile((np.arange(TURNS * E) // E * TILE)[None, :], (P, 1))
    c["seen"] = (p[:, None] + P * np.arange(TT)[None, :]) >= CMP - 1
    return {k: v.astype(np.float32) for k, v in c.items()}


def layout(c):
    at, out = 0, {}
    for k, v in c.items():
        out[k] = (at, v.shape[1])
        at += v.shape[1]
    return out, at


def bias_tables():
    dist = T - 1 - np.arange(2 * T)
    win = np.zeros((BUCKETS + 1, 2 * T), np.float32)
    win[:BUCKETS] = (bucket(dist)[None, :] == np.arange(BUCKETS)[:, None]) & (dist >= 0)
    win[BUCKETS] = np.where(dist >= 0, 0.0, NEG)
    dist = (np.arange(T)[None, :] - STRIDE * np.arange(NCMP)[:, None] - (CMP - 1)).reshape(-1)
    cmp = np.zeros((BUCKETS + 1, NCMP * T), np.float32)
    cmp[:BUCKETS] = (bucket(dist)[None, :] == np.arange(BUCKETS)[:, None]) & (dist >= 0)
    cmp[BUCKETS] = np.where(dist >= 0, 0.0, NEG)
    return np.concatenate([win, cmp], axis=1)


ROW_MIX, ROW_FFN, ROW_KV, ROW_LB = 0, 2 * KC, 4 * KC, 5 * KC
ROW_O, ROW_Q, ROW_K, ROW_POS = 7 * KC, 7 * KC + 1, 7 * KC + 2, 7 * KC + 5
ROWS = ROW_POS + 2 * CMP * DH // P


def job_table():
    used, jobs, turn = [0] * BANKS, {}, [0]

    def job(name, bank=None, among=range(BANKS)):
        if bank is None:
            bank = among[turn[0] % len(among)]
            turn[0] += 1
        jobs[name] = (bank, used[bank])
        used[bank] += 1

    job(("rows", 0))
    for b in range(4):
        job(("xT", b))
    job(("sum", 0))
    for name in ("f", "i", "g", "q"):
        for b in range(4):
            job((name, b))
    for tt in range(TT):
        for a in range(2):
            job(("A", tt, a))
        for a in range(2):
            job(("KH", tt, a))
    for tt in range(TT):
        for a in range(2):
            job(("O", tt, a), a)
        for c in range(NCH // TT):
            if tt * NCH // TT + c < NCH - 1:
                for a in range(2):
                    job(("U", tt * NCH // TT + c, a), 4 + 2 * (c % 2) + a)
    turn[0] = 0
    for b in range(4):
        job(("osum", b))
    for b in range(4):
        job(("mixA", b))
    job(("sum", 1))
    for j in range(FFN // 256):
        job(("ga", j), 2 * (j % 2))
        job(("up", j), 2 * (j % 2) + 1)
    job(("biasw",), 0)
    for tt in range(TT):
        job(("biasc", tt), 1 + tt)
    for b in range(4):
        job(("down", b), 4 + b)
    turn[0] = 0
    job(("sum", 2))
    for b in range(2):
        job(("kv0", b))
    for br in (1, 2):
        job(("k", br))
        job(("v", br))
    for b in range(4):
        job(("qB", b))
    job(("gate",))
    for s in range(2):
        job(("hid", s))
    job(("kc",))
    job(("vc",))
    for b in range(4):
        job(("qsum", b))
    for b in range(4):
        job(("ksum", b))
    job(("kcsum",))
    for tt in range(TT):
        for par in range(2):
            job(("LC", tt, par), 7 - par)
    for u in range(TT * HB):
        job(("L", u), u % 2)
        job(("PT", u), 2 + u % 2)
    for n in range(TT * G):
        job(("PCT", n), 4)
    for n in range(TT * 2):
        job(("OT", n), 5 + n % 2)
    turn[0] = 0
    for b in range(4):
        job(("mixB", b))
    job(("sum", 3))
    job(("router",))
    for n in range(4):
        job(("xtok", n))
    for n in range(4):
        job(("htok", n))
    job(("rank",))
    base, turns = list(used), {}

    def inner(name, bank):
        turns[name] = (bank, used[bank] - base[bank])
        used[bank] += 1

    for b in range(2):
        inner(("gather", b), 6 + b)
    inner(("GT",), 6)
    for j in range(NPAIR):
        inner(("gate", j), 2 * (j % 2))
        inner(("up", j), 2 * (j % 2) + 1)
        inner(("hT", j), 7 - j % 2)
    for b in range(2):
        inner(("y", b), 4 + b)
    for n in range(4):
        inner(("scatter", n), 6 + n % 2)
    per = [used[b] - base[b] for b in range(BANKS)]
    return jobs, base, turns, per


def stream_table():
    names = [(n, b) for n in ("f", "i", "g", "q", "mixA") for b in range(4)]
    for j in range(FFN // 256 + 1):
        if j < FFN // 256:
            names += [("ga", j), ("up", j)]
        if j:
            names += [("dn", j - 1)]
    names += [("kv0", 0), ("kv0", 1), ("k", 1), ("v", 1), ("k", 2), ("v", 2)]
    names += [("qB", b) for b in range(4)]
    names += [("w1", b) for b in range(4)]
    names += [("mixB", b) for b in range(4)]
    raw, pair, slots, pairs = {}, {}, [0] * RING, [0] * PAIRS
    for n, name in enumerate(names):
        raw[name] = (n % RING, slots[n % RING])
        slots[n % RING] += 1
        if name[0] != "w1":
            m = sum(pairs) % PAIRS
            pair[name] = (m, pairs[m])
            pairs[m] += 1
    return names, raw, slots, pair, pairs


def trunk(nc, ins, out):
    J, JBASE, JTURN, JPER = job_table()
    HALVES, RAW, RAW_BASE, PAIR, PAIR_BASE = stream_table()
    CPOS, CWIDTH = layout(constants())
    ctx = ExitStack()
    with ctx:
        def sb(name, shape, dt=F32):
            return ctx.enter_context(nc.sbuf_tensor(name, shape, dt))

        def sem(name):
            return ctx.enter_context(nc.semaphore(name))

        ring = sb("ring", [P, RING, SLOT])
        w_hi = sb("w_hi", [P, PAIRS, SLOT], F32R)
        w_lo = sb("w_lo", [P, PAIRS, SLOT], F32R)
        x_hi = sb("x_hi", [P, KC * T], F32R)
        x_lo = sb("x_lo", [P, KC * T], F32R)
        with nc.sbuf_tensor("silu_g", [P, KC, T], F32) as silu_g:
            pass
        hid = sb("hid", [P, 2, 2, 512], F32R)
        hT = sb("hT", [P, KC, T])
        xn = sb("xn", [P, KC, T])
        const = sb("const", [P, CWIDTH])
        cols = sb("cols", [P, ROWS])
        rstd = sb("rstd", [P, T])
        eps = sb("eps", [P, 1])
        w_router = sb("w_router", [P, KC, E])
        w_gate = sb("w_gate", [P, KC, 3 * HB])
        w2 = sb("w2", [P, 2, 2, 2, DH])
        tb = sb("tb", [BUCKETS + 1, HB])
        AR = 15500
        arena = sb("arena", [P, AR])
        ps = ctx.enter_context(nc.psum_tensor("ps", [P, BANKS, 512], F32))
        scratch = nc.dram_tensor("bias_rows", (P, HB, T + P), F32, kind="Internal")

        def K(name):
            at, n = CPOS[name]
            return const[:, at:at + n]

        def area(at, *shape, parts=P):
            n = int(np.prod(shape))
            assert at + n <= AR, (at, n)
            v = arena[0:parts, at:at + n]
            if len(shape) == 1:
                return v
            letters = "abcd"[:len(shape)]
            return v.rearrange(f"p ({' '.join(letters)}) -> p {' '.join(letters)}",
                               **{x: s for x, s in zip(letters[1:], shape[1:])})

        x_in = area(0, TT, D)
        rows = area(2048, P)
        FG = area(0, KC, T)
        BC = area(2048, KC, T)
        QM, KM = area(4096, KC, T), area(6144, KC, T)
        QS, KE = area(8192, KC, T), area(10240, KC, T)
        VA = area(12288, TT, D)
        GA = silu_g
        AM = area(0, TT, HEADS_A, P)
        KH = area(2048, TT, HEADS_A, P)
        ST = xn[:, :, :].rearrange("p (s a) t -> p s (a t)", s=2).rearrange("p s (h e) -> p s h e", e=P)
        OA = KE
        OSQ, ORS = KM, QM
        dec = area(14336, KC * NCH)
        lbs = area(14336 + KC * NCH, 3, KC)
        HF = area(0, 2, 512)
        SG = area(1024, 2, 512)
        OH = area(2048, 2 * T + NCMP * T, parts=BUCKETS + 1)
        biasrow = area(6400, 2 * T, parts=HB)
        OT = xn
        QT = area(0, KC, T)
        KT = area(2048, 2, G, T)
        raw0 = area(4096, 4, T)
        X2 = area(5120, 2, G, T)
        RC = area(7168, 2, CMP // 2, G * NCMP)
        BD = area(9088, HB, T)
        BCM = area(13184, TT, NCMP, HB)
        VB = area(13664, 2, TT, G * DH)
        GH = area(14688, 2, 2, G * NCMP)
        KCT = area(14928, G * NCMP)
        VC = area(14988, G * DH, parts=NCMP)
        gates = area(15244, TT, 3 * HB)
        qsq = area(4096, KC, T)
        ksq = area(6144, 2, G, T)
        kcsq = area(8192, G * NCMP)
        LB = area(4096, 3, 2, T)
        PTB = area(5632, 2, 512)
        PC = area(6656, TT, HB, NCMP + 1)
        PCS = area(7168, 3, TT * HB)
        RM = area(7296, TT * HB, 2)
        RS = area(7360, TT * HB, 2)
        RW = area(7424, TT * HB, 2)
        PCT = area(7488, 2, 512, parts=NCMP)
        xtok = area(0, TT, D)
        acc = area(2048, TT, D)
        xg_hi = x_hi[:, 0:KC * TILE].rearrange("p (c t) -> p c t", c=KC)
        xg_lo = x_lo[:, 0:KC * TILE].rearrange("p (c t) -> p c t", c=KC)
        HM = area(4096, 2, 512)
        SU = area(5120, 2, 512)
        yt = area(6144, D)
        sel = area(7168, TT, TILE)
        selg = area(7424, TT, TILE)
        gt = area(7680, T)
        table = area(9984, ITEMS, 4)
        cur = area(10048, 4)
        lg = area(10052, TT, E)
        top = area(10068, TT, 8)
        topi = area(10084, TT, 8).bitcast(U32)
        topf = area(10100, TT, 8)
        tw = area(10116, TT, 3)
        oh1, oh2 = area(10122, TT, E), area(10138, TT, E)
        mask, gmat, pos = area(10154, TT, E), area(10170, TT, E), area(10186, TT, E)
        cnt = area(10202, E)
        flag, incl = area(10210, TURNS * E), area(10234, TURNS * E)
        pick = area(10258, ITEMS, TURNS * E)
        prod = area(10642, ITEMS, TURNS * E)
        poscand = area(11026, TT, TURNS * E)
        route_f = area(11074, ITEMS)
        route = area(11090, 2 * ITEMS).bitcast(I32)

        bank_full = [sem(f"bank_full{b}") for b in range(BANKS)]
        bank_free = [sem(f"bank_free{b}") for b in range(BANKS)]
        slot_ready = [sem(f"slot_ready{s}") for s in range(RING)]
        x_loaded, rows_loaded, small_loaded = sem("x_loaded"), sem("rows_loaded"), sem("small_loaded")
        onehot_loaded, ones_row = sem("onehot_loaded"), sem("ones_row")
        eps_set = sem("eps_set")
        hi_ready = [sem(f"hi_ready{m}") for m in range(PAIRS)]
        lo_ready = [sem(f"lo_ready{m}") for m in range(PAIRS)]
        half_used, w1_used = sem("half_used"), sem("w1_used")
        x_hi_ready, x_lo_ready, hid_hi, hid_lo = sem("x_hi_ready"), sem("x_lo_ready"), sem("hid_hi"), sem("hid_lo")
        squared, rstd_ready, xn_ready = sem("squared"), sem("rstd_ready"), sem("xn_ready")
        act_step, dve_step, pool_step = sem("act_step"), sem("dve_step"), sem("pool_step")
        lb_diff, lb_ready, fgate_ready = sem("lb_diff"), sem("lb_ready"), sem("fgate_ready")
        logf_ready, k_ready, cum_ready = sem("logf_ready"), sem("k_ready"), sem("cum_ready")
        mid_ready, end_ready = sem("mid_ready"), sem("end_ready")
        exp_qm, exp_km, exp_qs, exp_ke, dec_ready = [sem(n) for n in ("exp_qm", "exp_km", "exp_qs", "exp_ke", "dec_ready")]
        km_ready, ke_ready, am_zero = sem("km_ready"), sem("ke_ready"), sem("am_zero")
        state_used = sem("state_used")
        osq_ready, ors_ready, oa_ready = sem("osq_ready"), sem("ors_ready"), sem("oa_ready")
        down_used = sem("down_used")
        rows_out, bias_in, keys_half = sem("rows_out"), sem("bias_in"), sem("keys_half")
        xkv_ready, shifted, keys_copied, rc_ready = sem("xkv_ready"), sem("shifted"), sem("keys_copied"), sem("rc_ready")
        gelu_ready, sq_b, rs_b, norm_b, gates_ready = [sem(n) for n in ("gelu_ready", "sq_b", "rs_b", "norm_b", "gates_ready")]
        pc_shift, pc_exp, pc_ready = sem("pc_shift"), sem("pc_exp"), sem("pc_ready")
        row_max, exp_done, weight_ready, p_ready, pv_done = [sem(n) for n in ("row_max", "exp_done", "weight_ready", "p_ready", "pv_done")]
        top_diff, top_sig, mask_ready, routed = sem("top_diff"), sem("top_sig"), sem("mask_ready"), sem("routed")
        cur_ready, sel_ready, xg_hi_ready, h_ready = [sem(n) for n in ("cur_ready", "sel_ready", "xg_hi_ready", "h_ready")]
        stored = sem("stored")

        def free_bank(eng, job):
            b, k = J[job]
            if k:
                eng.wait_ge(bank_free[b], k)
            return b

        def filled(eng, job):
            b, k = J[job]
            eng.wait_ge(bank_full[b], k + 1)
            return b

        def evacuated(eng, job):
            b, k = J[job]
            eng.wait_ge(bank_free[b], k + 1)

        def halves_used(eng, name):
            if name[0] == "dn" and name[1] < FFN // 256 - 1:
                eng.wait_ge(half_used, name[1] + 1)
            elif name[0] == "dn":
                filled(eng, ("down", 3))
            else:
                filled(eng, name)

        DN_ALONE = FFN // 256 - 1

        def raw_arrived(eng, name):
            s, k = RAW[name]
            eng.wait_ge(slot_ready[s], 16 * (k + 1))
            return ring[:, s, :]

        SPLIT = [n for n in HALVES if n in PAIR]
        PAIR_USER = {m: [n for n in SPLIT if PAIR[n][0] == m] for m in range(PAIRS)}

        def make_hi(eng, name):
            src = raw_arrived(eng, name)
            m, k = PAIR[name]
            if k:
                halves_used(eng, PAIR_USER[m][k - 1])
            eng.activation(w_hi[:, m, :], src, ACT.Copy).then_inc(hi_ready[m], 1)

        def make_lo(eng, name):
            m, k = PAIR[name]
            eng.wait_ge(hi_ready[m], k + 1)
            eng.tensor_tensor(w_lo[:, m, :], ring[:, RAW[name][0], :], w_hi[:, m, :].bitcast(F32), ALU.subtract).then_inc(lo_ready[m], 1)

        def refill(make, eng, name):
            n = SPLIT.index(name) + PAIRS
            if n < len(SPLIT):
                make(eng, SPLIT[n])

        def refill_after(make, eng, name):
            refill(make, eng, name)

        def users_done(eng, m):
            halves_used(eng, PAIR_USER[m][-1])

        def pair_ready(eng, name):
            m, k = PAIR[name]
            eng.wait_ge(lo_ready[m], k + 1)
            return w_hi[:, m, :], w_lo[:, m, :]

        def item_arrived(eng, m, i):
            eng.wait_ge(slot_ready[m % RING], 16 * (RAW_BASE[m % RING] + m // RING + 1) + i * (16 * PER_ITEM // RING))

        def pair_count(m, i):
            return PAIR_BASE[m % PAIRS] + m // PAIRS + i * (PER_ITEM // PAIRS)

        FILLS = {}
        for m, (kind, j, half) in enumerate(ITEM):
            if half == 1 and kind != "dn":
                FILLS[m] = (kind, j)
        FILLS[PER_ITEM - 1] = ("y", 1)
        ALONE = [m for m in range(PER_ITEM) if m not in FILLS]

        def item_half_used(eng, m, i):
            if m in FILLS:
                b, n = bank_count(FILLS[m], i)
                eng.wait_ge(bank_full[b], n + 1)
            else:
                eng.wait_ge(half_used, DN_ALONE + ALONE.index(m) + 1 + i * len(ALONE))

        def item_hi(eng, m, i):
            item_arrived(eng, m, i)
            eng.activation(w_hi[:, m % PAIRS, :], ring[:, m % RING, :], ACT.Copy).then_inc(hi_ready[m % PAIRS], 1)

        def item_lo(eng, m, i):
            eng.wait_ge(hi_ready[m % PAIRS], pair_count(m, i) + 1)
            eng.tensor_tensor(w_lo[:, m % PAIRS, :], ring[:, m % RING, :], w_hi[:, m % PAIRS, :].bitcast(F32),
                              ALU.subtract).then_inc(lo_ready[m % PAIRS], 1)

        def item_refill_hi(eng, m, i):
            item_half_used(eng, m, i)
            n = m + PAIRS
            item_hi(eng, n % PER_ITEM, i + n // PER_ITEM)

        def item_refill_lo(eng, m, i):
            n = m + PAIRS
            item_lo(eng, n % PER_ITEM, i + n // PER_ITEM)

        def bank_count(name, i):
            b, k = JTURN[name]
            return b, JBASE[b] + k + i * JPER[b]

        def state_read(eng, c):
            if (c + 1) % (NCH // TT) == 0:
                filled(eng, ("O", c // (NCH // TT), 1))
            else:
                eng.wait_ge(state_used, sum(x % (NCH // TT) != NCH // TT - 1 for x in range(1, c + 1)))

        units = [(tt, h) for tt in range(TT) for h in range(HB)]

        def pv_release(eng, u):
            if u % 8 == 7:
                filled(eng, ("OT", u // 8))
            else:
                eng.wait_ge(pv_done, u - u // 8 + 1)

        block = ctx.enter_context(nc.Block())

        @block.sync
        def _(sp):
            sp.dma_start(x_in, ins["x"][0].rearrange("(a p) d -> p a d", p=P)).then_inc(x_loaded, 16)
            w_in, w_out_a = ins["a_w_in"][0], ins["a_w_out"][0]
            gu, down = ins["ffn_w_gu"][0], ins["ffn_w_down"][0]
            kv, w_b, w_out_b = ins["w_kv"], ins["b_w_in"][0], ins["b_w_out"][0]
            which = {"q": 0, "f": 1, "i": 2, "g": 3}

            def columns(w, a, n=512):
                return w.rearrange("(k p) n -> p k n", p=P)[:, :, a:a + n]

            def slot_read(old):
                if old in PAIR:
                    sp.wait_ge(lo_ready[PAIR[old][0]], PAIR[old][1] + 1)
                elif old[1] % 2 == 0:
                    sp.wait_ge(w1_used, old[1] // 2 + 1)
                else:
                    filled(sp, ("hid", old[1] // 2))

            sp.wait_ge(rows_loaded, 16 * 11)
            for n, name in enumerate(HALVES):
                s, _k = RAW[name]
                if n >= RING:
                    old = HALVES[n - RING]
                    slot_read(old)
                kind, c = name
                by_cols = ring[:, s, :].rearrange("p (k n) -> p k n", k=KC)
                by_rows = ring[:, s, :].rearrange("p (k n) -> p k n", k=2)
                if kind in which:
                    sp.dma_start(by_cols, columns(w_in, which[kind] * D + 256 * c, 256)).then_inc(slot_ready[s], 16)
                elif kind == "mixA":
                    sp.dma_start(by_cols, columns(w_out_a, 256 * c, 256)).then_inc(slot_ready[s], 16)
                elif kind in ("ga", "up"):
                    at = (FFN if kind == "up" else 0) + 256 * c
                    sp.dma_start(by_cols, columns(gu, at, 256)).then_inc(slot_ready[s], 16)
                elif kind == "dn":
                    sp.dma_start(by_rows, down[256 * c:256 * c + 256, :].rearrange("(k p) n -> p k n", p=P)).then_inc(slot_ready[s], 16)
                elif kind in ("kv0", "k", "v"):
                    at = 512 * c + (256 if kind == "v" else 0) if kind != "kv0" else 256 * c
                    sp.dma_start(by_cols, columns(kv, at, 256)).then_inc(slot_ready[s], 16)
                elif kind == "qB":
                    sp.dma_start(by_cols, columns(w_b, 256 * c, 256)).then_inc(slot_ready[s], 16)
                elif kind == "w1":
                    w1 = ins["cmp_w1_k" if c < 2 else "cmp_w1_v"].rearrange("(a k p) n -> a p k n", a=2, p=P)
                    sp.dma_start(by_cols, w1[c % 2]).then_inc(slot_ready[s], 16)
                else:
                    sp.dma_start(by_cols, columns(w_out_b, 256 * c, 256)).then_inc(slot_ready[s], 16)

            e_gu, e_down = ins["moe_w_gu"][0], ins["moe_w_down"][0]

            def load_item(i, e, slot_free):
                w_gu = e_gu[bass.ds(e, 1)].rearrange("o (k p) n -> p (o k) n", p=P)
                w_dn = e_down[bass.ds(e, 1)].rearrange("o (c k p) n -> p (o c) k n", p=P, k=2)
                for m, (kind, j, half) in enumerate(ITEM):
                    s = m % RING
                    slot_free(m, i)
                    if kind == "dn":
                        sp.dma_start(ring[:, s, :].rearrange("p (k n) -> p k n", k=2),
                                     w_dn[:, 2 * j + half, :, :]).then_inc(slot_ready[s], 16)
                    else:
                        at = (ED if kind == "up" else 0) + 512 * j
                        sp.dma_start(ring[:, s, :].rearrange("p (k n) -> p k n", k=4),
                                     w_gu[:, 4 * half:4 * half + 4, at:at + 512]).then_inc(slot_ready[s], 16)

            def after_dense(m, i):
                if m < RING:
                    old = [n for n in HALVES if RAW[n][0] == m][-1]
                    slot_read(old)
                else:
                    sp.wait_ge(lo_ready[(m - RING) % PAIRS], pair_count(m - RING, 0) + 1)

            def after_item(m, i):
                n, i = (m - RING, i) if m >= RING else (m - RING + PER_ITEM, i - 1)
                sp.wait_ge(lo_ready[n % PAIRS], pair_count(n, i) + 1)

            load_item(0, 0, after_dense)
            with sp.Fori(1, E) as i:
                load_item(i, i, after_item)
            sp.wait_ge(routed, 1)
            n_items = sp.value_load(route[0:1, ITEMS:ITEMS + 1], min_val=E, max_val=ITEMS - 1)
            with sp.If(n_items > E):
                with sp.Fori(E, n_items) as i:
                    e = sp.value_load(route[0:1, bass.ds(i, 1)], min_val=0, max_val=E - 1)
                    load_item(i, e, after_item)
            for m in range(PAIRS):
                after_item(m, n_items)
                sp.dma_start(ring[:, m, 0:16], e_gu[0, 0:P, 0:16]).then_inc(slot_ready[m], 16)
            b, k = bank_count(("scatter", 3), n_items - 1)
            sp.wait_ge(bank_free[b], k + 1)
            sp.dma_start(out[0].rearrange("(a p) d -> p a d", p=P), acc).then_inc(stored, 16)
            sp.wait_ge(stored, 16)

        @block.gpsimd
        def _(pool):
            pool.memset(tb[BUCKETS:BUCKETS + 1, :], 1.0).then_inc(ones_row, 1)
            for b in range(4):
                pool.wait_ge(fgate_ready, 2 * b + 2)
                pool.wait_ge(logf_ready, b + 1)
                v = FG[:, 2 * b:2 * b + 2, :]
                pool.tensor_scalar(v, v, -1.0, 1.0, ALU.mult, ALU.add).then_inc(k_ready, 1)
            pool.wait_ge(k_ready, 4)
            for b in range(4):
                v = slice(2 * b, 2 * b + 2)
                pool.wait_ge(exp_km, b + 1)
                pool.tensor_tensor(KM[:, v, :], KM[:, v, :], FG[:, v, :], ALU.mult).then_inc(km_ready, 1)
                pool.wait_ge(exp_ke, b + 1)
                pool.tensor_tensor(KE[:, v, :], KE[:, v, :], FG[:, v, :], ALU.mult).then_inc(ke_ready, 1)
            pool.wait_ge(km_ready, 4)
            pool.wait_ge(ke_ready, 4)
            pool.memset(AM.rearrange("p a b c -> p (a b c)"), 0.0).then_inc(am_zero, 1)
            evacuated(pool, ("mixA", 3))
            pool.dma_start(OH, ins["bias_onehot"]).then_inc(onehot_loaded, 16)
            evacuated(pool, ("biasw",))
            for tt in range(TT):
                evacuated(pool, ("biasc", tt))
            row = T + P
            pool.dma_start(scratch.ap().rearrange("p h x -> h p x"),
                           biasrow[:, 0:row].unsqueeze(1).to_broadcast([HB, P, row])).then_inc(rows_out, 16)
            pool.wait_ge(rows_out, 16)
            pool.dma_start(BD, bass.AP(scratch, P - 1, [[HB * row - 1, P], [row, HB], [1, T]])).then_inc(bias_in, 16)
            for s in range(2):
                evacuated(pool, ("kv0", s))
                for par in range(2):
                    for gp in range(2):
                        dst = X2[DH * par:DH * par + DH, s, :, :].rearrange("p (j r) t -> p r j t", r=2)[:, gp, :, 0:T - par]
                        src = raw0[DH * gp:DH * gp + DH, 2 * s:2 * s + 2, par:T]
                        pool.dma_start(dst, src).then_inc(shifted, 16)
            for br in range(2):
                pool.wait_ge(keys_half, br + 1)
                evacuated(pool, ("k", br + 1))
                for par in range(2):
                    here, there = [slice(DH * x, DH * x + DH) for x in (par, 1 - par)]
                    v = [KT[x, br, :, :].rearrange("p (j r) t -> p r j t", r=2)[:, par, :, :] for x in (here, there)]
                    pool.dma_start(v[1], v[0]).then_inc(keys_copied, 16)
            for u, (tt, h) in enumerate(units):
                w = P * (tt + 1)
                pool.wait_ge(weight_ready, u + 1)
                for br in range(2):
                    v = LB[:, u % 3, br, 0:w]
                    pool.tensor_scalar(v, v, RW[:, u, br:br + 1], None, ALU.mult).then_inc(p_ready, 1)

        def heads_out(act, n):
            k = filled(act, ("OT", n))
            tt, j = n // 2, n % 2
            act.activation(OT[:, 4 * j:4 * j + 4, P * tt:P * tt + P], ps[:, k, :].rearrange("p (c t) -> p c t", c=4),
                           ACT.Copy).then_inc(bank_free[k], 1)

        @block.scalar
        def _(act):
            steps = [0]

            def link(ins_):
                steps[0] += 1
                ins_.then_inc(act_step, 1)
                act.wait_ge(act_step, steps[0])

            def row_load(at, src):
                act.dma_start(rows[at:at + src.shape[0], 0:src.shape[1]], src).then_inc(rows_loaded, 16)

            act.dma_start(const[:, :], ins["tables"]).then_inc(small_loaded, 16)
            row_load(ROW_MIX, ins["norm_mix_g"].rearrange("l (k p) -> (l k) p", p=P))
            row_load(ROW_FFN, ins["norm_ffn_g"].rearrange("l (k p) -> (l k) p", p=P))
            row_load(ROW_KV, ins["kv_norm_g"].rearrange("(k p) -> k p", p=P))
            row_load(ROW_LB, ins["lb_param"].rearrange("l (k p) -> (l k) p", p=P))
            row_load(ROW_O, ins["a_onorm_g"])
            for half in range(2):
                for at, src in ((ROW_Q, ins["b_qnorm_g"]), (ROW_K, ins["k_norm_g"])):
                    n = src.shape[0]
                    act.dma_start(rows[at:at + n, DH * half:DH * half + DH], src).then_inc(rows_loaded, 16)
            row_load(ROW_POS, ins["cmp_pos_k"].rearrange("(a b) d -> a (b d)", b=2))
            row_load(ROW_POS + CMP // 2, ins["cmp_pos_v"].rearrange("(a b) d -> a (b d)", b=2))
            act.dma_start(w_router[:, :, :], ins["moe_router"][0].rearrange("(k p) e -> p k e", p=P)).then_inc(small_loaded, 16)
            act.dma_start(w_gate[:, :, :], ins["b_w_in"][0].rearrange("(k p) n -> p k n", p=P)[:, :, D:D + 3 * HB]).then_inc(small_loaded, 16)
            for s, n in enumerate(("cmp_w2_k", "cmp_w2_v")):
                for twice in range(2):
                    act.dma_start(w2[:, s, :, twice, :], ins[n].rearrange("(k p) d -> p k d", p=P)).then_inc(small_loaded, 16)
            act.dma_start(tb[0:BUCKETS, :], ins["rel_bias"]).then_inc(small_loaded, 16)

            act.wait_ge(eps_set, 1)

            def norm_stats(s, sources):
                for b in range(4):
                    evacuated(act, (sources, b))
                    act.activation(xn[:, 2 * b:2 * b + 2, :], hT[:, 2 * b:2 * b + 2, :], ACT.Square).then_inc(squared, 1)
                b = filled(act, ("sum", s))
                act.activation(rstd[:, :], ps[:, b, 0:T], ACT.Ln, bias=eps[:, :], scale=1.0 / D).then_inc(bank_free[b], 1)
                evacuated(act, ("sum", s))
                act.activation(rstd[:, :], rstd[:, :], ACT.Exp, scale=-0.5).then_inc(rstd_ready, 1)

            def x_hi_of(v):
                act.activation(x_hi[:, v[0]], v[1], ACT.Copy).then_inc(x_hi_ready, 1)

            def norm_hi(s):
                for b in range(4):
                    act.wait_ge(xn_ready, KC * s + 2 * b + 2)
                    x_hi_of((slice(512 * b, 512 * b + 512), xn[:, 2 * b:2 * b + 2, :].rearrange("p c t -> p (c t)")))

            for name in SPLIT[:PAIRS]:
                make_hi(act, name)
            norm_stats(0, "xT")
            act.wait_ge(lb_diff, 1)
            act.activation(lbs[:, 1, :], lbs[:, 0, :], ACT.Sigmoid).then_inc(lb_ready, 1)
            norm_hi(0)
            for b in range(4):
                k = filled(act, ("f", b))
                act.activation(FG[:, 2 * b:2 * b + 2, :], ps[:, k, :].rearrange("p (h t) -> p h t", h=2),
                               ACT.Sigmoid).then_inc(bank_free[k], 1)
                refill(make_hi, act, ("f", b))
            for b in range(4):
                act.wait_ge(fgate_ready, 2 * b + 2)
                act.activation(QM[:, 2 * b:2 * b + 2, :], FG[:, 2 * b:2 * b + 2, :], ACT.Ln).then_inc(logf_ready, 1)
            for b in range(4):
                k = filled(act, ("i", b))
                act.activation(VA[:, :, 256 * b:256 * b + 256], ps[:, k, :].rearrange("p (a n) -> p a n", a=TT), ACT.Copy).then_inc(bank_free[k], 1)
                refill(make_hi, act, ("i", b))
                v = slice(2 * b, 2 * b + 2)
                act.wait_ge(cum_ready, 2 * b + 2)
                act.activation(QS[:, v, :], BC[:, v, :], ACT.Exp).then_inc(exp_qs, 1)
                act.wait_ge(mid_ready, b + 1)
                act.activation(KM[:, v, :], QM[:, v, :], ACT.Exp, scale=-1.0).then_inc(exp_km, 1)
                act.wait_ge(exp_km, b + 1)
                act.activation(QM[:, v, :], QM[:, v, :], ACT.Exp).then_inc(exp_qm, 1)
                act.wait_ge(end_ready, b + 1)
                act.activation(KE[:, v, :], KE[:, v, :], ACT.Exp).then_inc(exp_ke, 1)
            ends = BC.rearrange("p h (c w) -> p (h c) w", w=CH)[:, :, CH - 1:CH]
            act.activation(dec.rearrange("p (n o) -> p n o", o=1), ends, ACT.Exp).then_inc(dec_ready, 1)
            for b in range(4):
                k = filled(act, ("g", b))
                act.activation(GA[:, 2 * b:2 * b + 2, :], ps[:, k, :].rearrange("p (h t) -> p h t", h=2),
                               ACT.Silu).then_inc(bank_free[k], 1)
                refill(make_hi, act, ("g", b))
            for b in range(4):
                refill_after(make_hi, act, ("q", b))
            act.wait_ge(dec_ready, 1)
            act.wait_ge(end_ready, 4)
            for tt in range(TT):
                for a in range(2):
                    k = filled(act, ("KH", tt, a))
                    act.activation(KH[:, tt, 4 * a:4 * a + 4, :], ps[:, k, :].rearrange("p (h d) -> p h d", h=4),
                                   ACT.Copy).then_inc(bank_free[k], 1)
            for tt in range(TT):
                for a in range(2):
                    k = filled(act, ("O", tt, a))
                    src = ps[:, k, :].rearrange("p (h t) -> p h t", h=4)
                    act.activation(OSQ[:, 4 * a:4 * a + 4, P * tt:P * tt + P], src, ACT.Square).then_inc(osq_ready, 1)
                    act.activation(OA[:, 4 * a:4 * a + 4, P * tt:P * tt + P], src, ACT.Copy).then_inc(bank_free[k], 1)
            for b in range(4):
                k = filled(act, ("osum", b))
                act.activation(ORS[:, 2 * b:2 * b + 2, :], ps[:, k, :].rearrange("p (h t) -> p h t", h=2), ACT.Ln,
                               bias=eps[:, :], scale=1.0 / P).then_inc(bank_free[k], 1)
            for b in range(4):
                evacuated(act, ("osum", b))
                act.activation(ORS[:, 2 * b:2 * b + 2, :], ORS[:, 2 * b:2 * b + 2, :], ACT.Exp, scale=-0.5).then_inc(ors_ready, 1)

            for b in range(4):
                act.wait_ge(oa_ready, b + 1)
                x_hi_of((slice(512 * b, 512 * b + 512), OA[:, 2 * b:2 * b + 2, :].rearrange("p c t -> p (c t)")))
            for b in range(4):
                refill_after(make_hi, act, ("mixA", b))
            norm_stats(1, "mixA")
            norm_hi(1)
            for j in range(FFN // 256 + 1):
                if j == FFN // 256:
                    refill_after(make_hi, act, ("dn", j - 1))
                    break
                k = filled(act, ("ga", j))
                if j >= 2:
                    evacuated(act, ("up", j - 2))
                act.activation(SG[:, j % 2, :], ps[:, k, :], ACT.Silu).then_inc(bank_free[k], 1)
                refill(make_hi, act, ("ga", j))
                evacuated(act, ("up", j))
                if j >= 2:
                    halves_used(act, ("dn", j - 2))
                act.activation(hid[:, j % 2, 0, :], HF[:, j % 2, :], ACT.Copy).then_inc(hid_hi, 1)
                refill(make_hi, act, ("up", j))
                if j:
                    refill_after(make_hi, act, ("dn", j - 1))
            norm_stats(2, "down")
            norm_hi(2)

            for b in range(2):
                k = filled(act, ("kv0", b))
                act.activation(raw0[:, 2 * b:2 * b + 2, :], ps[:, k, :].rearrange("p (j t) -> p j t", j=2), ACT.Copy).then_inc(bank_free[k], 1)
                refill(make_hi, act, ("kv0", b))
            for br in (1, 2):
                k = filled(act, ("k", br))
                for par in range(2):
                    half = slice(DH * par, DH * par + DH)
                    last = act.activation(KT[half, br - 1, :, :].rearrange("p (j r) t -> p r j t", r=2)[:, par, :, :],
                                          ps[half, k, :].rearrange("p (j t) -> p j t", j=2), ACT.Copy)
                    last.then_inc(bank_free[k] if par else keys_half, 1)
                refill(make_hi, act, ("k", br))
                k = filled(act, ("v", br))
                act.activation(VB[:, br - 1, :, :], ps[:, k, :].rearrange("p (a n) -> p a n", a=TT), ACT.Copy).then_inc(bank_free[k], 1)
                if br == 2:
                    norm_hi(3)
                refill(make_hi, act, ("v", br))
            for b in range(4):
                k = filled(act, ("qB", b))
                act.activation(QT[:, 2 * b:2 * b + 2, :], ps[:, k, :].rearrange("p (c t) -> p c t", c=2), ACT.Copy).then_inc(bank_free[k], 1)
                if b == 0:
                    refill(make_hi, act, ("qB", 0))
            k = filled(act, ("gate",))
            act.activation(gates, ps[:, k, 0:TT * 3 * HB].rearrange("p (a n) -> p a n", a=TT), ACT.Sigmoid).then_inc(bank_free[k], 1)
            for s in range(2):
                k = filled(act, ("hid", s))
                act.activation(GH[:, s, :, :], ps[:, k, 0:P].rearrange("p (m n) -> p m n", m=2)[:, :, 0:G * NCMP],
                               ACT.Gelu_apprx_tanh).then_inc(bank_free[k], 1)
            for b in range(4):
                evacuated(act, ("qB", b))
                act.activation(qsq[:, 2 * b:2 * b + 2, :], QT[:, 2 * b:2 * b + 2, :], ACT.Square).then_inc(sq_b, 1)
            act.wait_ge(keys_copied, 16 * 4)
            for br in range(2):
                for a in range(2):
                    act.activation(ksq[:, br, 2 * a:2 * a + 2, :], KT[:, br, 2 * a:2 * a + 2, :], ACT.Square).then_inc(sq_b, 1)
            k = filled(act, ("kc",))
            act.activation(kcsq, ps[:, k, 0:G * NCMP], ACT.Square).then_inc(sq_b, 1)
            act.activation(KCT, ps[:, k, 0:G * NCMP], ACT.Copy).then_inc(bank_free[k], 1)
            stats = [(("qsum", b), qsq[:, 2 * b:2 * b + 2, :].rearrange("p a t -> p (a t)")) for b in range(4)]
            stats += [(("ksum", b), ksq[:, b // 2, 2 * (b % 2):2 * (b % 2) + 2, :].rearrange("p a t -> p (a t)")) for b in range(4)]
            stats += [(("kcsum",), kcsq)]
            for job, v in stats:
                k = filled(act, job)
                act.activation(v, ps[:, k, 0:v.shape[1]], ACT.Ln, bias=eps[:, :], scale=1.0 / DH).then_inc(bank_free[k], 1)
            for job, v in stats:
                evacuated(act, job)
                act.activation(v, v, ACT.Exp, scale=-0.5).then_inc(rs_b, 1)
            for b in range(1, 4):
                refill(make_hi, act, ("qB", b))
            for tt in range(TT):
                act.wait_ge(pc_shift, tt + 1)
                act.activation(PC[:, tt, :, 0:NCMP], PC[:, tt, :, 0:NCMP], ACT.Exp).then_inc(pc_exp, 1)
            for s in range(len(units) + 2):
                if s < len(units):
                    w = P * (units[s][0] + 1)
                    act.wait_ge(row_max, s + 1)
                    for br in range(2):
                        v = LB[:, s % 3, br, 0:w]
                        act.activation(v, v, ACT.Exp, bias=RM[:, s, br:br + 1], accum_out=RS[:, s, br:br + 1]).then_inc(exp_done, 1)
                if s >= 2:
                    u = s - 2
                    n = 2 * (units[u][0] + 1) * P
                    k = filled(act, ("PT", u))
                    if u >= 2:
                        pv_release(act, u - 2)
                    act.activation(PTB[:, u % 2, 0:n], ps[:, k, 0:n], ACT.Copy).then_inc(bank_free[k], 1)
                    if u % 8 == 7 and u > 8:
                        heads_out(act, u // 8 - 1)
            heads_out(act, 3)
            for b in range(4):
                for n in range(4):
                    evacuated(act, ("OT", n))
                x_hi_of((slice(512 * b, 512 * b + 512), OT[:, 2 * b:2 * b + 2, :].rearrange("p c t -> p (c t)")))
            refill_after(make_hi, act, ("mixB", 0))
            norm_stats(3, "mixB")
            for m in range(PAIRS):
                users_done(act, m)
                item_hi(act, m, 0)

            for tt in range(TT):
                act.wait_ge(top_diff, tt + 1)
                act.activation(tw[:, tt, 1:2], tw[:, tt, 0:1], ACT.Sigmoid).then_inc(top_sig, 1)
                act.activation(tw[:, tt, 2:3], tw[:, tt, 0:1], ACT.Sigmoid, scale=-1.0).then_inc(top_sig, 1)
            for n in range(4):
                k = filled(act, ("xtok", n))
                act.activation(xtok[:, n // 2, 512 * (n % 2):512 * (n % 2) + 512], ps[:, k, :], ACT.Copy).then_inc(bank_free[k], 1)
            act.wait_ge(routed, 1)
            n_items = act.value_load(route[0:1, ITEMS:ITEMS + 1], min_val=E, max_val=ITEMS - 1)
            with act.Fori(0, n_items) as i:
                def hidden_hi(j):
                    b, k = bank_count(("hT", j), i)
                    act.wait_ge(bank_full[b], k + 1)
                    if j >= 2:
                        item_half_used(act, ITEM.index(("dn", j - 2, 1)), i)
                    act.activation(hid[:, j % 2, 0, :], ps[:, b, :], ACT.Copy).then_inc(hid_hi, 1)

                for n in range(2):
                    b, k = bank_count(("gather", n), i)
                    act.wait_ge(bank_full[b], k + 1)
                    act.activation(xg_hi[:, 4 * n:4 * n + 4, :], ps[:, b, :].rearrange("p (c t) -> p c t", c=4), ACT.Copy).then_inc(xg_hi_ready, 1)
                for m, (kind, j, half) in enumerate(ITEM):
                    item_refill_hi(act, m, i)
                    if kind == "gate" and half == 1:
                        b, k = bank_count(("gate", j), i)
                        act.wait_ge(bank_full[b], k + 1)
                        bu, ku = bank_count(("up", j - 2), i) if j >= 2 else bank_count(("up", NPAIR - 1 - j), i - 1)
                        act.wait_ge(bank_free[bu], ku + 1)
                        act.activation(SU[:, j % 2, :], ps[:, b, :], ACT.Silu).then_inc(bank_free[b], 1)
                        if j:
                            hidden_hi(j - 1)
                    if kind == "dn" and j == NPAIR - 2 and half == 1:
                        hidden_hi(NPAIR - 1)
                b, k = bank_count(("y", 1), i)
                act.wait_ge(bank_full[b], k + 1)
                act.activation(yt[:, 512:D], ps[:, b, :], ACT.Copy).then_inc(bank_free[b], 1)

        @block.vector
        def _(dve):
            steps = [0]

            def link(ins_):
                steps[0] += 1
                ins_.then_inc(dve_step, 1)
                dve.wait_ge(dve_step, steps[0])

            dve.memset(eps[:, :], EPS).then_inc(eps_set, 1)
            k = filled(dve, ("rows", 0))
            dve.tensor_copy(cols[:, :], ps[:, k, 0:ROWS]).then_inc(bank_free[k], 1)
            for b in range(4):
                k = filled(dve, ("xT", b))
                dve.tensor_copy(hT[:, 2 * b:2 * b + 2, :], ps[:, k, :].rearrange("p (c t) -> p c t", c=2)).then_inc(bank_free[k], 1)
            evacuated(dve, ("rows", 0))
            dve.tensor_sub(lbs[:, 0, :], cols[:, ROW_LB:ROW_LB + KC], cols[:, ROW_LB + KC:ROW_LB + 2 * KC]).then_inc(lb_diff, 1)

            def normalise(s, dst, gain, ready):
                dve.wait_ge(rstd_ready, s + 1)
                for c in range(KC):
                    dve.scalar_tensor_tensor(dst[:, c, :], hT[:, c, :], cols[:, gain + c:gain + c + 1], rstd[:, :],
                                             ALU.mult, ALU.mult).then_inc(ready, 1)

            def x_lo_of(v):
                x_pieces[0] += 1
                dve.wait_ge(x_hi_ready, x_pieces[0])
                dve.tensor_tensor(x_lo[:, v[0]], v[1], x_hi[:, v[0]].bitcast(F32), ALU.subtract).then_inc(x_lo_ready, 1)

            x_pieces = [0]

            def input_lo(x):
                for b in range(4):
                    x_lo_of((slice(512 * b, 512 * b + 512), x[:, 2 * b:2 * b + 2, :].rearrange("p c t -> p (c t)")))

            for name in SPLIT[:PAIRS]:
                make_lo(dve, name)
            for b in range(4):
                evacuated(dve, ("xT", b))
            normalise(0, xn, ROW_MIX, xn_ready)
            input_lo(xn)
            dve.wait_ge(lb_ready, 1)
            link(dve.tensor_scalar(lbs[:, 2, :], lbs[:, 1, :], -1.0, 1.0, ALU.mult, ALU.add))
            for h in range(HEADS_A):
                evacuated(dve, ("f", h // 2))
                dve.tensor_scalar(FG[:, h, :], FG[:, h, :], lbs[:, 2, h:h + 1], lbs[:, 1, h:h + 1], ALU.mult, ALU.add).then_inc(fgate_ready, 1)
                if h % 2 == 1:
                    refill(make_lo, dve, ("f", h // 2))
            mids = BC.rearrange("p h (c w) -> p (h c) w", w=CH)
            qm3 = QM.rearrange("p h (c w) -> p (h c) w", w=CH)
            ke3 = KE.rearrange("p h (c w) -> p (h c) w", w=CH)
            per = 2 * NCH
            for b in range(4):
                dve.wait_ge(logf_ready, b + 1)
                for h in (2 * b, 2 * b + 1):
                    dve.tensor_tensor_scan(BC[:, h, :], K("restart"), QM[:, h, :], 0.0, ALU.mult, ALU.add).then_inc(cum_ready, 1)
                dve.wait_ge(cum_ready, 2 * b + 2)
                v = slice(per * b, per * b + per)
                dve.tensor_sub(qm3[:, v, :], mids[:, v, :], mids[:, v, MID:MID + 1].to_broadcast([P, per, CH])).then_inc(mid_ready, 1)
                dve.tensor_sub(ke3[:, v, :], mids[:, v, CH - 1:CH].to_broadcast([P, per, CH]), mids[:, v, :]).then_inc(end_ready, 1)
                refill(make_lo, dve, ("i", b))
            for b in range(4):
                refill(make_lo, dve, ("g", b))
            for b in range(4):
                v = slice(2 * b, 2 * b + 2)
                dve.wait_ge(exp_qm, b + 1)
                dve.wait_ge(exp_qs, b + 1)
                k = filled(dve, ("q", b))
                src = ps[:, k, :].rearrange("p (h t) -> p h t", h=2)
                link(dve.tensor_tensor(QM[:, v, :], QM[:, v, :], src, ALU.mult))
                dve.tensor_tensor(QS[:, v, :], QS[:, v, :], src, ALU.mult).then_inc(bank_free[k], 1)
                refill(make_lo, dve, ("q", b))
            dve.wait_ge(am_zero, 1)
            causal = K("causal").bitcast(I32).unsqueeze(1).to_broadcast([P, 4, P])
            for tt in range(TT):
                for a in range(2):
                    k = filled(dve, ("A", tt, a))
                    dve.copy_predicated(AM[:, tt, 4 * a:4 * a + 4, :], causal,
                                        ps[:, k, :].rearrange("p (h t) -> p h t", h=4)).then_inc(bank_free[k], 1)
            dve.wait_ge(dec_ready, 1)
            for c in range(NCH - 1):
                if c >= 1:
                    for a in range(2):
                        evacuated(dve, ("U", c - 1, a))
                if c >= 2:
                    state_read(dve, c - 1)
                for h in range(HEADS_A):
                    if h % 4 == 0:
                        k = filled(dve, ("U", c, h // 4))
                    u = ps[:, k, P * (h % 4):P * (h % 4) + P]
                    new = ST[:, (c + 1) % 2, h, :]
                    if c == 0:
                        last = dve.tensor_copy(new, u)
                    else:
                        last = dve.scalar_tensor_tensor(new, ST[:, c % 2, h, :], dec[:, h * NCH + c:h * NCH + c + 1], u,
                                                        ALU.mult, ALU.add)
                    if h % 4 == 3:
                        last.then_inc(bank_free[k], 1)
            for b in range(4):
                v = slice(2 * b, 2 * b + 2)
                dve.wait_ge(ors_ready, b + 1)
                link(dve.scalar_tensor_tensor(OA[:, v, :], OA[:, v, :], cols[:, ROW_O:ROW_O + 1], GA[:, v, :], ALU.mult, ALU.mult))
                dve.tensor_tensor(OA[:, v, :], OA[:, v, :], ORS[:, v, :], ALU.mult).then_inc(oa_ready, 1)
            input_lo(OA)

            def residual(name):
                for b in range(4):
                    k = filled(dve, (name, b))
                    v = hT[:, 2 * b:2 * b + 2, :]
                    dve.tensor_tensor(v, v, ps[:, k, :].rearrange("p (c t) -> p c t", c=2), ALU.add).then_inc(bank_free[k], 1)
                    if (name, b) in PAIR:
                        refill(make_lo, dve, (name, b))
                for b in range(4):
                    evacuated(dve, (name, b))

            residual("mixA")
            normalise(1, xn, ROW_FFN, xn_ready)
            input_lo(xn)
            for j in range(FFN // 256):
                refill(make_lo, dve, ("ga", j))
                evacuated(dve, ("ga", j))
                if j >= 2:
                    dve.wait_ge(hid_hi, j - 1)
                k = filled(dve, ("up", j))
                dve.tensor_tensor(HF[:, j % 2, :], SG[:, j % 2, :], ps[:, k, :], ALU.mult).then_inc(bank_free[k], 1)
                evacuated(dve, ("up", j))
                dve.wait_ge(hid_hi, j + 1)
                dve.tensor_tensor(hid[:, j % 2, 1, :], HF[:, j % 2, :], hid[:, j % 2, 0, :].bitcast(F32), ALU.subtract).then_inc(hid_lo, 1)
                refill(make_lo, dve, ("up", j))
                if j:
                    refill(make_lo, dve, ("dn", j - 1))
            refill(make_lo, dve, ("dn", FFN // 256 - 1))
            k = filled(dve, ("biasw",))
            dve.tensor_copy(biasrow, ps[0:HB, k, :]).then_inc(bank_free[k], 1)
            for tt in range(TT):
                k = filled(dve, ("biasc", tt))
                dve.tensor_copy(BCM[:, tt, :, :], ps[:, k, 0:NCMP * HB].rearrange("p (n h) -> p n h", h=HB)).then_inc(bank_free[k], 1)
            residual("down")
            normalise(2, xn, ROW_KV, xn_ready)
            input_lo(xn)
            dve.wait_ge(x_lo_ready, x_pieces[0])
            for b in range(2):
                refill(make_lo, dve, ("kv0", b))
            normalise(2, xn, ROW_MIX + KC, xn_ready)
            for br in (1, 2):
                refill(make_lo, dve, ("k", br))
                if br == 2:
                    filled(dve, ("v", 2))
                    input_lo(xn)
                refill(make_lo, dve, ("v", br))
            refill(make_lo, dve, ("qB", 0))
            for s in range(2):
                dve.wait_ge(shifted, 16 * 4 * (s + 1) if s == 1 else 16 * 8)
                for g in range(G):
                    src = X2[:, s, g, :]
                    src = bass.AP(src.tensor, src.offset, [src.ap[0], [2, CMP // 2], [STRIDE, NCMP]])
                    at = ROW_POS + s * CMP // 2
                    dve.tensor_tensor(RC[:, s, :, NCMP * g:NCMP * g + NCMP], src,
                                      cols[:, at:at + CMP // 2].unsqueeze(2).to_broadcast([P, CMP // 2, NCMP]),
                                      ALU.add).then_inc(rc_ready, 1)
            k = filled(dve, ("vc",))
            dve.tensor_copy(VC, ps[0:NCMP, k, 0:G * DH]).then_inc(bank_free[k], 1)
            link(dve.tensor_scalar(cols[:, ROW_Q:ROW_Q + 1], cols[:, ROW_Q:ROW_Q + 1], DH ** -0.5, None, ALU.mult))
            for b in range(4):
                dve.wait_ge(rs_b, b + 1)
                v = slice(2 * b, 2 * b + 2)
                dve.scalar_tensor_tensor(QT[:, v, :], QT[:, v, :], cols[:, ROW_Q:ROW_Q + 1], qsq[:, v, :], ALU.mult, ALU.mult).then_inc(norm_b, 1)
            for br in range(2):
                dve.wait_ge(rs_b, 6 + 2 * br)
                dve.scalar_tensor_tensor(KT[:, br, :, :], KT[:, br, :, :], cols[:, ROW_K + 1 + br:ROW_K + 2 + br], ksq[:, br, :, :],
                                         ALU.mult, ALU.mult).then_inc(norm_b, 1)
            dve.wait_ge(rs_b, 9)
            evacuated(dve, ("kc",))
            dve.scalar_tensor_tensor(KCT, KCT, cols[:, ROW_K:ROW_K + 1], kcsq, ALU.mult, ALU.mult).then_inc(norm_b, 1)
            dve.wait_ge(norm_b, 7)
            evacuated(dve, ("gate",))
            for b in range(1, 4):
                refill(make_lo, dve, ("qB", b))
            for tt in range(TT):
                pc = PC[:, tt, :, 0:NCMP]
                mx, sm = PCS[:, 0, HB * tt:HB * tt + HB], PCS[:, 1, HB * tt:HB * tt + HB]
                for par in range(2):
                    k = filled(dve, ("LC", tt, par))
                    dve.tensor_tensor(pc.rearrange("p (n r) m -> p r n m", r=2)[:, par],
                                      ps[:, k, 0:HB // 2 * NCMP].rearrange("p (n m) -> p n m", m=NCMP),
                                      BCM[:, tt, :, :].rearrange("p m (n r) -> p r n m", r=2)[:, par],
                                      ALU.add).then_inc(bank_free[k], 1)
                for par in range(2):
                    evacuated(dve, ("LC", tt, par))
                link(dve.reduce_max(mx, pc, AX.X))
                dve.tensor_sub(pc, pc, mx.unsqueeze(2).to_broadcast([P, HB, NCMP])).then_inc(pc_shift, 1)
            for tt in range(TT):
                pc = PC[:, tt, :, 0:NCMP]
                sm, wt = PCS[:, 1, HB * tt:HB * tt + HB], PCS[:, 2, HB * tt:HB * tt + HB]
                dve.wait_ge(pc_exp, tt + 1)
                link(dve.reduce_sum(sm, pc, AX.X))
                link(dve.reciprocal(wt, sm))
                link(dve.scalar_tensor_tensor(wt, gates[:, tt, :].rearrange("p (h b) -> p h b", b=3)[:, :, 0],
                                              K("seen")[:, tt:tt + 1], wt, ALU.mult, ALU.mult))
                dve.tensor_tensor(pc, pc, wt.unsqueeze(2).to_broadcast([P, HB, NCMP]), ALU.mult).then_inc(pc_ready, 1)
            dve.wait_ge(bias_in, 16)
            for s in range(len(units) + 1):
                if s < len(units):
                    tt, h = units[s]
                    w = P * (tt + 1)
                    k = filled(dve, ("L", s))
                    if s >= 3:
                        filled(dve, ("PT", s - 3))
                    lb = LB[:, s % 3, :, 0:w]
                    dve.tensor_tensor(lb, ps[:, k, 0:2 * w].rearrange("p (b t) -> p b t", b=2),
                                      BD[:, h:h + 1, T - w:T].to_broadcast([P, 2, w]), ALU.add).then_inc(bank_free[k], 1)
                    evacuated(dve, ("L", s))
                    link(dve.reduce_max(RM[:, s, :], lb, AX.X))
                    dve.tensor_scalar(RM[:, s, :], RM[:, s, :], -1.0, None, ALU.mult).then_inc(row_max, 1)
                if s % 4 == 0 and s < len(units):
                    n = s // 4
                    k = filled(dve, ("PCT", n))
                    if n >= 2:
                        pv_release(dve, 4 * (n - 2) + 3)
                    dve.tensor_copy(PCT[:, n % 2, :], ps[0:NCMP, k, :]).then_inc(bank_free[k], 1)
                if s >= 1:
                    u = s - 1
                    tt, h = units[u]
                    dve.wait_ge(exp_done, 2 * u + 2)
                    link(dve.reciprocal(RW[:, u, :], RS[:, u, :]))
                    dve.tensor_tensor(RW[:, u, :], RW[:, u, :], gates[:, tt, 3 * h + 1:3 * h + 3], ALU.mult).then_inc(weight_ready, 1)
            for n in range(4):
                evacuated(dve, ("OT", n))
            input_lo(OT)
            residual("mixB")
            normalise(3, xn, ROW_FFN + KC, xn_ready)
            for m in range(PAIRS):
                item_lo(dve, m, 0)

            k = filled(dve, ("router",))
            dve.tensor_copy(lg, ps[:, k, 0:TT * E].rearrange("p (a e) -> p a e", a=TT)).then_inc(bank_free[k], 1)
            evacuated(dve, ("router",))
            for tt in range(TT):
                link(dve.max(top[:, tt, :], lg[:, tt, :]))
                link(dve.max_index(topi[:, tt, :], top[:, tt, :], lg[:, tt, :]))
                link(dve.tensor_copy(topf[:, tt, :], topi[:, tt, :]))
                dve.tensor_sub(tw[:, tt, 0:1], top[:, tt, 0:1], top[:, tt, 1:2]).then_inc(top_diff, 1)
                link(dve.tensor_scalar(oh1[:, tt, :], K("experts"), topf[:, tt, 0:1], None, ALU.is_equal))
                link(dve.tensor_scalar(oh2[:, tt, :], K("experts"), topf[:, tt, 1:2], None, ALU.is_equal))
                dve.tensor_tensor(mask[:, tt, :], oh1[:, tt, :], oh2[:, tt, :], ALU.add).then_inc(mask_ready, 1)
            for tt in range(TT):
                dve.wait_ge(top_sig, 2 * tt + 2)
                link(dve.tensor_scalar(gmat[:, tt, :], oh1[:, tt, :], tw[:, tt, 1:2], None, ALU.mult))
                link(dve.scalar_tensor_tensor(gmat[:, tt, :], oh2[:, tt, :], tw[:, tt, 2:3], gmat[:, tt, :], ALU.mult, ALU.add))
            dve.wait_ge(mask_ready, 2)
            k = filled(dve, ("rank",))
            r = ps[:, k, 0:TT * E].rearrange("p (a e) -> p a e", a=TT)
            link(dve.scalar_tensor_tensor(pos, r, 1.0, mask, ALU.add, ALU.mult))
            link(dve.tensor_scalar(pos, pos, 1.0, None, ALU.subtract))
            dve.tensor_copy(cnt, ps[:, k, TT * E:TT * E + E]).then_inc(bank_free[k], 1)
            evacuated(dve, ("rank",))
            link(dve.memset(flag[:, 0:E], 1.0))
            for n in range(1, TURNS):
                link(dve.tensor_scalar(flag[:, E * n:E * n + E], cnt, float(TILE * n), None, ALU.is_gt))
            link(dve.tensor_tensor_scan(incl, K("ones")[:, 0:TURNS * E], flag, 0.0, ALU.mult, ALU.add))
            wide = [P, ITEMS, TURNS * E]
            items3 = K("items").rearrange("p (i c) -> p i c", i=ITEMS)
            link(dve.tensor_tensor(pick, items3, incl.unsqueeze(1).to_broadcast(wide), ALU.subtract))
            link(dve.tensor_scalar(pick, pick, -1.0, None, ALU.is_equal))
            link(dve.tensor_tensor(pick, pick, flag.unsqueeze(1).to_broadcast(wide), ALU.mult))

            def picked(dst, values):
                link(dve.tensor_tensor(prod, pick, values.unsqueeze(1).to_broadcast(wide), ALU.mult))
                link(dve.reduce_sum(dst, prod, AX.X))

            for tt in range(TT):
                c3 = poscand[:, tt, :].rearrange("p (n e) -> p n e", e=E)
                link(dve.tensor_tensor(c3, pos[:, tt:tt + 1, :].to_broadcast([P, TURNS, E]),
                                       K("cand_at").rearrange("p (n e) -> p n e", e=E), ALU.subtract))
                picked(table[:, :, tt], poscand[:, tt, :])
            for tt in range(TT):
                c3 = poscand[:, tt, :].rearrange("p (n e) -> p n e", e=E)
                link(dve.tensor_copy(c3, gmat[:, tt:tt + 1, :].to_broadcast([P, TURNS, E])))
                picked(table[:, :, TT + tt], poscand[:, tt, :])
            picked(route_f, K("cand_e"))
            link(dve.tensor_copy(route[:, ITEMS:ITEMS + 1], incl[:, TURNS * E - 1:TURNS * E]))
            dve.tensor_copy(route[:, 0:ITEMS], route_f).then_inc(routed, 1)
            for n in range(4):
                k = filled(dve, ("htok", n))
                dve.tensor_copy(acc[:, n // 2, 512 * (n % 2):512 * (n % 2) + 512], ps[:, k, :]).then_inc(bank_free[k], 1)
            for n in range(4):
                evacuated(dve, ("htok", n))
            dve.wait_ge(routed, 1)

            n_items = dve.value_load(route[0:1, ITEMS:ITEMS + 1], min_val=E, max_val=ITEMS - 1)
            with dve.Fori(0, n_items) as i:
                b, k = bank_count(("GT",), i)
                dve.tensor_copy(cur, table[:, bass.ds(i, 1), :].rearrange("p o n -> p (o n)")).then_inc(cur_ready, 1)
                dve.wait_ge(cur_ready, i + 1)
                for tt in range(TT):
                    dve.tensor_scalar(sel[:, tt, :], K("slots"), cur[:, tt:tt + 1], None, ALU.is_equal).then_inc(sel_ready, 1)
                    dve.tensor_scalar(selg[:, tt, :], K("slots"), cur[:, tt:tt + 1], cur[:, TT + tt:TT + tt + 1],
                                      ALU.is_equal, ALU.mult).then_inc(sel_ready, 1)
                for n in range(2):
                    bg, kg = bank_count(("gather", n), i)
                    dve.wait_ge(xg_hi_ready, 2 * i + n + 1)
                    dve.tensor_tensor(xg_lo[:, 4 * n:4 * n + 4, :], ps[:, bg, :].rearrange("p (c t) -> p c t", c=4),
                                      xg_hi[:, 4 * n:4 * n + 4, :].bitcast(F32), ALU.subtract).then_inc(bank_free[bg], 1)
                dve.wait_ge(bank_full[b], k + 1)
                dve.tensor_copy(gt, ps[:, b, 0:T]).then_inc(bank_free[b], 1)

                def hidden_lo(j):
                    b, k = bank_count(("hT", j), i)
                    dve.wait_ge(hid_hi, FFN // 256 + i * NPAIR + j + 1)
                    dve.tensor_tensor(hid[:, j % 2, 1, :], ps[:, b, :], hid[:, j % 2, 0, :].bitcast(F32), ALU.subtract).then_inc(bank_free[b], 1)

                for m, (kind, j, half) in enumerate(ITEM):
                    item_refill_lo(dve, m, i)
                    if kind == "gate" and half == 1 and j:
                        hidden_lo(j - 1)
                    if kind == "up" and half == 1:
                        b, k = bank_count(("gate", j), i)
                        dve.wait_ge(bank_free[b], k + 1)
                        b, k = bank_count(("up", j), i)
                        dve.wait_ge(bank_full[b], k + 1)
                        bh, kh = bank_count(("hT", j - 2), i) if j >= 2 else bank_count(("hT", NPAIR - 1 - j), i - 1)
                        dve.wait_ge(bank_full[bh], kh + 1)
                        dve.tensor_tensor(HM[:, j % 2, :], SU[:, j % 2, :], ps[:, b, :], ALU.mult).then_inc(bank_free[b], 1)
                    if kind == "dn" and j == NPAIR - 2 and half == 1:
                        hidden_lo(NPAIR - 1)
                b, k = bank_count(("y", 0), i)
                dve.wait_ge(bank_full[b], k + 1)
                dve.tensor_copy(yt[:, 0:512], ps[:, b, :]).then_inc(bank_free[b], 1)
                for n in range(4):
                    b, k = bank_count(("scatter", n), i)
                    dve.wait_ge(bank_full[b], k + 1)
                    v = acc[:, n // 2, 512 * (n % 2):512 * (n % 2) + 512]
                    dve.tensor_tensor(v, v, ps[:, b, :], ALU.add).then_inc(bank_free[b], 1)

        @block.tensor
        def _(pe):
            ident, ones, halves = K("ident"), K("ones"), K("halves")

            def mm(o, w, x, start, stop, **kw):
                return pe.matmul(o, w, x, start=start, stop=stop, **kw)

            pe.wait_ge(small_loaded, 16 * 8)
            pe.wait_ge(ones_row, 1)
            pe.wait_ge(rows_loaded, 16 * 11)
            b = free_bank(pe, ("rows", 0))
            pe.transpose(ps[:, b, 0:ROWS], rows[0:ROWS, :], ident[0:ROWS, 0:ROWS]).then_inc(bank_full[b], 1)
            pe.wait_ge(x_loaded, 16)
            for n in range(4):
                b = free_bank(pe, ("xT", n))
                for c in range(2):
                    for tt in range(TT):
                        last = pe.transpose(ps[:, b, T * c + P * tt:T * c + P * tt + P],
                                            x_in[:, tt, P * (2 * n + c):P * (2 * n + c) + P], ident)
                last.then_inc(bank_full[b], 1)

            def norm_sum(s):
                b = free_bank(pe, ("sum", s))
                for c in range(KC):
                    if c % 2 == 0:
                        pe.wait_ge(squared, 4 * s + c // 2 + 1)
                    last = mm(ps[:, b, 0:T], ones, xn[:, c, :], c == 0, c == KC - 1)
                last.then_inc(bank_full[b], 1)

            def split_product(o, w, x, start, stop, **kw):
                mm(o, w[0], x[0], start, False, **kw)
                mm(o, w[0], x[1], False, False, **kw)
                return mm(o, w[1], x[0], False, stop, **kw)

            def parts(pair, f):
                return [f(v) for v in pair]

            def x_part(c, tokens=slice(0, T)):
                return [v[:, T * c + tokens.start:T * c + tokens.stop] for v in (x_hi, x_lo)]

            x_pieces = [0]

            def project(name, wait_x):
                pair = pair_ready(pe, name)
                b = free_bank(pe, name)
                for m in range(2):
                    for c in range(KC):
                        if wait_x and m == 0 and c % 2 == 0:
                            pe.wait_ge(x_lo_ready, x_pieces[0] + c // 2 + 1)
                        w = [v[:, 256 * c + P * m:256 * c + P * m + P] for v in pair]
                        last = split_product(ps[:, b, T * m:T * m + T], w, x_part(c), c == 0, c == KC - 1)
                last.then_inc(bank_full[b], 1)
                if wait_x:
                    x_pieces[0] += 4

            def project_tokens(name):
                pair = pair_ready(pe, name)
                b = free_bank(pe, name)
                for tt in range(TT):
                    for c in range(KC):
                        w = [v[:, 256 * c:256 * c + 256] for v in pair]
                        last = split_product(ps[:, b, 256 * tt:256 * tt + 256], x_part(c, slice(P * tt, P * tt + P)), w, c == 0, c == KC - 1)
                last.then_inc(bank_full[b], 1)

            def dense(name):
                for b in range(4):
                    project((name, b), b == 0)

            norm_sum(0)
            dense("f")
            for b in range(4):
                project_tokens(("i", b))
            for name in ("g", "q"):
                for b in range(4):
                    project((name, b), False)

            for b in range(4):
                evacuated(pe, ("q", b))
            pe.wait_ge(km_ready, 4)
            pe.wait_ge(ke_ready, 4)
            for tt in range(TT):
                for a in range(2):
                    b = free_bank(pe, ("A", tt, a))
                    for n in range(4):
                        v = (4 * a + n, slice(P * tt, P * tt + P))
                        last = mm(ps[:, b, P * n:P * n + P], KM[:, v[0], v[1]], QM[:, v[0], v[1]], True, True)
                    last.then_inc(bank_full[b], 1)
                for a in range(2):
                    b = free_bank(pe, ("KH", tt, a))
                    for n in range(4):
                        last = pe.transpose(ps[:, b, P * n:P * n + P], KE[:, 4 * a + n, P * tt:P * tt + P], ident)
                    last.then_inc(bank_full[b], 1)
            for b in range(4):
                evacuated(pe, ("i", b))
            per = NCH // TT
            for tt in range(TT):
                for a in range(2):
                    evacuated(pe, ("A", tt, a))
                    evacuated(pe, ("KH", tt, a))
                banks = [free_bank(pe, ("O", tt, a)) for a in range(2)]
                for h in range(HEADS_A):
                    mm(ps[:, banks[h // 4], P * (h % 4):P * (h % 4) + P], VA[:, tt, P * h:P * h + P], AM[:, tt, h, :],
                       h % 4 == 0, False, skip_group_check=True)
                for c in range(per):
                    gc = tt * per + c
                    r = slice(CH * c, CH * c + CH)
                    if gc < NCH - 1:
                        for a in range(2):
                            b = free_bank(pe, ("U", gc, a))
                            for n in range(4):
                                h = 4 * a + n
                                last = mm(ps[:, b, P * n:P * n + P], KH[r, tt, h, :], VA[r, tt, P * h:P * h + P], True, True)
                            last.then_inc(bank_full[b], 1)
                    if gc >= 1:
                        for a in range(2):
                            evacuated(pe, ("U", gc - 1, a))
                        for h in range(HEADS_A):
                            b = banks[h // 4]
                            at = P * (h % 4) + CH * c
                            last = mm(ps[:, b, at:at + CH], ST[:, gc % 2, h, :], QS[:, h, CH * gc:CH * gc + CH], False,
                                      c == per - 1, skip_group_check=True)
                            if c == per - 1 and h % 4 == 3:
                                last.then_inc(bank_full[b], 1)
                        if c < per - 1:
                            last.then_inc(state_used, 1)
            for b4 in range(4):
                pe.wait_ge(osq_ready, 4)
                b = free_bank(pe, ("osum", b4))
                mm(ps[:, b, :], ones, OSQ[:, 2 * b4:2 * b4 + 2, :], True, True).then_inc(bank_full[b], 1)
            dense("mixA")

            norm_sum(1)
            def down(j):
                pair = pair_ready(pe, ("dn", j))
                pe.wait_ge(hid_lo, j + 1)
                for k in range(2):
                    first, final = j == 0 and k == 0, j == FFN // 256 - 1 and k == 1
                    h = [hid[:, j % 2, part, T * k:T * k + T] for part in range(2)]
                    for m in range(KC):
                        b = J[("down", m // 2)][0]
                        w = [v[:, D * k + P * m:D * k + P * m + P] for v in pair]
                        last = split_product(ps[:, b, T * (m % 2):T * (m % 2) + T], w, h, first and m % 2 == 0, final, skip_group_check=True)
                        if final and m % 2 == 1:
                            last.then_inc(bank_full[b], 1)
                if j < FFN // 256 - 1:
                    last.then_inc(half_used, 1)

            for n in range(4):
                free_bank(pe, ("down", n))
            for j in range(FFN // 256 + 1):
                if j < FFN // 256:
                    project(("ga", j), j == 0)
                    project(("up", j), False)
                if j:
                    down(j - 1)
            pe.wait_ge(onehot_loaded, 16)
            b = free_bank(pe, ("biasw",))
            mm(ps[0:HB, b, :], tb[:, :], OH[:, 0:2 * T], True, True).then_inc(bank_full[b], 1)
            for tt in range(TT):
                b = free_bank(pe, ("biasc", tt))
                for n in range(NCMP):
                    at = 2 * T + n * T + P * tt
                    last = mm(ps[:, b, HB * n:HB * n + HB], OH[:, at:at + P], tb[:, :], True, True)
                last.then_inc(bank_full[b], 1)

            norm_sum(2)
            project(("kv0", 0), True)
            project(("kv0", 1), False)
            for br in (1, 2):
                project(("k", br), False)
                project_tokens(("v", br))
            dense("qB")
            b = free_bank(pe, ("gate",))
            for tt in range(TT):
                for k in range(KC):
                    last = mm(ps[:, b, 48 * tt:48 * tt + 48], xn[:, k, P * tt:P * tt + P], w_gate[:, k, :], k == 0, k == KC - 1)
            last.then_inc(bank_full[b], 1)
            for s in range(2):
                pe.wait_ge(rc_ready, G * (s + 1))
                b = free_bank(pe, ("hid", s))
                for half in range(2):
                    w = raw_arrived(pe, ("w1", 2 * s + half)).rearrange("p (k n) -> p k n", n=HID)
                    for m in range(2):
                        for k in range(CMP // 4):
                            last = mm(ps[:, b, 64 * m:64 * m + G * NCMP], w[:, k, P * m:P * m + P], RC[:, s, CMP // 4 * half + k, :],
                                      half == 0 and m == 0 and k == 0, half == 1 and k == CMP // 4 - 1, skip_group_check=True)
                    last.then_inc(w1_used if half == 0 else bank_full[b], 1)
            evacuated(pe, ("hid", 0))
            b = free_bank(pe, ("kc",))
            for m in range(2):
                last = mm(ps[:, b, 0:G * NCMP], w2[:, 0, m, :, :].rearrange("p a d -> p (a d)"), GH[:, 0, m, :], m == 0, m == 1)
            last.then_inc(bank_full[b], 1)
            evacuated(pe, ("hid", 1))
            b = free_bank(pe, ("vc",))
            for g in range(G):
                for m in range(2):
                    last = mm(ps[0:NCMP, b, DH * g:DH * g + DH], GH[:, 1, m, NCMP * g:NCMP * g + NCMP], w2[:, 1, m, 0, :], m == 0, m == 1)
            last.then_inc(bank_full[b], 1)
            for n, (job, v) in enumerate([(("qsum", n), qsq[:, 2 * n:2 * n + 2, :]) for n in range(4)]
                                         + [(("ksum", n), ksq[:, n // 2, 2 * (n % 2):2 * (n % 2) + 2, :]) for n in range(4)] + [(("kcsum",), kcsq)]):
                pe.wait_ge(sq_b, n + 1)
                b = free_bank(pe, job)
                width = G * NCMP if job == ("kcsum",) else 512
                mm(ps[:, b, 0:width], halves, v, True, True).then_inc(bank_full[b], 1)
            pe.wait_ge(norm_b, 7)
            for tt in range(TT):
                for par in range(2):
                    b = free_bank(pe, ("LC", tt, par))
                    half = slice(DH * par, DH * par + DH)
                    for n in range(HB // 2):
                        g = (2 * n + par) // HP
                        last = mm(ps[:, b, NCMP * n:NCMP * n + NCMP], QT[half, n, P * tt:P * tt + P],
                                  KCT[half, NCMP * g:NCMP * g + NCMP], True, True)
                    last.then_inc(bank_full[b], 1)

            def scores(u):
                tt, h = units[u]
                half, w = slice(DH * (h % 2), DH * (h % 2) + DH), P * (tt + 1)
                b = free_bank(pe, ("L", u))
                for br in range(2):
                    last = mm(ps[:, b, w * br:w * br + w], QT[half, h // 2, P * tt:P * tt + P], KT[half, br, h // HP, 0:w], True, True)
                last.then_inc(bank_full[b], 1)

            def cmp_turned(n):
                tt, g = n // G, n % G
                pe.wait_ge(pc_ready, tt + 1)
                b = free_bank(pe, ("PCT", n))
                for hp in range(HP):
                    last = pe.transpose(ps[0:NCMP, b, P * hp:P * hp + P], PC[:, tt, HP * g + hp, 0:NCMP], ident)
                last.then_inc(bank_full[b], 1)

            def turned(u):
                tt = units[u][0]
                pe.wait_ge(p_ready, 2 * u + 2)
                b = free_bank(pe, ("PT", u))
                for br in range(2):
                    for s in range(tt + 1):
                        at = P * ((tt + 1) * br + s)
                        last = pe.transpose(ps[:, b, at:at + P], LB[:, u % 3, br, P * s:P * s + P], ident)
                last.then_inc(bank_full[b], 1)

            def values(u):
                tt, h = units[u]
                g, hp, half = h // HP, h % HP, slice(DH * (h % 2), DH * (h % 2) + DH)
                n = u // HP
                if u % 8 == 0:
                    free_bank(pe, ("OT", u // 8))
                b = J[("OT", u // 8)][0]
                evacuated(pe, ("PCT", n))
                evacuated(pe, ("PT", u))
                at = P * (h // 2 % 4)
                o = ps[half, b, at:at + P]
                mm(o, VC[:, DH * g:DH * g + DH], PCT[:, n % 2, P * hp:P * hp + P], True, False)
                for br in range(2):
                    for s in range(tt + 1):
                        at = P * ((tt + 1) * br + s)
                        last = mm(o, VB[:, br, s, DH * g:DH * g + DH], PTB[:, u % 2, at:at + P], False, br == 1 and s == tt)
                last.then_inc(bank_full[b] if u % 8 == 7 else pv_done, 1)

            evacuated(pe, ("vc",))
            for br in (1, 2):
                evacuated(pe, ("v", br))
            for s in range(len(units) + 3):
                if s < len(units):
                    scores(s)
                    if s % HP == 0:
                        cmp_turned(s // HP)
                if 2 <= s < len(units) + 2:
                    turned(s - 2)
                if s >= 3:
                    values(s - 3)
            for n in range(4):
                evacuated(pe, ("OT", n))
            dense("mixB")

            norm_sum(3)
            pe.wait_ge(xn_ready, 5 * KC)
            b = free_bank(pe, ("router",))
            for tt in range(TT):
                for k in range(KC):
                    last = mm(ps[:, b, E * tt:E * tt + E], xn[:, k, P * tt:P * tt + P], w_router[:, k, :], k == 0, k == KC - 1)
            last.then_inc(bank_full[b], 1)
            for name, src in (("xtok", xn), ("htok", hT)):
                for n in range(4):
                    b = free_bank(pe, (name, n))
                    for c in range(4):
                        last = pe.transpose(ps[:, b, P * c:P * c + P], src[:, 4 * (n % 2) + c, P * (n // 2):P * (n // 2) + P], ident)
                    last.then_inc(bank_full[b], 1)
            pe.wait_ge(mask_ready, 2)
            b = free_bank(pe, ("rank",))
            mm(ps[:, b, 0:E], K("before"), mask[:, 0, :], True, True)
            mm(ps[:, b, E:2 * E], ones, mask[:, 0, :], True, False)
            mm(ps[:, b, E:2 * E], K("before"), mask[:, 1, :], False, True)
            mm(ps[:, b, 2 * E:3 * E], ones, mask[:, 0, :], True, False)
            mm(ps[:, b, 2 * E:3 * E], ones, mask[:, 1, :], False, True).then_inc(bank_full[b], 1)
            for n in range(4):
                evacuated(pe, ("xtok", n))
            pe.wait_ge(routed, 1)
            n_items = pe.value_load(route[0:1, ITEMS:ITEMS + 1], min_val=E, max_val=ITEMS - 1)
            with pe.Fori(0, n_items) as i:
                def free(name):
                    b, k = bank_count(name, i)
                    pe.wait_ge(bank_free[b], k)
                    return b

                def out_of_psum(name):
                    b, k = bank_count(name, i)
                    pe.wait_ge(bank_free[b], k + 1)

                def pair(m):
                    pe.wait_ge(lo_ready[m % PAIRS], pair_count(m, i) + 1)
                    return w_hi[:, m % PAIRS, :], w_lo[:, m % PAIRS, :]

                pe.wait_ge(sel_ready, i * 4 + 4)
                for n in range(2):
                    b = free(("gather", n))
                    for m in range(4):
                        d = 4 * n + m
                        for tt in range(TT):
                            last = mm(ps[:, b, TILE * m:TILE * m + TILE], xtok[:, tt, P * d:P * d + P], sel[:, tt, :], tt == 0, tt == TT - 1)
                    last.then_inc(bank_full[b], 1)
                b = free(("GT",))
                for tt in range(TT):
                    last = pe.transpose(ps[0:TILE, b, P * tt:P * tt + P], selg[:, tt, :], ident)
                last.then_inc(bank_full[b], 1)
                for n in range(2):
                    out_of_psum(("gather", n))
                def turned_hidden(j):
                    out_of_psum(("up", j))
                    b = free(("hT", j))
                    for c in range(4):
                        last = pe.transpose(ps[:, b, P * c:P * c + P], HM[:, j % 2, P * c:P * c + P], ident)
                    last.then_inc(bank_full[b], 1)

                for m, (kind, j, half) in enumerate(ITEM):
                    if kind == "dn":
                        if j == NPAIR - 1 and half == 0:
                            turned_hidden(j)
                        w = pair(m)
                        if half == 0:
                            out_of_psum(("hT", j))
                            if j == 0:
                                for n in range(2):
                                    free(("y", n))
                        for c in (2 * half, 2 * half + 1):
                            h = [hid[:, j % 2, part, P * c:P * c + P] for part in range(2)]
                            for n in range(2):
                                b = JTURN[("y", n)][0]
                                at = D * (c % 2) + 512 * n
                                final = j == NPAIR - 1 and c == 3
                                last = split_product(ps[:, b, :], h, [v[:, at:at + 512] for v in w], j == 0 and c == 0, final)
                                if final:
                                    last.then_inc(bank_full[b], 1)
                        if m in ALONE:
                            last.then_inc(half_used, 1)
                        continue
                    w = pair(m)
                    b = free((kind, j)) if half == 0 else JTURN[(kind, j)][0]
                    for k in range(4):
                        x = [v[:, 4 * half + k, :] for v in (xg_hi, xg_lo)]
                        last = split_product(ps[:, b, :], x, [v[:, 512 * k:512 * k + 512] for v in w], half == 0 and k == 0, half == 1 and k == 3)
                    last.then_inc(half_used if half == 0 else bank_full[b], 1)
                    if kind == "gate" and half == 1 and j:
                        turned_hidden(j - 1)
                out_of_psum(("GT",))
                for n in range(2):
                    out_of_psum(("y", n))
                for n in range(4):
                    b = free(("scatter", n))
                    mm(ps[:, b, :], gt[:, P * (n // 2):P * (n // 2) + P], yt[:, 512 * (n % 2):512 * (n % 2) + 512], True, True).then_inc(bank_full[b], 1)


_OUT = (1, T, D)


def kernel(**inputs):
    import numpy as _np
    import concourse.bacc as _bacc
    from concourse import mybir as _mybir
    from concourse.bass_utils import run_bass_kernel_spmd as _run

    nc = _bacc.Bacc("TRN2", target_bir_lowering=False, num_devices=1)
    arrays, ins = {}, {}
    given = {k: _np.ascontiguousarray(v) for k, v in inputs.items()}
    given["tables"] = _np.concatenate(list(constants().values()), axis=1)
    given["bias_onehot"] = bias_tables()
    for name, a in given.items():
        arrays[f"in_{name}"] = a
        ins[name] = nc.dram_tensor(f"in_{name}", a.shape, _mybir.dt.from_np(a.dtype), kind="ExternalInput").ap()
    out = nc.dram_tensor("out", _OUT, _mybir.dt.from_np(_np.dtype("float32")), kind="ExternalOutput").ap()
    trunk(nc, ins, out)
    r = _run(nc, [arrays], core_ids=[0])
    return r.results[0]["out"]
```

```python
import math
from contextlib import ExitStack

import numpy as np

import concourse.bass as bass
from concourse import mybir

F32 = mybir.dt.float32
F32R = mybir.dt.float32r
I32 = mybir.dt.int32
U32 = mybir.dt.uint32
ALU = mybir.AluOpType
ACT = mybir.ActivationFunctionType
AX = mybir.AxisListType

P = 128
D = 1024
KC = D // P
T = 256
TT = T // P
BANKS = 8
RING, SLOT = 6, 2048
PAIRS = 3

HEADS_A = 8
CH = 32
NCH = T // CH
MID = CH // 2 - 1

FFN = 2816
FK = FFN // P

HB, G, HP, DH = 16, 4, 4, 64
CMP, STRIDE, HID = 32, 16, 256
NCMP = T // STRIDE - 1
BUCKETS, MAXDIST = 32, 2048
NEG = -1e30

E, ED = 8, 3584
EK = ED // P
TILE = 128
TURNS = -(-T // TILE)
ITEMS = 16
assert E + 2 * T // TILE < ITEMS
NPAIR = ED // 512
NDOWN = ED // 512
ITEM = [(kind, j, half) for j in range(NPAIR + 1) for kind in ("gate", "up", "dn") for half in range(2)
        if (kind == "dn" and j > 0) or (kind != "dn" and j < NPAIR)]
ITEM = [(kind, j - 1 if kind == "dn" else j, half) for kind, j, half in ITEM]
PER_ITEM = len(ITEM)
LAG = 3
GT_AFTER = NPAIR // 2
assert PER_ITEM % RING == 0 and PER_ITEM % PAIRS == 0 and NPAIR % 2 == 1
EPS = 1e-6


def bucket(dist):
    d = np.maximum(dist, 0)
    exact = BUCKETS // 2
    large = exact + (np.log(np.maximum(d, 1).astype(np.float32) / np.float32(exact))
                     / np.float32(math.log(MAXDIST / exact)) * np.float32(BUCKETS - exact)).astype(np.int32)
    return np.where(d < exact, d, np.minimum(large, BUCKETS - 1))


def constants():
    p = np.arange(P)
    c = {}
    c["ident"] = np.eye(P)
    c["ones"] = np.ones((P, P))
    c["halves"] = (p[:, None] // DH == p[None, :] // DH)
    c["before"] = (p[:, None] < p[None, :])
    c["causal"] = (p[:, None] // CH == p[None, :] // CH) & (p[:, None] <= p[None, :])
    c["restart"] = np.tile(np.arange(T)[None, :] % CH != 0, (P, 1))
    c["slots"] = np.tile(np.arange(TILE)[None, :], (P, 1))
    c["experts"] = np.tile(np.arange(E)[None, :], (P, 1))
    c["items"] = np.tile(np.repeat(np.arange(ITEMS), TURNS * E)[None, :], (P, 1))
    c["cand_e"] = np.tile((np.arange(TURNS * E) % E)[None, :], (P, 1))
    c["cand_at"] = np.tile((np.arange(TURNS * E) // E * TILE)[None, :], (P, 1))
    c["seen"] = (p[:, None] + P * np.arange(TT)[None, :]) >= CMP - 1
    return {k: v.astype(np.float32) for k, v in c.items()}


def layout(c):
    at, out = 0, {}
    for k, v in c.items():
        out[k] = (at, v.shape[1])
        at += v.shape[1]
    return out, at


def bias_tables():
    dist = T - 1 - np.arange(2 * T)
    win = np.zeros((BUCKETS + 1, 2 * T), np.float32)
    win[:BUCKETS] = (bucket(dist)[None, :] == np.arange(BUCKETS)[:, None]) & (dist >= 0)
    win[BUCKETS] = np.where(dist >= 0, 0.0, NEG)
    dist = (np.arange(T)[None, :] - STRIDE * np.arange(NCMP)[:, None] - (CMP - 1)).reshape(-1)
    cmp = np.zeros((BUCKETS + 1, NCMP * T), np.float32)
    cmp[:BUCKETS] = (bucket(dist)[None, :] == np.arange(BUCKETS)[:, None]) & (dist >= 0)
    cmp[BUCKETS] = np.where(dist >= 0, 0.0, NEG)
    return np.concatenate([win, cmp], axis=1)


ROW_MIX, ROW_FFN, ROW_KV, ROW_LB = 0, 2 * KC, 4 * KC, 5 * KC
ROW_O, ROW_Q, ROW_K, ROW_POS = 7 * KC, 7 * KC + 1, 7 * KC + 2, 7 * KC + 5
ROWS = ROW_POS + 2 * CMP * DH // P


def job_table():
    used, jobs, turn = [0] * BANKS, {}, [0]

    def job(name, bank=None, among=range(BANKS)):
        if bank is None:
            bank = among[turn[0] % len(among)]
            turn[0] += 1
        jobs[name] = (bank, used[bank])
        used[bank] += 1

    for b in range(4):
        job(("xT", b))
    job(("rows", 0))
    job(("sum", 0))
    for name in ("f", "i", "g", "q"):
        for b in range(4):
            job((name, b))
    for tt in range(TT):
        for a in range(2):
            job(("A", tt, a))
        for a in range(2):
            job(("KH", tt, a))
    for tt in range(TT):
        for a in range(2):
            job(("O", tt, a), a)
        for c in range(NCH // TT):
            if tt * NCH // TT + c < NCH - 1:
                for a in range(2):
                    job(("U", tt * NCH // TT + c, a), 4 + 2 * (c % 2) + a)
    turn[0] = 0
    for b in range(4):
        job(("osum", b))
    for b in range(4):
        job(("mixA", b))
    job(("sum", 1))
    for j in range(FFN // 256):
        job(("ga", j), 2 * (j % 2))
        job(("up", j), 2 * (j % 2) + 1)
    job(("biasw",), 0)
    for tt in range(TT):
        job(("biasc", tt), 1 + tt)
    for b in range(4):
        job(("down", b), 4 + b)
    turn[0] = 0
    job(("sum", 2))
    for b in range(2):
        job(("kv0", b))
    for br in (1, 2):
        job(("k", br))
        job(("v", br))
        job(("ksum", br))
    for b in range(4):
        job(("qB", b))
    job(("gate",))
    for b in range(4):
        job(("qsum", b))
    for s in range(2):
        job(("hid", s))
    job(("kc",))
    job(("vc",))
    job(("kcsum",))
    for tt in range(TT):
        for par in range(2):
            job(("LC", tt, par), 7 - par)
    for u in range(TT * HB):
        job(("L", u), u % 2)
        job(("PT", u), 2 + u % 2)
    for n in range(TT * G):
        job(("PCT", n), 4)
    for n in range(TT * 2):
        job(("OT", n), 5 + n % 2)
    turn[0] = 0
    for b in range(4):
        job(("mixB", b))
    job(("sum", 3))
    job(("logits",))
    job(("router",))
    job(("rank",))
    for n in range(4):
        job(("xtok", n))
    for n in range(2):
        job(("gather", n), 6 + n)
    for n in range(4):
        job(("htok", n), 2 + n)
    base, turns = list(used), {}

    def inner(name, bank):
        turns[name] = (bank, used[bank] - base[bank])
        used[bank] += 1

    for n in range(4):
        inner(("scatter", n), 6 + n % 2)
    for j in range(NPAIR):
        if j == GT_AFTER + 1:
            inner(("GT",), 6)
        inner(("gate", j), 2 * (j % 2))
        inner(("up", j), 2 * (j % 2) + 1)
        inner(("hT", j), 7 - j % 2)
    for b in range(2):
        inner(("y", b), 4 + b)
    for n in range(2):
        inner(("gather", n), 6 + n)
    per = [used[b] - base[b] for b in range(BANKS)]
    return jobs, base, turns, per


def stream_table():
    names = [(n, b) for n in ("f", "i", "g", "q", "mixA") for b in range(4)]
    for j in range(FFN // 256 + 1):
        if j < FFN // 256:
            names += [("ga", j), ("up", j)]
        if j:
            names += [("dn", j - 1)]
    names += [("kv0", 0), ("kv0", 1), ("k", 1), ("v", 1), ("k", 2), ("v", 2)]
    names += [("qB", b) for b in range(4)]
    names += [("w1", b) for b in range(4)]
    names += [("mixB", b) for b in range(4)]
    raw, pair, slots, pairs = {}, {}, [0] * RING, [0] * PAIRS
    for n, name in enumerate(names):
        raw[name] = (n % RING, slots[n % RING])
        slots[n % RING] += 1
        if name[0] != "w1":
            m = sum(pairs) % PAIRS
            pair[name] = (m, pairs[m])
            pairs[m] += 1
    return names, raw, slots, pair, pairs


def trunk(nc, ins, out):
    J, JBASE, JTURN, JPER = job_table()
    HALVES, RAW, RAW_BASE, PAIR, PAIR_BASE = stream_table()
    CPOS, CWIDTH = layout(constants())
    ctx = ExitStack()
    with ctx:
        def sb(name, shape, dt=F32):
            return ctx.enter_context(nc.sbuf_tensor(name, shape, dt))

        def sem(name):
            return ctx.enter_context(nc.semaphore(name))

        ring = sb("ring", [P, RING, SLOT])
        w_hi = sb("w_hi", [P, PAIRS, SLOT], F32R)
        w_lo = sb("w_lo", [P, PAIRS, SLOT], F32R)
        x_hi = sb("x_hi", [P, KC * T], F32R)
        x_lo = sb("x_lo", [P, KC * T], F32R)
        with nc.sbuf_tensor("silu_g", [P, KC, T], F32) as silu_g:
            pass
        hid = sb("hid", [P, 2, 2, 512], F32R)
        hT = sb("hT", [P, KC, T])
        xn = sb("xn", [P, KC, T])
        const = sb("const", [P, CWIDTH])
        cols = sb("cols", [P, ROWS])
        rstd = sb("rstd", [P, T])
        eps = sb("eps", [P, 1])
        w_router = sb("w_router", [P, KC, E])
        w_gate = sb("w_gate", [P, KC, 3 * HB])
        w2 = sb("w2", [P, 2, 2, 2, DH])
        tb = sb("tb", [BUCKETS + 1, HB])
        AR = 15500
        arena = sb("arena", [P, AR])
        ps = ctx.enter_context(nc.psum_tensor("ps", [P, BANKS, 512], F32))
        scratch = nc.dram_tensor("bias_rows", (P, HB, T + P), F32, kind="Internal")

        def K(name):
            at, n = CPOS[name]
            return const[:, at:at + n]

        def area(at, *shape, parts=P):
            n = int(np.prod(shape))
            assert at + n <= AR, (at, n)
            v = arena[0:parts, at:at + n]
            if len(shape) == 1:
                return v
            letters = "abcd"[:len(shape)]
            return v.rearrange(f"p ({' '.join(letters)}) -> p {' '.join(letters)}",
                               **{x: s for x, s in zip(letters[1:], shape[1:])})

        x_in = area(0, TT, D)
        rows = area(2048, P)
        FG = area(0, KC, T)
        BC = area(2048, KC, T)
        QM, KM = area(4096, KC, T), area(6144, KC, T)
        QS, KE = area(8192, KC, T), area(10240, KC, T)
        VA = area(12288, TT, D)
        GA = silu_g
        AM = area(0, TT, HEADS_A, P)
        KH = area(2048, TT, HEADS_A, P)
        ST = xn[:, :, :].rearrange("p (s a) t -> p s (a t)", s=2).rearrange("p s (h e) -> p s h e", e=P)
        OA = KE
        OSQ, ORS = KM, QM
        dec = area(14336, KC * NCH)
        lbs = area(14336 + KC * NCH, 3, KC)
        HF = area(0, 2, 512)
        SG = area(1024, 2, 512)
        OH = area(2048, 2 * T + NCMP * T, parts=BUCKETS + 1)
        biasrow = area(6400, 2 * T, parts=HB)
        OT = xn
        QT = area(0, KC, T)
        KT = area(2048, 2, G, T)
        raw0 = area(4096, 4, T)
        X2 = area(5120, 2, G, T)
        RC = area(7168, 2, CMP // 2, G * NCMP)
        BD = area(9088, HB, T)
        BCM = area(13184, TT, NCMP, HB)
        VB = area(13664, 2, TT, G * DH)
        GH = area(14688, 2, 2, G * NCMP)
        KCT = area(14928, G * NCMP)
        VC = area(14988, G * DH, parts=NCMP)
        gates = area(15244, TT, 3 * HB)
        qsq = silu_g
        ksq = [silu_g[:, 4 + 2 * br:6 + 2 * br, :] for br in range(2)]
        kcsq = area(8192, G * NCMP)
        LB = area(4096, LAG + 1, 2, T)
        PTB = area(6144, 2, 512)
        PC = area(8512, TT, HB, NCMP + 1)
        PCS = area(7168, 3, TT * HB)
        RM = area(7296, TT * HB, 2)
        RS = area(7360, TT * HB, 2)
        RW = area(7424, TT * HB, 2)
        PCT = area(7488, 2, 512, parts=NCMP)
        xtok = area(0, TT, D)
        acc = area(2048, TT, D)
        xg_hi = x_hi[:, 0:KC * TILE].rearrange("p (c t) -> p c t", c=KC)
        xg_lo = x_lo[:, 0:KC * TILE].rearrange("p (c t) -> p c t", c=KC)
        HM = area(4096, 2, 512)
        SU = area(5120, 2, 512)
        yt = area(6144, D)
        sel = area(7168, TT, TILE)
        selg = area(7424, TT, TILE)
        gt = area(7680, T)
        table = area(9984, ITEMS, 4)
        cur = area(10048, 4)
        lg = area(10052, TT, E)
        top = area(10068, TT, 8)
        topi = area(10084, TT, 8).bitcast(U32)
        topf = area(10100, TT, 8)
        tw = area(10116, TT, 3)
        oh = area(10122, TT, 2, E)
        mask, gmat, pos = area(10154, TT, E), area(10170, TT, E), area(10186, TT, E)
        cnt = area(10202, E)
        flag, incl = area(10210, TURNS * E), area(10234, TURNS * E)
        pick = area(10258, ITEMS, TURNS * E)
        prod = area(10642, ITEMS, TURNS * E)
        poscand = area(11026, TT, TURNS * E)
        route_f = area(11074, ITEMS)
        route = area(11090, 2 * ITEMS).bitcast(I32)

        lgT = area(11122, T, parts=E)

        bank_full = [sem(f"bank_full{b}") for b in range(BANKS)]
        bank_free = [sem(f"bank_free{b}") for b in range(BANKS)]
        slot_ready = [sem(f"slot_ready{s}") for s in range(RING)]
        x_loaded, const_loaded = sem("x_loaded"), sem("const_loaded")
        rows_loaded, small_loaded = sem("rows_loaded"), sem("small_loaded")
        onehot_loaded, ones_row = sem("onehot_loaded"), sem("ones_row")
        eps_set = sem("eps_set")
        hi_ready = [sem(f"hi_ready{m}") for m in range(PAIRS)]
        lo_ready = [sem(f"lo_ready{m}") for m in range(PAIRS)]
        half_used, w1_used = sem("half_used"), sem("w1_used")
        x_hi_ready, x_lo_ready, hid_hi, hid_lo = sem("x_hi_ready"), sem("x_lo_ready"), sem("hid_hi"), sem("hid_lo")
        squared, rstd_ready, xn_ready = sem("squared"), sem("rstd_ready"), sem("xn_ready")
        act_step, dve_step, pool_step = sem("act_step"), sem("dve_step"), sem("pool_step")
        lb_diff, lb_ready, fgate_ready = sem("lb_diff"), sem("lb_ready"), sem("fgate_ready")
        logf_ready, k_ready, cum_ready = sem("logf_ready"), sem("k_ready"), sem("cum_ready")
        mid_ready, end_ready = sem("mid_ready"), sem("end_ready")
        exp_qm, exp_km, exp_qs, exp_ke, dec_ready = [sem(n) for n in ("exp_qm", "exp_km", "exp_qs", "exp_ke", "dec_ready")]
        km_ready, ke_ready, am_zero = sem("km_ready"), sem("ke_ready"), sem("am_zero")
        state_used = sem("state_used")
        osq_ready, ors_ready, oa_ready = sem("osq_ready"), sem("ors_ready"), sem("oa_ready")
        down_used = sem("down_used")
        rows_out, bias_in, p2_ready = sem("rows_out"), sem("bias_in"), sem("p2_ready")
        xkv_ready, shifted, keys_copied, rc_ready = sem("xkv_ready"), sem("shifted"), sem("keys_copied"), sem("rc_ready")
        gelu_ready, sq_b, rs_b, norm_b, gates_ready = [sem(n) for n in ("gelu_ready", "sq_b", "rs_b", "norm_b", "gates_ready")]
        pc_shift, pc_exp, pc_ready = sem("pc_shift"), sem("pc_exp"), sem("pc_ready")
        row_max, exp_done, weight_ready, p_ready, pv_done = [sem(n) for n in ("row_max", "exp_done", "weight_ready", "p_ready", "pv_done")]
        top_diff, top_sig, mask_ready = sem("top_diff"), sem("top_sig"), sem("mask_ready")
        counted, routed = sem("counted"), sem("routed")
        zeroed = sem("zeroed")
        cur_ready, sel_ready, xg_hi_ready, h_ready = [sem(n) for n in ("cur_ready", "sel_ready", "xg_hi_ready", "h_ready")]
        stored = sem("stored")

        def free_bank(eng, job):
            b, k = J[job]
            if k:
                eng.wait_ge(bank_free[b], k)
            return b

        def filled(eng, job):
            b, k = J[job]
            eng.wait_ge(bank_full[b], k + 1)
            return b

        def evacuated(eng, job):
            b, k = J[job]
            eng.wait_ge(bank_free[b], k + 1)

        def halves_used(eng, name):
            if name[0] == "dn" and name[1] < FFN // 256 - 1:
                eng.wait_ge(half_used, name[1] + 1)
            elif name[0] == "dn":
                filled(eng, ("down", 3))
            else:
                filled(eng, name)

        DN_ALONE = FFN // 256 - 1

        def raw_arrived(eng, name):
            s, k = RAW[name]
            eng.wait_ge(slot_ready[s], 16 * (k + 1))
            return ring[:, s, :]

        SPLIT = [n for n in HALVES if n in PAIR]
        PAIR_USER = {m: [n for n in SPLIT if PAIR[n][0] == m] for m in range(PAIRS)}

        def make_hi(eng, name):
            src = raw_arrived(eng, name)
            m, k = PAIR[name]
            if k:
                halves_used(eng, PAIR_USER[m][k - 1])
            eng.activation(w_hi[:, m, :], src, ACT.Copy).then_inc(hi_ready[m], 1)

        def make_lo(eng, name):
            m, k = PAIR[name]
            eng.wait_ge(hi_ready[m], k + 1)
            eng.tensor_tensor(w_lo[:, m, :], ring[:, RAW[name][0], :], w_hi[:, m, :].bitcast(F32), ALU.subtract).then_inc(lo_ready[m], 1)

        def refill(make, eng, name):
            n = SPLIT.index(name) + PAIRS
            if n < len(SPLIT):
                make(eng, SPLIT[n])

        def refill_after(make, eng, name):
            refill(make, eng, name)

        def users_done(eng, m):
            halves_used(eng, PAIR_USER[m][-1])

        def pair_ready(eng, name):
            m, k = PAIR[name]
            eng.wait_ge(lo_ready[m], k + 1)
            return w_hi[:, m, :], w_lo[:, m, :]

        def item_arrived(eng, m, i):
            eng.wait_ge(slot_ready[m % RING], 16 * (RAW_BASE[m % RING] + m // RING + 1) + i * (16 * PER_ITEM // RING))

        def pair_count(m, i):
            return PAIR_BASE[m % PAIRS] + m // PAIRS + i * (PER_ITEM // PAIRS)

        FILLS = {}
        for m, (kind, j, half) in enumerate(ITEM):
            if half == 1 and kind != "dn":
                FILLS[m] = (kind, j)
        FILLS[PER_ITEM - 1] = ("y", 1)
        ALONE = [m for m in range(PER_ITEM) if m not in FILLS]

        def item_half_used(eng, m, i):
            if m in FILLS:
                b, n = bank_count(FILLS[m], i)
                eng.wait_ge(bank_full[b], n + 1)
            else:
                eng.wait_ge(half_used, DN_ALONE + ALONE.index(m) + 1 + i * len(ALONE))

        def item_hi(eng, m, i):
            item_arrived(eng, m, i)
            eng.activation(w_hi[:, m % PAIRS, :], ring[:, m % RING, :], ACT.Copy).then_inc(hi_ready[m % PAIRS], 1)

        def item_lo(eng, m, i):
            eng.wait_ge(hi_ready[m % PAIRS], pair_count(m, i) + 1)
            eng.tensor_tensor(w_lo[:, m % PAIRS, :], ring[:, m % RING, :], w_hi[:, m % PAIRS, :].bitcast(F32),
                              ALU.subtract).then_inc(lo_ready[m % PAIRS], 1)

        def item_refill_hi(eng, m, i):
            item_half_used(eng, m, i)
            n = m + PAIRS
            item_hi(eng, n % PER_ITEM, i + n // PER_ITEM)

        def item_refill_lo(eng, m, i):
            n = m + PAIRS
            item_lo(eng, n % PER_ITEM, i + n // PER_ITEM)

        def bank_count(name, i):
            b, k = JTURN[name]
            return b, JBASE[b] + k + i * JPER[b]

        def state_read(eng, c):
            if (c + 1) % (NCH // TT) == 0:
                filled(eng, ("O", c // (NCH // TT), 1))
            else:
                eng.wait_ge(state_used, sum(x % (NCH // TT) != NCH // TT - 1 for x in range(1, c + 1)))

        CMP_AT = [2 + HB // 2 * tt for tt in range(TT)]
        units = [(tt, h) for tt in range(TT) for h in range(HB)]

        def pv_release(eng, u):
            if u % 8 == 7:
                filled(eng, ("OT", u // 8))
            else:
                eng.wait_ge(pv_done, u - u // 8 + 1)

        block = ctx.enter_context(nc.Block())

        @block.sync
        def _(sp):
            sp.dma_start(x_in, ins["x"][0].rearrange("(a p) d -> p a d", p=P)).then_inc(x_loaded, 16)
            w_in, w_out_a = ins["a_w_in"][0], ins["a_w_out"][0]
            gu, down = ins["ffn_w_gu"][0], ins["ffn_w_down"][0]
            kv, w_b, w_out_b = ins["w_kv"], ins["b_w_in"][0], ins["b_w_out"][0]
            which = {"q": 0, "f": 1, "i": 2, "g": 3}

            def columns(w, a, n=512):
                return w.rearrange("(k p) n -> p k n", p=P)[:, :, a:a + n]

            def slot_read(old):
                if old in PAIR:
                    sp.wait_ge(lo_ready[PAIR[old][0]], PAIR[old][1] + 1)
                elif old[1] % 2 == 0:
                    sp.wait_ge(w1_used, old[1] // 2 + 1)
                else:
                    filled(sp, ("hid", old[1] // 2))

            sp.wait_ge(rows_loaded, 16 * 11)
            for n, name in enumerate(HALVES):
                s, _k = RAW[name]
                if n >= RING:
                    old = HALVES[n - RING]
                    slot_read(old)
                kind, c = name
                by_cols = ring[:, s, :].rearrange("p (k n) -> p k n", k=KC)
                by_rows = ring[:, s, :].rearrange("p (k n) -> p k n", k=2)
                if kind in which:
                    sp.dma_start(by_cols, columns(w_in, which[kind] * D + 256 * c, 256)).then_inc(slot_ready[s], 16)
                elif kind == "mixA":
                    sp.dma_start(by_cols, columns(w_out_a, 256 * c, 256)).then_inc(slot_ready[s], 16)
                elif kind in ("ga", "up"):
                    at = (FFN if kind == "up" else 0) + 256 * c
                    sp.dma_start(by_cols, columns(gu, at, 256)).then_inc(slot_ready[s], 16)
                elif kind == "dn":
                    sp.dma_start(by_rows, down[256 * c:256 * c + 256, :].rearrange("(k p) n -> p k n", p=P)).then_inc(slot_ready[s], 16)
                elif kind in ("kv0", "k", "v"):
                    at = 512 * c + (256 if kind == "v" else 0) if kind != "kv0" else 256 * c
                    sp.dma_start(by_cols, columns(kv, at, 256)).then_inc(slot_ready[s], 16)
                elif kind == "qB":
                    sp.dma_start(by_cols, columns(w_b, 256 * c, 256)).then_inc(slot_ready[s], 16)
                elif kind == "w1":
                    w1 = ins["cmp_w1_k" if c < 2 else "cmp_w1_v"].rearrange("(a k p) n -> a p k n", a=2, p=P)
                    sp.dma_start(by_cols, w1[c % 2]).then_inc(slot_ready[s], 16)
                else:
                    sp.dma_start(by_cols, columns(w_out_b, 256 * c, 256)).then_inc(slot_ready[s], 16)

            e_gu, e_down = ins["moe_w_gu"][0], ins["moe_w_down"][0]

            def load_item(i, e, slot_free):
                w_gu = e_gu[bass.ds(e, 1)].rearrange("o (k p) n -> p (o k) n", p=P)
                w_dn = e_down[bass.ds(e, 1)].rearrange("o (c k p) n -> p (o c) k n", p=P, k=2)
                for m, (kind, j, half) in enumerate(ITEM):
                    s = m % RING
                    slot_free(m, i)
                    if kind == "dn":
                        sp.dma_start(ring[:, s, :].rearrange("p (k n) -> p k n", k=2),
                                     w_dn[:, 2 * j + half, :, :]).then_inc(slot_ready[s], 16)
                    else:
                        at = (ED if kind == "up" else 0) + 512 * j
                        sp.dma_start(ring[:, s, :].rearrange("p (k n) -> p k n", k=4),
                                     w_gu[:, 4 * half:4 * half + 4, at:at + 512]).then_inc(slot_ready[s], 16)

            def after_dense(m, i):
                if m < RING:
                    old = [n for n in HALVES if RAW[n][0] == m][-1]
                    slot_read(old)
                else:
                    sp.wait_ge(lo_ready[(m - RING) % PAIRS], pair_count(m - RING, 0) + 1)

            def after_item(m, i):
                n, i = (m - RING, i) if m >= RING else (m - RING + PER_ITEM, i - 1)
                sp.wait_ge(lo_ready[n % PAIRS], pair_count(n, i) + 1)

            load_item(0, 0, after_dense)
            with sp.Fori(1, E) as i:
                load_item(i, i, after_item)
            sp.wait_ge(routed, 1)
            n_items = sp.value_load(route[0:1, ITEMS:ITEMS + 1], min_val=E, max_val=ITEMS - 1)
            with sp.If(n_items > E):
                with sp.Fori(E, n_items) as i:
                    e = sp.value_load(route[0:1, bass.ds(i, 1)], min_val=0, max_val=E - 1)
                    load_item(i, e, after_item)
            for m in range(PAIRS):
                after_item(m, n_items)
                sp.dma_start(ring[:, m, 0:16], e_gu[0, 0:P, 0:16]).then_inc(slot_ready[m], 16)
            for tt in range(TT):
                b, k = bank_count(("scatter", 2 * tt + 1), n_items)
                sp.wait_ge(bank_free[b], k + 1)
                sp.dma_start(out[0, P * tt:P * tt + P, :], acc[:, tt, :]).then_inc(stored, 16)
            sp.wait_ge(stored, 16 * TT)

        @block.gpsimd
        def _(pool):
            pool.memset(tb[BUCKETS:BUCKETS + 1, :], 1.0).then_inc(ones_row, 1)
            pool.wait_ge(ones_row, 1)
            for b in range(4):
                pool.wait_ge(fgate_ready, 2 * b + 2)
                pool.wait_ge(logf_ready, b + 1)
                v = FG[:, 2 * b:2 * b + 2, :]
                pool.tensor_scalar(v, v, -1.0, 1.0, ALU.mult, ALU.add).then_inc(k_ready, 1)
            pool.wait_ge(k_ready, 4)
            for b in range(4):
                v = slice(2 * b, 2 * b + 2)
                pool.wait_ge(exp_km, b + 1)
                pool.tensor_tensor(KM[:, v, :], KM[:, v, :], FG[:, v, :], ALU.mult).then_inc(km_ready, 1)
                pool.wait_ge(exp_ke, b + 1)
                pool.tensor_tensor(KE[:, v, :], KE[:, v, :], FG[:, v, :], ALU.mult).then_inc(ke_ready, 1)
            pool.wait_ge(km_ready, 4)
            pool.wait_ge(ke_ready, 4)
            pool.memset(AM.rearrange("p a b c -> p (a b c)"), 0.0).then_inc(am_zero, 1)
            evacuated(pool, ("mixA", 3))
            pool.dma_start(OH, ins["bias_onehot"]).then_inc(onehot_loaded, 16)
            evacuated(pool, ("biasw",))
            for tt in range(TT):
                evacuated(pool, ("biasc", tt))
            row = T + P
            pool.dma_start(scratch.ap().rearrange("p h x -> h p x"),
                           biasrow[:, 0:row].unsqueeze(1).to_broadcast([HB, P, row])).then_inc(rows_out, 16)
            pool.wait_ge(rows_out, 16)
            pool.dma_start(BD, bass.AP(scratch, P - 1, [[HB * row - 1, P], [row, HB], [1, T]])).then_inc(bias_in, 16)
            for s in range(2):
                evacuated(pool, ("kv0", s))
                for par in range(2):
                    for gp in range(2):
                        dst = X2[DH * par:DH * par + DH, s, :, :].rearrange("p (j r) t -> p r j t", r=2)[:, gp, :, 0:T - par]
                        src = raw0[DH * gp:DH * gp + DH, 2 * s:2 * s + 2, par:T]
                        pool.dma_start(dst, src).then_inc(shifted, 16)
            for br in range(2):
                evacuated(pool, ("k", br + 1))
                for par in range(2):
                    here, there = [slice(DH * x, DH * x + DH) for x in (par, 1 - par)]
                    v = [KT[x, br, :, :].rearrange("p (j r) t -> p r j t", r=2)[:, par, :, :] for x in (here, there)]
                    pool.dma_start(v[1], v[0]).then_inc(keys_copied, 16)

            for u, (tt, h) in enumerate(units):
                pool.wait_ge(weight_ready, u + 1)
                v = LB[:, u % (LAG + 1), 1, 0:P * (tt + 1)]
                pool.tensor_scalar(v, v, RW[:, u, 1:2], None, ALU.mult).then_inc(p2_ready, 1)
            evacuated(pool, ("mixB", 3))
            pool.memset(yt, 0.0).then_inc(zeroed, 1)
            pool.wait_ge(zeroed, 1)
            pool.memset(gt, 0.0).then_inc(zeroed, 1)

        def heads_out(act, n):
            k = filled(act, ("OT", n))
            tt, j = n // 2, n % 2
            act.activation(OT[:, 4 * j:4 * j + 4, P * tt:P * tt + P], ps[:, k, :].rearrange("p (c t) -> p c t", c=4),
                           ACT.Copy).then_inc(bank_free[k], 1)

        @block.scalar
        def _(act):
            steps = [0]

            def link(ins_):
                steps[0] += 1
                ins_.then_inc(act_step, 1)
                act.wait_ge(act_step, steps[0])

            def row_load(at, src):
                act.dma_start(rows[at:at + src.shape[0], 0:src.shape[1]], src).then_inc(rows_loaded, 16)

            act.dma_start(const[:, :], ins["tables"]).then_inc(const_loaded, 16)
            row_load(ROW_MIX, ins["norm_mix_g"].rearrange("l (k p) -> (l k) p", p=P))
            row_load(ROW_FFN, ins["norm_ffn_g"].rearrange("l (k p) -> (l k) p", p=P))
            row_load(ROW_KV, ins["kv_norm_g"].rearrange("(k p) -> k p", p=P))
            row_load(ROW_LB, ins["lb_param"].rearrange("l (k p) -> (l k) p", p=P))
            row_load(ROW_O, ins["a_onorm_g"])
            for half in range(2):
                for at, src in ((ROW_Q, ins["b_qnorm_g"]), (ROW_K, ins["k_norm_g"])):
                    n = src.shape[0]
                    act.dma_start(rows[at:at + n, DH * half:DH * half + DH], src).then_inc(rows_loaded, 16)
            row_load(ROW_POS, ins["cmp_pos_k"].rearrange("(a b) d -> a (b d)", b=2))
            row_load(ROW_POS + CMP // 2, ins["cmp_pos_v"].rearrange("(a b) d -> a (b d)", b=2))
            act.dma_start(w_router[:, :, :], ins["moe_router"][0].rearrange("(k p) e -> p k e", p=P)).then_inc(small_loaded, 16)
            act.dma_start(w_gate[:, :, :], ins["b_w_in"][0].rearrange("(k p) n -> p k n", p=P)[:, :, D:D + 3 * HB]).then_inc(small_loaded, 16)
            for s, n in enumerate(("cmp_w2_k", "cmp_w2_v")):
                for twice in range(2):
                    act.dma_start(w2[:, s, :, twice, :], ins[n].rearrange("(k p) d -> p k d", p=P)).then_inc(small_loaded, 16)
            act.dma_start(tb[0:BUCKETS, :], ins["rel_bias"]).then_inc(small_loaded, 16)

            act.wait_ge(eps_set, 1)

            def norm_stats(s, sources, meanwhile=lambda: None):
                for b in range(4):
                    evacuated(act, (sources, b))
                    act.activation(xn[:, 2 * b:2 * b + 2, :], hT[:, 2 * b:2 * b + 2, :], ACT.Square).then_inc(squared, 1)
                meanwhile()
                b = filled(act, ("sum", s))
                act.activation(rstd[:, :], ps[:, b, 0:T], ACT.Ln, bias=eps[:, :], scale=1.0 / D).then_inc(bank_free[b], 1)
                evacuated(act, ("sum", s))
                act.activation(rstd[:, :], rstd[:, :], ACT.Exp, scale=-0.5).then_inc(rstd_ready, 1)

            def x_hi_of(v):
                act.activation(x_hi[:, v[0]], v[1], ACT.Copy).then_inc(x_hi_ready, 1)

            def norm_hi(s):
                for b in range(4):
                    act.wait_ge(xn_ready, KC * s + 2 * b + 2)
                    x_hi_of((slice(512 * b, 512 * b + 512), xn[:, 2 * b:2 * b + 2, :].rearrange("p c t -> p (c t)")))

            norm_stats(0, "xT", lambda: make_hi(act, SPLIT[0]))
            act.wait_ge(lb_diff, 1)
            act.activation(lbs[:, 1, :], lbs[:, 0, :], ACT.Sigmoid).then_inc(lb_ready, 1)
            norm_hi(0)
            for name in SPLIT[1:PAIRS]:
                make_hi(act, name)
            for b in range(4):
                k = filled(act, ("f", b))
                act.activation(FG[:, 2 * b:2 * b + 2, :], ps[:, k, :].rearrange("p (h t) -> p h t", h=2),
                               ACT.Sigmoid).then_inc(bank_free[k], 1)
                refill(make_hi, act, ("f", b))
            for b in range(4):
                act.wait_ge(fgate_ready, 2 * b + 2)
                act.activation(QM[:, 2 * b:2 * b + 2, :], FG[:, 2 * b:2 * b + 2, :], ACT.Ln).then_inc(logf_ready, 1)
            for b in range(4):
                k = filled(act, ("i", b))
                act.activation(VA[:, :, 256 * b:256 * b + 256], ps[:, k, :].rearrange("p (a n) -> p a n", a=TT), ACT.Copy).then_inc(bank_free[k], 1)
                refill(make_hi, act, ("i", b))
                v = slice(2 * b, 2 * b + 2)
                act.wait_ge(cum_ready, 2 * b + 2)
                act.activation(QS[:, v, :], BC[:, v, :], ACT.Exp).then_inc(exp_qs, 1)
                act.wait_ge(mid_ready, b + 1)
                act.activation(KM[:, v, :], QM[:, v, :], ACT.Exp, scale=-1.0).then_inc(exp_km, 1)
                act.wait_ge(exp_km, b + 1)
                act.activation(QM[:, v, :], QM[:, v, :], ACT.Exp).then_inc(exp_qm, 1)
                act.wait_ge(end_ready, b + 1)
                act.activation(KE[:, v, :], KE[:, v, :], ACT.Exp).then_inc(exp_ke, 1)
            ends = BC.rearrange("p h (c w) -> p (h c) w", w=CH)[:, :, CH - 1:CH]
            act.activation(dec.rearrange("p (n o) -> p n o", o=1), ends, ACT.Exp).then_inc(dec_ready, 1)
            for b in range(4):
                k = filled(act, ("g", b))
                act.activation(GA[:, 2 * b:2 * b + 2, :], ps[:, k, :].rearrange("p (h t) -> p h t", h=2),
                               ACT.Silu).then_inc(bank_free[k], 1)
                refill(make_hi, act, ("g", b))
            for b in range(4):
                refill_after(make_hi, act, ("q", b))
            act.wait_ge(dec_ready, 1)
            act.wait_ge(end_ready, 4)
            for tt in range(TT):
                for a in range(2):
                    k = filled(act, ("KH", tt, a))
                    act.activation(KH[:, tt, 4 * a:4 * a + 4, :], ps[:, k, :].rearrange("p (h d) -> p h d", h=4),
                                   ACT.Copy).then_inc(bank_free[k], 1)
            for tt in range(TT):
                for a in range(2):
                    k = filled(act, ("O", tt, a))
                    src = ps[:, k, :].rearrange("p (h t) -> p h t", h=4)
                    act.activation(OSQ[:, 4 * a:4 * a + 4, P * tt:P * tt + P], src, ACT.Square).then_inc(osq_ready, 1)
                    act.activation(OA[:, 4 * a:4 * a + 4, P * tt:P * tt + P], src, ACT.Copy).then_inc(bank_free[k], 1)
            for b in range(4):
                k = filled(act, ("osum", b))
                act.activation(ORS[:, 2 * b:2 * b + 2, :], ps[:, k, :].rearrange("p (h t) -> p h t", h=2), ACT.Ln,
                               bias=eps[:, :], scale=1.0 / P).then_inc(bank_free[k], 1)
            for b in range(4):
                evacuated(act, ("osum", b))
                act.activation(ORS[:, 2 * b:2 * b + 2, :], ORS[:, 2 * b:2 * b + 2, :], ACT.Exp, scale=-0.5).then_inc(ors_ready, 1)

            for b in range(4):
                act.wait_ge(oa_ready, b + 1)
                x_hi_of((slice(512 * b, 512 * b + 512), OA[:, 2 * b:2 * b + 2, :].rearrange("p c t -> p (c t)")))
            for b in range(3):
                refill_after(make_hi, act, ("mixA", b))
            norm_stats(1, "mixA", lambda: refill_after(make_hi, act, ("mixA", 3)))
            norm_hi(1)
            for j in range(FFN // 256):
                k = filled(act, ("ga", j))
                if j >= 2:
                    evacuated(act, ("up", j - 2))
                act.activation(SG[:, j % 2, :], ps[:, k, :], ACT.Silu).then_inc(bank_free[k], 1)
                refill(make_hi, act, ("ga", j))
                evacuated(act, ("up", j))
                if j >= 2:
                    halves_used(act, ("dn", j - 2))
                act.activation(hid[:, j % 2, 0, :], HF[:, j % 2, :], ACT.Copy).then_inc(hid_hi, 1)
                refill(make_hi, act, ("up", j))
                if j:
                    refill_after(make_hi, act, ("dn", j - 1))
            norm_stats(2, "down", lambda: refill_after(make_hi, act, ("dn", FFN // 256 - 1)))
            norm_hi(2)

            for b in range(2):
                k = filled(act, ("kv0", b))
                act.activation(raw0[:, 2 * b:2 * b + 2, :], ps[:, k, :].rearrange("p (j t) -> p j t", j=2), ACT.Copy).then_inc(bank_free[k], 1)
                refill(make_hi, act, ("kv0", b))
            for br in (1, 2):
                k = filled(act, ("k", br))
                act.activation(ksq[br - 1], ps[:, k, :].rearrange("p (j t) -> p j t", j=2), ACT.Square).then_inc(sq_b, 1)
                refill(make_hi, act, ("k", br))
                k = filled(act, ("v", br))
                act.activation(VB[:, br - 1, :, :], ps[:, k, :].rearrange("p (a n) -> p a n", a=TT), ACT.Copy).then_inc(bank_free[k], 1)
                if br == 2:
                    norm_hi(3)
                refill(make_hi, act, ("v", br))
                k = filled(act, ("ksum", br))
                act.activation(ksq[br - 1], ps[:, k, :].rearrange("p (j t) -> p j t", j=2), ACT.Ln, bias=eps[:, :],
                               scale=1.0 / DH).then_inc(bank_free[k], 1)
                evacuated(act, ("ksum", br))
                act.activation(ksq[br - 1], ksq[br - 1], ACT.Exp, scale=-0.5).then_inc(rs_b, 1)
            for b in range(4):
                k = filled(act, ("qB", b))
                if b >= 2:
                    evacuated(act, ("k", b - 1))
                v = ps[:, k, :].rearrange("p (c t) -> p c t", c=2)
                act.activation(QT[:, 2 * b:2 * b + 2, :], v, ACT.Copy)
                act.activation(qsq[:, 2 * b:2 * b + 2, :], v, ACT.Square).then_inc(bank_free[k], 1)
                if b == 0:
                    refill(make_hi, act, ("qB", 0))
            k = filled(act, ("gate",))
            act.activation(gates, ps[:, k, 0:TT * 3 * HB].rearrange("p (a n) -> p a n", a=TT), ACT.Sigmoid).then_inc(bank_free[k], 1)
            for b in range(4):
                k = filled(act, ("qsum", b))
                act.activation(qsq[:, 2 * b:2 * b + 2, :], ps[:, k, :].rearrange("p (c t) -> p c t", c=2), ACT.Ln, bias=eps[:, :],
                               scale=1.0 / DH).then_inc(bank_free[k], 1)
            for b in range(4):
                evacuated(act, ("qsum", b))
                v = qsq[:, 2 * b:2 * b + 2, :]
                act.activation(v, v, ACT.Exp, scale=-0.5).then_inc(rs_b, 1)
            for s in range(2):
                k = filled(act, ("hid", s))
                act.activation(GH[:, s, :, :], ps[:, k, 0:P].rearrange("p (m n) -> p m n", m=2)[:, :, 0:G * NCMP],
                               ACT.Gelu_apprx_tanh).then_inc(bank_free[k], 1)
                if s == 0:
                    for b in (1, 2):
                        refill(make_hi, act, ("qB", b))
            k = filled(act, ("kc",))
            act.activation(kcsq, ps[:, k, 0:G * NCMP], ACT.Square).then_inc(sq_b, 1)
            act.activation(KCT, ps[:, k, 0:G * NCMP], ACT.Copy).then_inc(bank_free[k], 1)
            k = filled(act, ("kcsum",))
            act.activation(kcsq, ps[:, k, 0:G * NCMP], ACT.Ln, bias=eps[:, :], scale=1.0 / DH).then_inc(bank_free[k], 1)
            evacuated(act, ("kcsum",))
            act.activation(kcsq, kcsq, ACT.Exp, scale=-0.5).then_inc(rs_b, 1)
            refill(make_hi, act, ("qB", 3))
            for s in range(len(units) + LAG):
                if s < len(units):
                    w = P * (units[s][0] + 1)
                    act.wait_ge(row_max, s + 1)
                    for br in range(2):
                        v = LB[:, s % (LAG + 1), br, 0:w]
                        act.activation(v, v, ACT.Exp, bias=RM[:, s, br:br + 1], accum_out=RS[:, s, br:br + 1]).then_inc(exp_done, 1)
                if s in CMP_AT:
                    tt = CMP_AT.index(s)
                    act.wait_ge(pc_shift, tt + 1)
                    act.activation(PC[:, tt, :, 0:NCMP], PC[:, tt, :, 0:NCMP], ACT.Exp).then_inc(pc_exp, 1)
                if 1 <= s <= len(units):
                    u = s - 1
                    act.wait_ge(weight_ready, u + 1)
                    v = LB[:, u % (LAG + 1), 0, 0:P * (units[u][0] + 1)]
                    act.activation(v, v, ACT.Copy, scale=RW[:, u, 0:1]).then_inc(p_ready, 1)
                if s >= LAG:
                    u = s - LAG
                    n = 2 * (units[u][0] + 1) * P
                    k = filled(act, ("PT", u))
                    if u >= 2:
                        pv_release(act, u - 2)
                    act.activation(PTB[:, u % 2, 0:n], ps[:, k, 0:n], ACT.Copy).then_inc(bank_free[k], 1)
                    if u % 8 == 7 and u > 8:
                        heads_out(act, u // 8 - 1)
            heads_out(act, 3)
            for b in range(4):
                for n in range(4):
                    evacuated(act, ("OT", n))
                x_hi_of((slice(512 * b, 512 * b + 512), OT[:, 2 * b:2 * b + 2, :].rearrange("p c t -> p (c t)")))
            refill_after(make_hi, act, ("mixB", 0))
            norm_stats(3, "mixB")
            for m in range(PAIRS):
                users_done(act, m)
                item_hi(act, m, 0)

            act.wait_ge(top_diff, 1)
            act.activation(tw[:, :, 1:2], tw[:, :, 0:1], ACT.Sigmoid).then_inc(top_sig, 1)
            act.activation(tw[:, :, 2:3], tw[:, :, 0:1], ACT.Sigmoid, scale=-1.0).then_inc(top_sig, 1)
            for n in range(4):
                k = filled(act, ("xtok", n))
                act.activation(xtok[:, n // 2, 512 * (n % 2):512 * (n % 2) + 512], ps[:, k, :], ACT.Copy).then_inc(bank_free[k], 1)

            def gathered_hi(n):
                act.activation(xg_hi[:, 4 * n:4 * n + 4, :], ps[:, 6 + n, :].rearrange("p (c t) -> p c t", c=4), ACT.Copy).then_inc(xg_hi_ready, 1)

            for n in range(2):
                filled(act, ("gather", n))
                gathered_hi(n)
            for n in range(4):
                k = filled(act, ("htok", n))
                act.activation(acc[:, n // 2, 512 * (n % 2):512 * (n % 2) + 512], ps[:, k, :], ACT.Copy).then_inc(bank_free[k], 1)
            act.wait_ge(counted, 1)
            n_items = act.value_load(route[0:1, ITEMS:ITEMS + 1], min_val=E, max_val=ITEMS - 1)
            with act.Fori(0, n_items) as i:
                def hidden_hi(j):
                    b, k = bank_count(("hT", j), i)
                    act.wait_ge(bank_full[b], k + 1)
                    if j >= 2:
                        item_half_used(act, ITEM.index(("dn", j - 2, 1)), i)
                    act.activation(hid[:, j % 2, 0, :], ps[:, b, :], ACT.Copy).then_inc(hid_hi, 1)

                for m, (kind, j, half) in enumerate(ITEM):
                    if m == PER_ITEM - 1:
                        b, k = bank_count(("y", 1), i)
                        act.wait_ge(bank_full[b], k + 1)
                        act.activation(yt[:, 512:D], ps[:, b, :], ACT.Copy).then_inc(bank_free[b], 1)
                    item_refill_hi(act, m, i)
                    if kind == "gate" and half == 1:
                        b, k = bank_count(("gate", j), i)
                        act.wait_ge(bank_full[b], k + 1)
                        bu, ku = bank_count(("up", j - 2), i) if j >= 2 else bank_count(("up", NPAIR - 1 - j), i - 1)
                        act.wait_ge(bank_free[bu], ku + 1)
                        act.activation(SU[:, j % 2, :], ps[:, b, :], ACT.Silu).then_inc(bank_free[b], 1)
                        if j:
                            hidden_hi(j - 1)
                    if kind == "dn" and j == NPAIR - 2:
                        if half == 0:
                            hidden_hi(NPAIR - 1)
                        b, k = bank_count(("gather", half), i)
                        act.wait_ge(bank_full[b], k + 1)
                        gathered_hi(half)

        @block.vector
        def _(dve):
            steps = [0]

            def link(ins_):
                steps[0] += 1
                ins_.then_inc(dve_step, 1)
                dve.wait_ge(dve_step, steps[0])

            dve.memset(eps[:, :], EPS).then_inc(eps_set, 1)
            for b in range(4):
                k = filled(dve, ("xT", b))
                dve.tensor_copy(hT[:, 2 * b:2 * b + 2, :], ps[:, k, :].rearrange("p (c t) -> p c t", c=2)).then_inc(bank_free[k], 1)
            k = filled(dve, ("rows", 0))
            dve.tensor_copy(cols[:, :], ps[:, k, 0:ROWS]).then_inc(bank_free[k], 1)
            evacuated(dve, ("rows", 0))
            dve.tensor_sub(lbs[:, 0, :], cols[:, ROW_LB:ROW_LB + KC], cols[:, ROW_LB + KC:ROW_LB + 2 * KC]).then_inc(lb_diff, 1)

            def normalise(s, dst, gain, ready):
                dve.wait_ge(rstd_ready, s + 1)
                for c in range(KC):
                    dve.scalar_tensor_tensor(dst[:, c, :], hT[:, c, :], cols[:, gain + c:gain + c + 1], rstd[:, :],
                                             ALU.mult, ALU.mult).then_inc(ready, 1)

            def x_lo_of(v):
                x_pieces[0] += 1
                dve.wait_ge(x_hi_ready, x_pieces[0])
                dve.tensor_tensor(x_lo[:, v[0]], v[1], x_hi[:, v[0]].bitcast(F32), ALU.subtract).then_inc(x_lo_ready, 1)

            x_pieces = [0]

            def input_lo(x):
                for b in range(4):
                    x_lo_of((slice(512 * b, 512 * b + 512), x[:, 2 * b:2 * b + 2, :].rearrange("p c t -> p (c t)")))

            def normalise_input(s, gain):
                dve.wait_ge(rstd_ready, s + 1)
                for b in range(5):
                    if b < 4:
                        for c in (2 * b, 2 * b + 1):
                            dve.scalar_tensor_tensor(xn[:, c, :], hT[:, c, :], cols[:, gain + c:gain + c + 1], rstd[:, :],
                                                     ALU.mult, ALU.mult).then_inc(xn_ready, 1)
                    if b >= 1:
                        x_lo_of((slice(512 * b - 512, 512 * b), xn[:, 2 * b - 2:2 * b, :].rearrange("p c t -> p (c t)")))

            make_lo(dve, SPLIT[0])
            for b in range(4):
                evacuated(dve, ("xT", b))
            normalise_input(0, ROW_MIX)
            for name in SPLIT[1:PAIRS]:
                make_lo(dve, name)
            dve.wait_ge(lb_ready, 1)
            link(dve.tensor_scalar(lbs[:, 2, :], lbs[:, 1, :], -1.0, 1.0, ALU.mult, ALU.add))
            for h in range(HEADS_A):
                evacuated(dve, ("f", h // 2))
                dve.tensor_scalar(FG[:, h, :], FG[:, h, :], lbs[:, 2, h:h + 1], lbs[:, 1, h:h + 1], ALU.mult, ALU.add).then_inc(fgate_ready, 1)
                if h % 2 == 1:
                    refill(make_lo, dve, ("f", h // 2))
            mids = BC.rearrange("p h (c w) -> p (h c) w", w=CH)
            qm3 = QM.rearrange("p h (c w) -> p (h c) w", w=CH)
            ke3 = KE.rearrange("p h (c w) -> p (h c) w", w=CH)
            per = 2 * NCH
            for b in range(4):
                dve.wait_ge(logf_ready, b + 1)
                for h in (2 * b, 2 * b + 1):
                    dve.tensor_tensor_scan(BC[:, h, :], K("restart"), QM[:, h, :], 0.0, ALU.mult, ALU.add).then_inc(cum_ready, 1)
                dve.wait_ge(cum_ready, 2 * b + 2)
                v = slice(per * b, per * b + per)
                dve.tensor_sub(qm3[:, v, :], mids[:, v, :], mids[:, v, MID:MID + 1].to_broadcast([P, per, CH])).then_inc(mid_ready, 1)
                dve.tensor_sub(ke3[:, v, :], mids[:, v, CH - 1:CH].to_broadcast([P, per, CH]), mids[:, v, :]).then_inc(end_ready, 1)
                refill(make_lo, dve, ("i", b))
            for b in range(4):
                refill(make_lo, dve, ("g", b))
            for b in range(4):
                v = slice(2 * b, 2 * b + 2)
                dve.wait_ge(exp_qm, b + 1)
                dve.wait_ge(exp_qs, b + 1)
                k = filled(dve, ("q", b))
                src = ps[:, k, :].rearrange("p (h t) -> p h t", h=2)
                link(dve.tensor_tensor(QM[:, v, :], QM[:, v, :], src, ALU.mult))
                dve.tensor_tensor(QS[:, v, :], QS[:, v, :], src, ALU.mult).then_inc(bank_free[k], 1)
                refill(make_lo, dve, ("q", b))
            dve.wait_ge(am_zero, 1)
            causal = K("causal").bitcast(I32).unsqueeze(1).to_broadcast([P, 4, P])
            for tt in range(TT):
                for a in range(2):
                    k = filled(dve, ("A", tt, a))
                    dve.copy_predicated(AM[:, tt, 4 * a:4 * a + 4, :], causal,
                                        ps[:, k, :].rearrange("p (h t) -> p h t", h=4)).then_inc(bank_free[k], 1)
            dve.wait_ge(dec_ready, 1)
            for c in range(NCH - 1):
                if c >= 1:
                    for a in range(2):
                        evacuated(dve, ("U", c - 1, a))
                if c >= 2:
                    state_read(dve, c - 1)
                for h in range(HEADS_A):
                    if h % 4 == 0:
                        k = filled(dve, ("U", c, h // 4))
                    u = ps[:, k, P * (h % 4):P * (h % 4) + P]
                    new = ST[:, (c + 1) % 2, h, :]
                    if c == 0:
                        last = dve.tensor_copy(new, u)
                    else:
                        last = dve.scalar_tensor_tensor(new, ST[:, c % 2, h, :], dec[:, h * NCH + c:h * NCH + c + 1], u,
                                                        ALU.mult, ALU.add)
                    if h % 4 == 3:
                        last.then_inc(bank_free[k], 1)
            for tt in range(TT):
                for a in range(2):
                    evacuated(dve, ("O", tt, a))
            for b in range(4):
                v = slice(2 * b, 2 * b + 2)
                link(dve.scalar_tensor_tensor(OA[:, v, :], OA[:, v, :], cols[:, ROW_O:ROW_O + 1], GA[:, v, :], ALU.mult, ALU.mult))
            for b in range(4):
                v = slice(2 * b, 2 * b + 2)
                dve.wait_ge(ors_ready, b + 1)
                dve.tensor_tensor(OA[:, v, :], OA[:, v, :], ORS[:, v, :], ALU.mult).then_inc(oa_ready, 1)
            input_lo(OA)

            def residual(name):
                for b in range(4):
                    k = filled(dve, (name, b))
                    v = hT[:, 2 * b:2 * b + 2, :]
                    dve.tensor_tensor(v, v, ps[:, k, :].rearrange("p (c t) -> p c t", c=2), ALU.add).then_inc(bank_free[k], 1)
                    if (name, b) in PAIR:
                        refill(make_lo, dve, (name, b))
                for b in range(4):
                    evacuated(dve, (name, b))

            residual("mixA")
            normalise_input(1, ROW_FFN)
            for j in range(FFN // 256):
                refill(make_lo, dve, ("ga", j))
                evacuated(dve, ("ga", j))
                if j >= 2:
                    dve.wait_ge(hid_hi, j - 1)
                k = filled(dve, ("up", j))
                dve.tensor_tensor(HF[:, j % 2, :], SG[:, j % 2, :], ps[:, k, :], ALU.mult).then_inc(bank_free[k], 1)
                evacuated(dve, ("up", j))
                dve.wait_ge(hid_hi, j + 1)
                dve.tensor_tensor(hid[:, j % 2, 1, :], HF[:, j % 2, :], hid[:, j % 2, 0, :].bitcast(F32), ALU.subtract).then_inc(hid_lo, 1)
                refill(make_lo, dve, ("up", j))
                if j:
                    refill(make_lo, dve, ("dn", j - 1))
            k = filled(dve, ("biasw",))
            dve.tensor_copy(biasrow, ps[0:HB, k, :]).then_inc(bank_free[k], 1)
            for tt in range(TT):
                k = filled(dve, ("biasc", tt))
                dve.tensor_copy(BCM[:, tt, :, :], ps[:, k, 0:NCMP * HB].rearrange("p (n h) -> p n h", h=HB)).then_inc(bank_free[k], 1)
            residual("down")
            refill(make_lo, dve, ("dn", FFN // 256 - 1))
            normalise_input(2, ROW_KV)
            dve.wait_ge(x_lo_ready, x_pieces[0])
            for b in range(2):
                refill(make_lo, dve, ("kv0", b))
            normalise(2, xn, ROW_MIX + KC, xn_ready)
            for br in (1, 2):
                refill(make_lo, dve, ("k", br))
                if br == 2:
                    filled(dve, ("v", 2))
                    input_lo(xn)
                refill(make_lo, dve, ("v", br))
                dve.wait_ge(rs_b, br)
                k = filled(dve, ("k", br))
                for par in range(2):
                    half = slice(DH * par, DH * par + DH)
                    last = dve.scalar_tensor_tensor(KT[half, br - 1, :, :].rearrange("p (j r) t -> p r j t", r=2)[:, par],
                                                    ps[half, k, :].rearrange("p (j t) -> p j t", j=2), cols[half, ROW_K + br:ROW_K + br + 1],
                                                    ksq[br - 1][half], ALU.mult, ALU.mult)
                last.then_inc(bank_free[k], 1)
            refill(make_lo, dve, ("qB", 0))
            for s in range(2):
                dve.wait_ge(shifted, 16 * 4 * (s + 1) if s == 1 else 16 * 8)
                for g in range(G):
                    src = X2[:, s, g, :]
                    src = bass.AP(src.tensor, src.offset, [src.ap[0], [2, CMP // 2], [STRIDE, NCMP]])
                    at = ROW_POS + s * CMP // 2
                    dve.tensor_tensor(RC[:, s, :, NCMP * g:NCMP * g + NCMP], src,
                                      cols[:, at:at + CMP // 2].unsqueeze(2).to_broadcast([P, CMP // 2, NCMP]),
                                      ALU.add).then_inc(rc_ready, 1)
            link(dve.tensor_scalar(cols[:, ROW_Q:ROW_Q + 1], cols[:, ROW_Q:ROW_Q + 1], DH ** -0.5, None, ALU.mult))
            for b in range(4):
                dve.wait_ge(rs_b, b + 3)
                evacuated(dve, ("qB", b))
                v = slice(2 * b, 2 * b + 2)
                dve.scalar_tensor_tensor(QT[:, v, :], QT[:, v, :], cols[:, ROW_Q:ROW_Q + 1], qsq[:, v, :], ALU.mult, ALU.mult).then_inc(norm_b, 1)
            for b in (1, 2):
                refill(make_lo, dve, ("qB", b))
            k = filled(dve, ("vc",))
            dve.tensor_copy(VC, ps[0:NCMP, k, 0:G * DH]).then_inc(bank_free[k], 1)
            dve.wait_ge(rs_b, 7)
            evacuated(dve, ("kc",))
            dve.scalar_tensor_tensor(KCT, KCT, cols[:, ROW_K:ROW_K + 1], kcsq, ALU.mult, ALU.mult).then_inc(norm_b, 1)
            evacuated(dve, ("gate",))
            refill(make_lo, dve, ("qB", 3))
            def cmp_scores(tt):
                pc = PC[:, tt, :, 0:NCMP]
                mx = PCS[:, 0, HB * tt:HB * tt + HB]
                for par in range(2):
                    k = filled(dve, ("LC", tt, par))
                    dve.tensor_tensor(pc.rearrange("p (n r) m -> p r n m", r=2)[:, par],
                                      ps[:, k, 0:HB // 2 * NCMP].rearrange("p (n m) -> p n m", m=NCMP),
                                      BCM[:, tt, :, :].rearrange("p m (n r) -> p r n m", r=2)[:, par],
                                      ALU.add).then_inc(bank_free[k], 1)
                for par in range(2):
                    evacuated(dve, ("LC", tt, par))
                link(dve.reduce_max(mx, pc, AX.X))
                dve.tensor_sub(pc, pc, mx.unsqueeze(2).to_broadcast([P, HB, NCMP])).then_inc(pc_shift, 1)

            def cmp_weights(tt):
                pc = PC[:, tt, :, 0:NCMP]
                sm, wt = PCS[:, 1, HB * tt:HB * tt + HB], PCS[:, 2, HB * tt:HB * tt + HB]
                dve.wait_ge(pc_exp, tt + 1)
                link(dve.reduce_sum(sm, pc, AX.X))
                link(dve.reciprocal(wt, sm))
                link(dve.scalar_tensor_tensor(wt, gates[:, tt, :].rearrange("p (h b) -> p h b", b=3)[:, :, 0],
                                              K("seen")[:, tt:tt + 1], wt, ALU.mult, ALU.mult))
                dve.tensor_tensor(pc, pc, wt.unsqueeze(2).to_broadcast([P, HB, NCMP]), ALU.mult).then_inc(pc_ready, 1)

            dve.wait_ge(bias_in, 16)
            for s in range(len(units) + 1):
                if s < len(units):
                    tt, h = units[s]
                    w = P * (tt + 1)
                    k = filled(dve, ("L", s))
                    if s > LAG:
                        filled(dve, ("PT", s - LAG - 1))
                    lb = LB[:, s % (LAG + 1), :, 0:w]
                    dve.tensor_tensor(lb, ps[:, k, 0:2 * w].rearrange("p (b t) -> p b t", b=2),
                                      BD[:, h:h + 1, T - w:T].to_broadcast([P, 2, w]), ALU.add).then_inc(bank_free[k], 1)
                    evacuated(dve, ("L", s))
                    link(dve.reduce_max(RM[:, s, :], lb, AX.X))
                    dve.tensor_scalar(RM[:, s, :], RM[:, s, :], -1.0, None, ALU.mult).then_inc(row_max, 1)
                if s in CMP_AT:
                    cmp_scores(CMP_AT.index(s))
                if s - 1 in CMP_AT:
                    cmp_weights(CMP_AT.index(s - 1))
                if s % HP == HP - 1:
                    n = s // HP
                    k = filled(dve, ("PCT", n))
                    if n >= 2:
                        pv_release(dve, 4 * (n - 2) + 3)
                    dve.tensor_copy(PCT[:, n % 2, :], ps[0:NCMP, k, :]).then_inc(bank_free[k], 1)
                if s >= 1:
                    u = s - 1
                    tt, h = units[u]
                    dve.wait_ge(exp_done, 2 * u + 2)
                    link(dve.reciprocal(RW[:, u, :], RS[:, u, :]))
                    dve.tensor_tensor(RW[:, u, :], RW[:, u, :], gates[:, tt, 3 * h + 1:3 * h + 3], ALU.mult).then_inc(weight_ready, 1)
            for n in range(4):
                evacuated(dve, ("OT", n))
            input_lo(OT)
            residual("mixB")
            normalise(3, xn, ROW_FFN + KC, xn_ready)
            k = filled(dve, ("logits",))
            dve.tensor_copy(lgT, ps[0:E, k, 0:T]).then_inc(bank_free[k], 1)
            item_lo(dve, 0, 0)

            def choose(at):
                dve.tensor_copy(cur, at).then_inc(cur_ready, 1)

            def one_hot(v, tt, *gate):
                dve.tensor_scalar(v[:, tt, :], K("slots"), cur[:, tt:tt + 1], gate[0] if gate else None, ALU.is_equal,
                                  *([ALU.mult] if gate else [])).then_inc(sel_ready, 1)

            def gathered_lo(n):
                dve.tensor_tensor(xg_lo[:, 4 * n:4 * n + 4, :], ps[:, 6 + n, :].rearrange("p (c t) -> p c t", c=4),
                                  xg_hi[:, 4 * n:4 * n + 4, :].bitcast(F32), ALU.subtract).then_inc(bank_free[6 + n], 1)

            k = filled(dve, ("router",))
            dve.tensor_copy(lg, ps[:, k, 0:TT * E].rearrange("p (a e) -> p a e", a=TT)).then_inc(bank_free[k], 1)
            evacuated(dve, ("router",))
            for tt in range(TT):
                link(dve.max(top[:, tt, :], lg[:, tt, :]))
            for tt in range(TT):
                link(dve.max_index(topi[:, tt, :], top[:, tt, :], lg[:, tt, :]))
            link(dve.tensor_copy(topf, topi))
            link(dve.tensor_tensor(oh, K("experts").unsqueeze(1).unsqueeze(1).to_broadcast([P, TT, 2, E]),
                                   topf[:, :, 0:2].unsqueeze(3).to_broadcast([P, TT, 2, E]), ALU.is_equal))
            dve.tensor_tensor(mask, oh[:, :, 0, :], oh[:, :, 1, :], ALU.add).then_inc(mask_ready, 1)
            dve.tensor_tensor(tw[:, :, 0:1], top[:, :, 0:1], top[:, :, 1:2], ALU.subtract).then_inc(top_diff, 1)
            dve.wait_ge(mask_ready, 1)
            k = filled(dve, ("rank",))
            r = ps[:, k, 0:TT * E].rearrange("p (a e) -> p a e", a=TT)
            link(dve.scalar_tensor_tensor(pos, r, 1.0, mask, ALU.add, ALU.mult))
            link(dve.tensor_scalar(pos, pos, 1.0, None, ALU.subtract))
            dve.tensor_copy(cnt, ps[:, k, TT * E:TT * E + E]).then_inc(bank_free[k], 1)
            evacuated(dve, ("rank",))
            for tt in range(TT):
                dve.tensor_scalar(sel[:, tt, :], K("slots"), pos[:, tt, 0:1], None, ALU.is_equal).then_inc(sel_ready, 1)
            link(dve.memset(flag[:, 0:E], 1.0))
            for n in range(1, TURNS):
                link(dve.tensor_scalar(flag[:, E * n:E * n + E], cnt, float(TILE * n), None, ALU.is_gt))
            link(dve.tensor_tensor_scan(incl, K("ones")[:, 0:TURNS * E], flag, 0.0, ALU.mult, ALU.add))
            dve.tensor_copy(route[:, ITEMS:ITEMS + 1], incl[:, TURNS * E - 1:TURNS * E]).then_inc(counted, 1)
            for m in range(1, PAIRS):
                item_lo(dve, m, 0)
            for n in range(2):
                dve.wait_ge(xg_hi_ready, n + 1)
                gathered_lo(n)
            for tt in range(TT):
                dve.wait_ge(top_sig, 2)
                link(dve.tensor_scalar(gmat[:, tt, :], oh[:, tt, 0, :], tw[:, tt, 1:2], None, ALU.mult))
                link(dve.scalar_tensor_tensor(gmat[:, tt, :], oh[:, tt, 1, :], tw[:, tt, 2:3], gmat[:, tt, :], ALU.mult, ALU.add))
            wide = [P, ITEMS, TURNS * E]
            items3 = K("items").rearrange("p (i c) -> p i c", i=ITEMS)
            link(dve.tensor_tensor(pick, items3, incl.unsqueeze(1).to_broadcast(wide), ALU.subtract))
            link(dve.tensor_scalar(pick, pick, -1.0, None, ALU.is_equal))
            link(dve.tensor_tensor(pick, pick, flag.unsqueeze(1).to_broadcast(wide), ALU.mult))

            def picked(dst, values):
                link(dve.tensor_tensor(prod, pick, values.unsqueeze(1).to_broadcast(wide), ALU.mult))
                link(dve.reduce_sum(dst, prod, AX.X))

            for tt in range(TT):
                c3 = poscand[:, tt, :].rearrange("p (n e) -> p n e", e=E)
                link(dve.tensor_tensor(c3, pos[:, tt:tt + 1, :].to_broadcast([P, TURNS, E]),
                                       K("cand_at").rearrange("p (n e) -> p n e", e=E), ALU.subtract))
                picked(table[:, :, tt], poscand[:, tt, :])
            for tt in range(TT):
                c3 = poscand[:, tt, :].rearrange("p (n e) -> p n e", e=E)
                link(dve.tensor_copy(c3, gmat[:, tt:tt + 1, :].to_broadcast([P, TURNS, E])))
                picked(table[:, :, TT + tt], poscand[:, tt, :])
            picked(route_f, K("cand_e"))
            dve.tensor_copy(route[:, 0:ITEMS], route_f).then_inc(routed, 1)
            choose(table[:, 0, :])
            dve.wait_ge(cur_ready, 1)
            for n in range(4):
                evacuated(dve, ("htok", n))
            dve.wait_ge(counted, 1)
            dve.wait_ge(routed, 1)
            n_items = dve.value_load(route[0:1, ITEMS:ITEMS + 1], min_val=E, max_val=ITEMS - 1)
            with dve.Fori(0, n_items) as i:
                def added(n, i):
                    b, k = bank_count(("scatter", n), i)
                    dve.wait_ge(bank_full[b], k + 1)
                    v = acc[:, n // 2, 512 * (n % 2):512 * (n % 2) + 512]
                    dve.tensor_tensor(v, v, ps[:, b, :], ALU.add).then_inc(bank_free[b], 1)

                def hidden_lo(j):
                    b, k = bank_count(("hT", j), i)
                    dve.wait_ge(hid_hi, FFN // 256 + i * NPAIR + j + 1)
                    dve.tensor_tensor(hid[:, j % 2, 1, :], ps[:, b, :], hid[:, j % 2, 0, :].bitcast(F32), ALU.subtract).then_inc(bank_free[b], 1)

                for m, (kind, j, half) in enumerate(ITEM):
                    if m == PER_ITEM - 1:
                        b, k = bank_count(("y", 0), i)
                        dve.wait_ge(bank_full[b], k + 1)
                        dve.tensor_copy(yt[:, 0:512], ps[:, b, :]).then_inc(bank_free[b], 1)
                    item_refill_lo(dve, m, i)
                    if kind == "gate" and half == 1 and j:
                        hidden_lo(j - 1)
                    if kind == "up" and half == 1:
                        b, k = bank_count(("gate", j), i)
                        dve.wait_ge(bank_free[b], k + 1)
                        b, k = bank_count(("up", j), i)
                        dve.wait_ge(bank_full[b], k + 1)
                        bh, kh = bank_count(("hT", j - 2), i) if j >= 2 else bank_count(("hT", NPAIR - 1 - j), i - 1)
                        dve.wait_ge(bank_full[bh], kh + 1)
                        dve.tensor_tensor(HM[:, j % 2, :], SU[:, j % 2, :], ps[:, b, :], ALU.mult).then_inc(bank_free[b], 1)
                    if kind != "dn" and j == 0 and half == 1:
                        for n in range(2):
                            added(2 * (kind == "up") + n, i)
                    if kind == "up" and j == GT_AFTER and half == 1:
                        for tt in range(TT):
                            one_hot(selg, tt, cur[:, TT + tt:TT + tt + 1])
                        dve.wait_ge(sel_ready, i * 4 + 4)
                        choose(table[:, bass.ds(i + 1, 1), :].rearrange("p o n -> p (o n)"))
                        dve.wait_ge(cur_ready, i + 2)
                        for tt in range(TT):
                            one_hot(sel, tt)
                    if kind == "dn" and j == GT_AFTER and half == 1:
                        b, k = bank_count(("GT",), i)
                        dve.wait_ge(bank_full[b], k + 1)
                        dve.tensor_copy(gt, ps[:, b, 0:T]).then_inc(bank_free[b], 1)
                    if kind == "dn" and j == NPAIR - 2:
                        if half == 0:
                            hidden_lo(NPAIR - 1)
                        dve.wait_ge(xg_hi_ready, 2 * i + half + 3)
                        gathered_lo(half)
            for n in range(4):
                added(n, n_items)

        @block.tensor
        def _(pe):
            ident, ones, halves = K("ident"), K("ones"), K("halves")

            def mm(o, w, x, start, stop, **kw):
                return pe.matmul(o, w, x, start=start, stop=stop, **kw)

            pe.wait_ge(const_loaded, 16)
            pe.wait_ge(x_loaded, 16)
            for n in range(4):
                b = free_bank(pe, ("xT", n))
                for c in range(2):
                    for tt in range(TT):
                        last = pe.transpose(ps[:, b, T * c + P * tt:T * c + P * tt + P],
                                            x_in[:, tt, P * (2 * n + c):P * (2 * n + c) + P], ident)
                last.then_inc(bank_full[b], 1)
            pe.wait_ge(rows_loaded, 16 * 11)
            b = free_bank(pe, ("rows", 0))
            pe.transpose(ps[:, b, 0:ROWS], rows[0:ROWS, :], ident[0:ROWS, 0:ROWS]).then_inc(bank_full[b], 1)

            def norm_sum(s):
                b = free_bank(pe, ("sum", s))
                for c in range(KC):
                    if c % 2 == 0:
                        pe.wait_ge(squared, 4 * s + c // 2 + 1)
                    last = mm(ps[:, b, 0:T], ones, xn[:, c, :], c == 0, c == KC - 1)
                last.then_inc(bank_full[b], 1)

            def split_product(o, w, x, start, stop, **kw):
                mm(o, w[0], x[0], start, False, **kw)
                mm(o, w[0], x[1], False, False, **kw)
                return mm(o, w[1], x[0], False, stop, **kw)

            def parts(pair, f):
                return [f(v) for v in pair]

            def x_part(c, tokens=slice(0, T)):
                return [v[:, T * c + tokens.start:T * c + tokens.stop] for v in (x_hi, x_lo)]

            x_pieces = [0]

            def project(name, wait_x):
                pair = pair_ready(pe, name)
                b = free_bank(pe, name)
                for m in range(2):
                    for c in range(KC):
                        if wait_x and m == 0 and c % 2 == 0:
                            pe.wait_ge(x_lo_ready, x_pieces[0] + c // 2 + 1)
                        w = [v[:, 256 * c + P * m:256 * c + P * m + P] for v in pair]
                        last = split_product(ps[:, b, T * m:T * m + T], w, x_part(c), c == 0, c == KC - 1)
                last.then_inc(bank_full[b], 1)
                if wait_x:
                    x_pieces[0] += 4

            def project_tokens(name):
                pair = pair_ready(pe, name)
                b = free_bank(pe, name)
                for tt in range(TT):
                    for c in range(KC):
                        w = [v[:, 256 * c:256 * c + 256] for v in pair]
                        last = split_product(ps[:, b, 256 * tt:256 * tt + 256], x_part(c, slice(P * tt, P * tt + P)), w, c == 0, c == KC - 1)
                last.then_inc(bank_full[b], 1)

            def dense(name):
                for b in range(4):
                    project((name, b), b == 0)

            norm_sum(0)
            dense("f")
            for b in range(4):
                project_tokens(("i", b))
            for name in ("g", "q"):
                for b in range(4):
                    project((name, b), False)

            for b in range(4):
                evacuated(pe, ("q", b))
            pe.wait_ge(km_ready, 4)
            pe.wait_ge(ke_ready, 4)
            for tt in range(TT):
                for a in range(2):
                    b = free_bank(pe, ("A", tt, a))
                    for n in range(4):
                        v = (4 * a + n, slice(P * tt, P * tt + P))
                        last = mm(ps[:, b, P * n:P * n + P], KM[:, v[0], v[1]], QM[:, v[0], v[1]], True, True)
                    last.then_inc(bank_full[b], 1)
                for a in range(2):
                    b = free_bank(pe, ("KH", tt, a))
                    for n in range(4):
                        last = pe.transpose(ps[:, b, P * n:P * n + P], KE[:, 4 * a + n, P * tt:P * tt + P], ident)
                    last.then_inc(bank_full[b], 1)
            for b in range(4):
                evacuated(pe, ("i", b))
            per = NCH // TT
            for tt in range(TT):
                for a in range(2):
                    evacuated(pe, ("A", tt, a))
                    evacuated(pe, ("KH", tt, a))
                banks = [free_bank(pe, ("O", tt, a)) for a in range(2)]
                for h in range(HEADS_A):
                    mm(ps[:, banks[h // 4], P * (h % 4):P * (h % 4) + P], VA[:, tt, P * h:P * h + P], AM[:, tt, h, :],
                       h % 4 == 0, False, skip_group_check=True)
                for c in range(per):
                    gc = tt * per + c
                    r = slice(CH * c, CH * c + CH)
                    if gc < NCH - 1:
                        for a in range(2):
                            b = free_bank(pe, ("U", gc, a))
                            for n in range(4):
                                h = 4 * a + n
                                last = mm(ps[:, b, P * n:P * n + P], KH[r, tt, h, :], VA[r, tt, P * h:P * h + P], True, True)
                            last.then_inc(bank_full[b], 1)
                    if gc >= 1:
                        for a in range(2):
                            evacuated(pe, ("U", gc - 1, a))
                        for h in range(HEADS_A):
                            b = banks[h // 4]
                            at = P * (h % 4) + CH * c
                            last = mm(ps[:, b, at:at + CH], ST[:, gc % 2, h, :], QS[:, h, CH * gc:CH * gc + CH], False,
                                      c == per - 1, skip_group_check=True)
                            if c == per - 1 and h % 4 == 3:
                                last.then_inc(bank_full[b], 1)
                        if c < per - 1:
                            last.then_inc(state_used, 1)
            for b4 in range(4):
                pe.wait_ge(osq_ready, 4)
                b = free_bank(pe, ("osum", b4))
                mm(ps[:, b, :], ones, OSQ[:, 2 * b4:2 * b4 + 2, :], True, True).then_inc(bank_full[b], 1)
            dense("mixA")

            norm_sum(1)
            pe.wait_ge(small_loaded, 16 * 7)
            pe.wait_ge(ones_row, 1)

            def down(j):
                pair = pair_ready(pe, ("dn", j))
                pe.wait_ge(hid_lo, j + 1)
                for k in range(2):
                    first, final = j == 0 and k == 0, j == FFN // 256 - 1 and k == 1
                    h = [hid[:, j % 2, part, T * k:T * k + T] for part in range(2)]
                    for m in range(KC):
                        b = J[("down", m // 2)][0]
                        w = [v[:, D * k + P * m:D * k + P * m + P] for v in pair]
                        last = split_product(ps[:, b, T * (m % 2):T * (m % 2) + T], w, h, first and m % 2 == 0, final, skip_group_check=True)
                        if final and m % 2 == 1:
                            last.then_inc(bank_full[b], 1)
                if j < FFN // 256 - 1:
                    last.then_inc(half_used, 1)

            for n in range(4):
                free_bank(pe, ("down", n))
            for j in range(FFN // 256 + 1):
                if j < FFN // 256:
                    project(("ga", j), j == 0)
                    project(("up", j), False)
                if j:
                    down(j - 1)
            pe.wait_ge(onehot_loaded, 16)
            b = free_bank(pe, ("biasw",))
            mm(ps[0:HB, b, :], tb[:, :], OH[:, 0:2 * T], True, True).then_inc(bank_full[b], 1)
            for tt in range(TT):
                b = free_bank(pe, ("biasc", tt))
                for n in range(NCMP):
                    at = 2 * T + n * T + P * tt
                    last = mm(ps[:, b, HB * n:HB * n + HB], OH[:, at:at + P], tb[:, :], True, True)
                last.then_inc(bank_full[b], 1)

            norm_sum(2)
            project(("kv0", 0), True)
            project(("kv0", 1), False)
            for br in (1, 2):
                project(("k", br), False)
                project_tokens(("v", br))
                pe.wait_ge(sq_b, br)
                b = free_bank(pe, ("ksum", br))
                mm(ps[:, b, :], halves, ksq[br - 1], True, True).then_inc(bank_full[b], 1)
            dense("qB")
            b = free_bank(pe, ("gate",))
            for tt in range(TT):
                for k in range(KC):
                    last = mm(ps[:, b, 48 * tt:48 * tt + 48], xn[:, k, P * tt:P * tt + P], w_gate[:, k, :], k == 0, k == KC - 1)
            last.then_inc(bank_full[b], 1)
            for n in range(4):
                evacuated(pe, ("qB", n))
                b = free_bank(pe, ("qsum", n))
                mm(ps[:, b, :], halves, qsq[:, 2 * n:2 * n + 2, :], True, True).then_inc(bank_full[b], 1)
            for s in range(2):
                pe.wait_ge(rc_ready, G * (s + 1))
                b = free_bank(pe, ("hid", s))
                for half in range(2):
                    w = raw_arrived(pe, ("w1", 2 * s + half)).rearrange("p (k n) -> p k n", n=HID)
                    for m in range(2):
                        for k in range(CMP // 4):
                            last = mm(ps[:, b, 64 * m:64 * m + G * NCMP], w[:, k, P * m:P * m + P], RC[:, s, CMP // 4 * half + k, :],
                                      half == 0 and m == 0 and k == 0, half == 1 and k == CMP // 4 - 1, skip_group_check=True)
                    last.then_inc(w1_used if half == 0 else bank_full[b], 1)
            evacuated(pe, ("hid", 0))
            b = free_bank(pe, ("kc",))
            for m in range(2):
                last = mm(ps[:, b, 0:G * NCMP], w2[:, 0, m, :, :].rearrange("p a d -> p (a d)"), GH[:, 0, m, :], m == 0, m == 1)
            last.then_inc(bank_full[b], 1)
            evacuated(pe, ("hid", 1))
            b = free_bank(pe, ("vc",))
            for g in range(G):
                for m in range(2):
                    last = mm(ps[0:NCMP, b, DH * g:DH * g + DH], GH[:, 1, m, NCMP * g:NCMP * g + NCMP], w2[:, 1, m, 0, :], m == 0, m == 1)
            last.then_inc(bank_full[b], 1)
            pe.wait_ge(sq_b, 3)
            b = free_bank(pe, ("kcsum",))
            mm(ps[:, b, 0:G * NCMP], halves, kcsq, True, True).then_inc(bank_full[b], 1)
            pe.wait_ge(norm_b, 4)
            pe.wait_ge(keys_copied, 16 * 4)

            def cmp_scores(tt, piece):
                pe.wait_ge(norm_b, 5)
                par, first = piece // 2, piece % 2 == 0
                b = free_bank(pe, ("LC", tt, par)) if first else J[("LC", tt, par)][0]
                half = slice(DH * par, DH * par + DH)
                for n in range(0, HB // 4) if first else range(HB // 4, HB // 2):
                    g = (2 * n + par) // HP
                    last = mm(ps[:, b, NCMP * n:NCMP * n + NCMP], QT[half, n, P * tt:P * tt + P],
                              KCT[half, NCMP * g:NCMP * g + NCMP], True, True)
                if not first:
                    last.then_inc(bank_full[b], 1)

            def scores(u):
                tt, h = units[u]
                half, w = slice(DH * (h % 2), DH * (h % 2) + DH), P * (tt + 1)
                b = free_bank(pe, ("L", u))
                for br in range(2):
                    last = mm(ps[:, b, w * br:w * br + w], QT[half, h // 2, P * tt:P * tt + P], KT[half, br, h // HP, 0:w], True, True)
                last.then_inc(bank_full[b], 1)

            def cmp_turned(n):
                tt, g = n // G, n % G
                pe.wait_ge(pc_ready, tt + 1)
                b = free_bank(pe, ("PCT", n))
                for hp in range(HP):
                    last = pe.transpose(ps[0:NCMP, b, P * hp:P * hp + P], PC[:, tt, HP * g + hp, 0:NCMP], ident)
                last.then_inc(bank_full[b], 1)

            def turned(u):
                tt = units[u][0]
                pe.wait_ge(p_ready, u + 1)
                pe.wait_ge(p2_ready, u + 1)
                b = free_bank(pe, ("PT", u))
                for br in range(2):
                    for s in range(tt + 1):
                        at = P * ((tt + 1) * br + s)
                        last = pe.transpose(ps[:, b, at:at + P], LB[:, u % (LAG + 1), br, P * s:P * s + P], ident)
                last.then_inc(bank_full[b], 1)

            def values(u):
                tt, h = units[u]
                g, hp, half = h // HP, h % HP, slice(DH * (h % 2), DH * (h % 2) + DH)
                n = u // HP
                if u % 8 == 0:
                    free_bank(pe, ("OT", u // 8))
                b = J[("OT", u // 8)][0]
                evacuated(pe, ("PCT", n))
                evacuated(pe, ("PT", u))
                at = P * (h // 2 % 4)
                o = ps[half, b, at:at + P]
                mm(o, VC[:, DH * g:DH * g + DH], PCT[:, n % 2, P * hp:P * hp + P], True, False)
                for br in range(2):
                    for s in range(tt + 1):
                        at = P * ((tt + 1) * br + s)
                        last = mm(o, VB[:, br, s, DH * g:DH * g + DH], PTB[:, u % 2, at:at + P], False, br == 1 and s == tt)
                last.then_inc(bank_full[b] if u % 8 == 7 else pv_done, 1)

            evacuated(pe, ("vc",))
            for br in (1, 2):
                evacuated(pe, ("v", br))
            for s in range(len(units) + LAG + 1):
                if s < len(units):
                    scores(s)
                    for tt in range(TT):
                        for piece in range(4):
                            if s == max(CMP_AT[tt] - 3 + piece, 0):
                                cmp_scores(tt, piece)
                    if s % HP == HP - 1:
                        cmp_turned(s // HP)
                if LAG <= s < len(units) + LAG:
                    turned(s - LAG)
                if s > LAG:
                    values(s - LAG - 1)
            for n in range(4):
                evacuated(pe, ("OT", n))
            dense("mixB")

            norm_sum(3)
            b = free_bank(pe, ("logits",))
            for k in range(KC):
                pe.wait_ge(xn_ready, 4 * KC + k + 1)
                last = mm(ps[0:E, b, 0:T], w_router[:, k, :], xn[:, k, :], k == 0, k == KC - 1)
            last.then_inc(bank_full[b], 1)
            evacuated(pe, ("logits",))
            b = free_bank(pe, ("router",))
            for tt in range(TT):
                last = pe.transpose(ps[:, b, E * tt:E * tt + E], lgT[:, P * tt:P * tt + P], ident[0:E, 0:E])
            last.then_inc(bank_full[b], 1)

            def to_tokens(name, src):
                for n in range(4):
                    b = free_bank(pe, (name, n))
                    for c in range(4):
                        last = pe.transpose(ps[:, b, P * c:P * c + P], src[:, 4 * (n % 2) + c, P * (n // 2):P * (n // 2) + P], ident)
                    last.then_inc(bank_full[b], 1)
            pe.wait_ge(mask_ready, 1)
            b = free_bank(pe, ("rank",))
            mm(ps[:, b, 0:2 * E], K("before"), mask, True, False, skip_group_check=True)
            mm(ps[:, b, E:3 * E].rearrange("p (a e) -> p a e", e=E), ones, mask[:, 0:1, :].to_broadcast([P, 2, E]), False, False, skip_group_check=True)
            mm(ps[:, b, 2 * E:3 * E], ones, mask[:, 1, :], False, True, skip_group_check=True).then_inc(bank_full[b], 1)
            to_tokens("xtok", xn)
            for n in range(4):
                evacuated(pe, ("xtok", n))

            def gather(n):
                b = 6 + n
                for m in range(4):
                    d = 4 * n + m
                    for tt in range(TT):
                        last = mm(ps[:, b, TILE * m:TILE * m + TILE], xtok[:, tt, P * d:P * d + P], sel[:, tt, :], tt == 0, tt == TT - 1)
                last.then_inc(bank_full[b], 1)

            pe.wait_ge(sel_ready, 2)
            for n in range(2):
                free_bank(pe, ("gather", n))
                gather(n)
            to_tokens("htok", hT)
            pe.wait_ge(zeroed, 2)
            pe.wait_ge(counted, 1)
            n_items = pe.value_load(route[0:1, ITEMS:ITEMS + 1], min_val=E, max_val=ITEMS - 1)
            with pe.Fori(0, n_items) as i:
                def free(name):
                    b, k = bank_count(name, i)
                    pe.wait_ge(bank_free[b], k)
                    return b

                def out_of_psum(name):
                    b, k = bank_count(name, i)
                    pe.wait_ge(bank_free[b], k + 1)

                def pair(m):
                    pe.wait_ge(lo_ready[m % PAIRS], pair_count(m, i) + 1)
                    return w_hi[:, m % PAIRS, :], w_lo[:, m % PAIRS, :]

                for n in range(2):
                    pe.wait_ge(bank_free[6 + n], JBASE[6 + n] + i * JPER[6 + n])

                def scatter(n):
                    b = free(("scatter", n))
                    mm(ps[:, b, :], gt[:, P * (n // 2):P * (n // 2) + P], yt[:, 512 * (n % 2):512 * (n % 2) + 512], True, True).then_inc(bank_full[b], 1)

                def turned_hidden(j):
                    out_of_psum(("up", j))
                    b = free(("hT", j))
                    for c in range(4):
                        last = pe.transpose(ps[:, b, P * c:P * c + P], HM[:, j % 2, P * c:P * c + P], ident)
                    last.then_inc(bank_full[b], 1)

                for m, (kind, j, half) in enumerate(ITEM):
                    if kind == "dn":
                        w = pair(m)
                        if half == 0:
                            out_of_psum(("hT", j))
                            if j == 0:
                                for n in range(2):
                                    free(("y", n))
                        for c in (2 * half, 2 * half + 1):
                            h = [hid[:, j % 2, part, P * c:P * c + P] for part in range(2)]
                            for n in range(2):
                                b = JTURN[("y", n)][0]
                                at = D * (c % 2) + 512 * n
                                final = j == NPAIR - 1 and c == 3
                                last = split_product(ps[:, b, :], h, [v[:, at:at + 512] for v in w], j == 0 and c == 0, final)
                                if final:
                                    last.then_inc(bank_full[b], 1)
                        if m in ALONE:
                            last.then_inc(half_used, 1)
                        if j == GT_AFTER and half == 1:
                            pe.wait_ge(sel_ready, i * 4 + 4)
                            b = free(("GT",))
                            for tt in range(TT):
                                last = pe.transpose(ps[0:TILE, b, P * tt:P * tt + P], selg[:, tt, :], ident)
                            last.then_inc(bank_full[b], 1)
                        if j == NPAIR - 2 and half == 0:
                            turned_hidden(NPAIR - 1)
                            pe.wait_ge(sel_ready, i * 4 + 6)
                        if j == NPAIR - 2:
                            free(("gather", half))
                            gather(half)
                        continue
                    w = pair(m)
                    b = free((kind, j)) if half == 0 else JTURN[(kind, j)][0]
                    for k in range(4):
                        x = [v[:, 4 * half + k, :] for v in (xg_hi, xg_lo)]
                        last = split_product(ps[:, b, :], x, [v[:, 512 * k:512 * k + 512] for v in w], half == 0 and k == 0, half == 1 and k == 3)
                    last.then_inc(half_used if half == 0 else bank_full[b], 1)
                    if kind == "gate" and half == 1 and j:
                        turned_hidden(j - 1)
                    if j == 0 and half == 1:
                        if kind == "gate":
                            pe.wait_ge(bank_free[4], JBASE[4] + i * JPER[4])
                            pe.wait_ge(bank_free[5], JBASE[5] + i * JPER[5])
                        for n in range(2):
                            scatter(2 * (kind == "up") + n)
            for n in range(2):
                pe.wait_ge(bank_free[4 + n], JBASE[4 + n] + n_items * JPER[4 + n])
            for n in range(4):
                b, k = bank_count(("scatter", n), n_items)
                pe.wait_ge(bank_free[b], k)
                mm(ps[:, b, :], gt[:, P * (n // 2):P * (n // 2) + P], yt[:, 512 * (n % 2):512 * (n % 2) + 512], True, True).then_inc(bank_full[b], 1)


_OUT = (1, T, D)


def kernel(**inputs):
    import numpy as _np
    import concourse.bacc as _bacc
    from concourse import mybir as _mybir
    from concourse.bass_utils import run_bass_kernel_spmd as _run

    nc = _bacc.Bacc("TRN2", target_bir_lowering=False, num_devices=1)
    arrays, ins = {}, {}
    given = {k: _np.ascontiguousarray(v) for k, v in inputs.items()}
    given["tables"] = _np.concatenate(list(constants().values()), axis=1)
    given["bias_onehot"] = bias_tables()
    for name, a in given.items():
        arrays[f"in_{name}"] = a
        ins[name] = nc.dram_tensor(f"in_{name}", a.shape, _mybir.dt.from_np(a.dtype), kind="ExternalInput").ap()
    out = nc.dram_tensor("out", _OUT, _mybir.dt.from_np(_np.dtype("float32")), kind="ExternalOutput").ap()
    trunk(nc, ins, out)
    r = _run(nc, [arrays], core_ids=[0])
    return r.results[0]["out"]
```
